# Optimizing a Trainium2 kernel written in Bass

```python
import jax, jax.numpy as jnp
from jax import lax
import numpy as np
import math

D_MODEL = 1024
BATCH = 1
SEQ = 256
DEPTH = 2

N_MIXERS = 2
N_MLSTM_LAYERS = (DEPTH + N_MIXERS - 1) // N_MIXERS
N_ATTN_LAYERS = DEPTH // N_MIXERS

MLSTM_HEADS = 4
MLSTM_QK_DIM = D_MODEL // (2 * MLSTM_HEADS)
MLSTM_V_DIM = D_MODEL // MLSTM_HEADS
MLSTM_CHUNK = 128
MLSTM_N_GATES = 4 * MLSTM_HEADS
MLSTM_IN_WIDTH = 2 * MLSTM_HEADS * MLSTM_QK_DIM + 2 * D_MODEL + MLSTM_N_GATES
FGATE_BIAS_LO = 3.0
FGATE_BIAS_HI = 6.0

ATTN_HEAD_DIM = 64
ATTN_Q_HEADS = D_MODEL // ATTN_HEAD_DIM
ATTN_KV_HEADS = 4
ATTN_GROUP = ATTN_Q_HEADS // ATTN_KV_HEADS
WINDOW = 128
ATTN_BLOCK = 128
ATTN_IN_WIDTH = (ATTN_Q_HEADS + 2 * ATTN_KV_HEADS) * ATTN_HEAD_DIM
ROPE_THETA = 10000.0

D_FF = -(-(8 * D_MODEL) // (3 * 256)) * 256
EPS = 1e-6


def rmsnorm(x, w):
    xf = x.astype(jnp.float32)
    y = xf * lax.rsqrt(jnp.mean(xf * xf, axis=-1, keepdims=True) + EPS)
    return (y * w.astype(jnp.float32)).astype(x.dtype)

def rope(x, positions):
    half = x.shape[-1] // 2
    inv_freq = ROPE_THETA ** (-jnp.arange(half, dtype=jnp.float32) / half)
    ang = positions.astype(jnp.float32)[..., None] * inv_freq
    cos = jnp.cos(ang)[:, :, None, :]
    sin = jnp.sin(ang)[:, :, None, :]
    xf = x.astype(jnp.float32)
    x1, x2 = xf[..., :half], xf[..., half:]
    return jnp.concatenate([x1 * cos - x2 * sin, x2 * cos + x1 * sin], axis=-1)

def mlstm_chunkwise(q, k, v, log_i, log_f):
    B, H, S, dk = q.shape
    dv = v.shape[-1]
    L = MLSTM_CHUNK
    NC = S // L
    q = q.reshape(B, H, NC, L, dk)
    k = k.reshape(B, H, NC, L, dk)
    v = v.reshape(B, H, NC, L, dv)
    log_i = log_i.reshape(B, H, NC, L)
    b = jnp.cumsum(log_f.reshape(B, H, NC, L), axis=-1)
    b_last = b[..., -1]

    a = b_last[..., None] - b + log_i
    a_max = jnp.max(a, axis=-1)
    w = jnp.exp(a - a_max[..., None])
    kv_chunk = jnp.einsum('bhcl,bhcld,bhcle->bhcde', w, k, v)
    k_chunk = jnp.einsum('bhcl,bhcld->bhcd', w, k)

    def step(carry, xs):
        C, n, m = carry
        kv_c, k_c, bl_c, am_c = xs
        m_new = jnp.maximum(bl_c + m, am_c)
        s_prev = jnp.exp(bl_c + m - m_new)
        s_cur = jnp.exp(am_c - m_new)
        C_new = s_prev[..., None, None] * C + s_cur[..., None, None] * kv_c
        n_new = s_prev[..., None] * n + s_cur[..., None] * k_c
        return (C_new, n_new, m_new), (C, n, m)

    init = (jnp.zeros((B, H, dk, dv), jnp.float32),
            jnp.zeros((B, H, dk), jnp.float32),
            jnp.zeros((B, H), jnp.float32))
    xs = (jnp.moveaxis(kv_chunk, 2, 0), jnp.moveaxis(k_chunk, 2, 0),
          jnp.moveaxis(b_last, 2, 0), jnp.moveaxis(a_max, 2, 0))
    _, (C_prev, n_prev, m_prev) = lax.scan(step, init, xs)
    C_prev = jnp.moveaxis(C_prev, 0, 2)
    n_prev = jnp.moveaxis(n_prev, 0, 2)
    m_prev = jnp.moveaxis(m_prev, 0, 2)

    tril = jnp.tril(jnp.ones((L, L), dtype=bool))
    D = b[..., :, None] - b[..., None, :] + log_i[..., None, :]
    D = jnp.where(tril, D, -jnp.inf)
    g = b + m_prev[..., None]
    m_t = jnp.maximum(g, jnp.max(D, axis=-1))
    s = jnp.einsum('bhcld,bhcsd->bhcls', q, k) * jnp.exp(D - m_t[..., None])
    inter = jnp.exp(g - m_t)
    num = (jnp.einsum('bhcls,bhcse->bhcle', s, v)
           + inter[..., None] * jnp.einsum('bhcld,bhcde->bhcle', q, C_prev))
    den = jnp.sum(s, axis=-1) + inter * jnp.einsum('bhcld,bhcd->bhcl', q, n_prev)
    den = jnp.maximum(jnp.abs(den), jnp.exp(-m_t))
    return (num / den[..., None]).reshape(B, H, S, dv)

def mlstm_mixer(h, w_in, b_gate, norm_w, w_out):
    B, S, _ = h.shape
    H, dk, dv = MLSTM_HEADS, MLSTM_QK_DIM, MLSTM_V_DIM
    proj = h @ w_in
    o1 = H * dk
    o2 = 2 * H * dk
    o3 = o2 + D_MODEL
    o4 = o3 + D_MODEL
    q = proj[..., :o1].reshape(B, S, H, dk).transpose(0, 2, 1, 3).astype(jnp.float32) * (dk ** -0.5)
    k = proj[..., o1:o2].reshape(B, S, H, dk).transpose(0, 2, 1, 3).astype(jnp.float32)
    v = proj[..., o2:o3].reshape(B, S, H, dv).transpose(0, 2, 1, 3).astype(jnp.float32)
    o_gate = jax.nn.sigmoid(proj[..., o3:o4].astype(jnp.float32))
    gates = (proj[..., o4:] + b_gate).astype(jnp.float32)
    gates = gates.reshape(B, S, 4, H).transpose(2, 0, 3, 1)
    i_fwd, f_fwd, i_bwd, f_bwd = gates[0], gates[1], gates[2], gates[3]

    h_fwd = mlstm_chunkwise(q, k, v, i_fwd, jax.nn.log_sigmoid(f_fwd))
    flip = lambda t: t[:, :, ::-1]
    h_bwd = flip(mlstm_chunkwise(flip(q), flip(k), flip(v), flip(i_bwd),
                                 flip(jax.nn.log_sigmoid(f_bwd))))
    hs = h_fwd + h_bwd
    hs = hs * lax.rsqrt(jnp.mean(hs * hs, axis=-1, keepdims=True) + EPS)
    hs = hs.transpose(0, 2, 1, 3).reshape(B, S, H * dv) * norm_w.astype(jnp.float32)
    return (hs * o_gate).astype(h.dtype) @ w_out

def window_attn_mixer(h, positions, w_in, sink, w_out):
    B, S, _ = h.shape
    Hq, Hkv, G, hd, L = ATTN_Q_HEADS, ATTN_KV_HEADS, ATTN_GROUP, ATTN_HEAD_DIM, ATTN_BLOCK
    NB = S // L
    proj = h @ w_in
    q = proj[..., :Hq * hd].reshape(B, S, Hq, hd)
    k = proj[..., Hq * hd:(Hq + Hkv) * hd].reshape(B, S, Hkv, hd)
    v = proj[..., (Hq + Hkv) * hd:].reshape(B, S, Hkv, hd)
    q = rope(q, positions).reshape(B, NB, L, Hkv, G, hd)
    k = rope(k, positions)

    def band(t):
        tp = jnp.pad(t, ((0, 0), (L, L), (0, 0), (0, 0))).reshape(B, NB + 2, L, Hkv, hd)
        return jnp.concatenate([tp[:, :-2], tp[:, 1:-1], tp[:, 2:]], axis=2)

    k_band = band(k)
    v_band = band(v).astype(jnp.float32)
    scores = jnp.einsum('bcqhgd,bckhd->bchgqk', q, k_band) * (hd ** -0.5)

    qi = jnp.arange(L)
    kj = jnp.arange(3 * L)
    in_window = jnp.abs(kj[None, :] - L - qi[:, None]) <= WINDOW
    k_pos = jnp.arange(NB)[:, None] * L - L + kj[None, :]
    k_valid = (k_pos >= 0) & (k_pos < S)
    mask = in_window[None, :, :] & k_valid[:, None, :]
    scores = jnp.where(mask[None, :, None, None], scores, -jnp.inf)

    sink_l = sink.astype(jnp.float32).reshape(Hkv, G)[None, None, :, :, None]
    m = jnp.maximum(jnp.max(scores, axis=-1), sink_l)
    p = jnp.exp(scores - m[..., None])
    denom = jnp.sum(p, axis=-1) + jnp.exp(sink_l - m)
    out = jnp.einsum('bchgqk,bckhd->bcqhgd', p, v_band)
    out = out / denom.transpose(0, 1, 4, 2, 3)[..., None]
    return out.reshape(B, S, Hq * hd).astype(h.dtype) @ w_out

def swiglu(h, w_in, w_out):
    gu = h @ w_in
    gate, up = gu[..., :D_FF], gu[..., D_FF:]
    return (jax.nn.silu(gate) * up) @ w_out

def first_inputs(seed: int = 0) -> dict:
    key = jax.random.key(seed)
    ks = jax.random.split(key, 16)
    f32 = jnp.float32

    def w(k, shape, fan_in):
        return jax.random.normal(k, shape, f32) * (fan_in ** -0.5)

    x = jax.random.normal(ks[0], (BATCH, SEQ, D_MODEL), f32)
    positions = jnp.broadcast_to(jnp.arange(SEQ, dtype=jnp.int32), (BATCH, SEQ))
    norm_mix_w = 1.0 + 0.02 * jax.random.normal(ks[1], (DEPTH, D_MODEL), f32)
    norm_ffn_w = 1.0 + 0.02 * jax.random.normal(ks[2], (DEPTH, D_MODEL), f32)
    norm_final_w = 1.0 + 0.02 * jax.random.normal(ks[3], (D_MODEL,), f32)

    mlstm_w_in = w(ks[4], (N_MLSTM_LAYERS, D_MODEL, MLSTM_IN_WIDTH), D_MODEL)
    fbias = jnp.linspace(FGATE_BIAS_LO, FGATE_BIAS_HI, MLSTM_HEADS, dtype=f32)
    base = jnp.stack([jnp.zeros_like(fbias), fbias, jnp.zeros_like(fbias), fbias], axis=0)
    mlstm_b_gate = (base[None] + 0.1 * jax.random.normal(ks[5], (N_MLSTM_LAYERS, 4, MLSTM_HEADS), f32)
                    ).reshape(N_MLSTM_LAYERS, MLSTM_N_GATES)
    mlstm_norm_w = 1.0 + 0.02 * jax.random.normal(ks[6], (N_MLSTM_LAYERS, D_MODEL), f32)
    mlstm_w_out = w(ks[7], (N_MLSTM_LAYERS, D_MODEL, D_MODEL), D_MODEL)

    attn_w_in = w(ks[8], (N_ATTN_LAYERS, D_MODEL, ATTN_IN_WIDTH), D_MODEL)
    attn_sink = 0.5 * jax.random.normal(ks[9], (N_ATTN_LAYERS, ATTN_Q_HEADS), f32)
    attn_w_out = w(ks[10], (N_ATTN_LAYERS, ATTN_Q_HEADS * ATTN_HEAD_DIM, D_MODEL), ATTN_Q_HEADS * ATTN_HEAD_DIM)

    ffn_w_in = w(ks[11], (DEPTH, D_MODEL, 2 * D_FF), D_MODEL)
    ffn_w_out = w(ks[12], (DEPTH, D_FF, D_MODEL), D_FF)
    return {"x": x, "positions": positions, "norm_mix_w": norm_mix_w, "norm_ffn_w": norm_ffn_w,
            "norm_final_w": norm_final_w, "mlstm_w_in": mlstm_w_in, "mlstm_b_gate": mlstm_b_gate,
            "mlstm_norm_w": mlstm_norm_w, "mlstm_w_out": mlstm_w_out, "attn_w_in": attn_w_in,
            "attn_sink": attn_sink, "attn_w_out": attn_w_out, "ffn_w_in": ffn_w_in,
            "ffn_w_out": ffn_w_out}

def first_block(x, positions, norm_mix_w, norm_ffn_w, norm_final_w, mlstm_w_in, mlstm_b_gate,
              mlstm_norm_w, mlstm_w_out, attn_w_in, attn_sink, attn_w_out, ffn_w_in, ffn_w_out):
    for i in range(DEPTH):
        j = i // N_MIXERS
        hn = rmsnorm(x, norm_mix_w[i])
        if i % N_MIXERS == 0:
            x = x + mlstm_mixer(hn, mlstm_w_in[j], mlstm_b_gate[j], mlstm_norm_w[j], mlstm_w_out[j])
        else:
            x = x + window_attn_mixer(hn, positions, attn_w_in[j], attn_sink[j], attn_w_out[j])
        x = x + swiglu(rmsnorm(x, norm_ffn_w[i]), ffn_w_in[i], ffn_w_out[i])
    return rmsnorm(x, norm_final_w)


DEPTH_2 = 1

N_META = 16
BLOCK_Q = 128
RMS_EPS = 1e-6

MLA_HEADS = 16
MLA_Q_RANK = 256
MLA_KV_RANK = 128
MLA_NOPE_DIM = 64
MLA_ROPE_DIM = 32
MLA_V_DIM = 64
MLA_WIDTH = MLA_HEADS * MLA_V_DIM
MLA_SCALE = 1.0 / math.sqrt(MLA_NOPE_DIM + MLA_ROPE_DIM)

FOX_HEADS = 16
FOX_HEAD_DIM = 64
FOX_WIDTH = FOX_HEADS * FOX_HEAD_DIM
FOX_SCALE = 1.0 / math.sqrt(FOX_HEAD_DIM)

IN_SPLITS = (MLA_Q_RANK, MLA_KV_RANK, MLA_ROPE_DIM, MLA_WIDTH,
             FOX_WIDTH, FOX_WIDTH, FOX_WIDTH, FOX_HEADS, FOX_WIDTH,
             D_MODEL, D_MODEL)
IN_WIDTH = sum(IN_SPLITS)


def rmsnorm_2(x, g):
    xf = x.astype(jnp.float32)
    y = xf * lax.rsqrt(jnp.mean(xf * xf, axis=-1, keepdims=True) + RMS_EPS)
    return (y * g.astype(jnp.float32)).astype(x.dtype)

def rope_2(x, pos):
    half = x.shape[-1] // 2
    inv_freq = ROPE_THETA ** (-jnp.arange(half, dtype=jnp.float32) / half)
    ang = pos.astype(jnp.float32)[:, None] * inv_freq[None, :]
    cos, sin = jnp.cos(ang), jnp.sin(ang)
    x1 = x[..., :half].astype(jnp.float32)
    x2 = x[..., half:].astype(jnp.float32)
    return jnp.concatenate([x1 * cos - x2 * sin, x1 * sin + x2 * cos], axis=-1).astype(x.dtype)

def causal_block_attention(q, k, v, scale, cum=None):
    B, H, L, _ = q.shape
    n_real = L - N_META
    nb = n_real // BLOCK_Q
    key_pos = jnp.arange(L)

    def attend(qb, qpos, cq=None):
        s = jnp.einsum('bhqd,bhkd->bhqk', qb, k, preferred_element_type=jnp.float32) * scale
        if cq is not None:
            s = s + (cq[..., :, None] - cum[:, :, None, :])
        s = jnp.where(key_pos[None, :] <= qpos[:, None], s, -jnp.inf)
        p = jax.nn.softmax(s, axis=-1)
        return jnp.einsum('bhqk,bhkd->bhqd', p.astype(v.dtype), v)

    out_meta = attend(q[:, :, :N_META], key_pos[:N_META],
                      None if cum is None else cum[:, :, :N_META])

    def to_blocks(a):
        a = a[:, :, N_META:]
        a = a.reshape((B, H, nb, BLOCK_Q) + a.shape[3:])
        return jnp.moveaxis(a, 2, 0)

    xs = (to_blocks(q), key_pos[N_META:].reshape(nb, BLOCK_Q))
    if cum is not None:
        xs = xs + (to_blocks(cum),)
    out_real = lax.map(lambda args: attend(*args), xs)
    out_real = jnp.moveaxis(out_real, 0, 2).reshape(B, H, n_real, v.shape[-1])
    return jnp.concatenate([out_meta, out_real], axis=2)

def second_inputs(seed: int = 0) -> dict:
    key = jax.random.key(seed)
    ks = jax.random.split(key, 13)
    f32 = jnp.float32

    def gain(k, n):
        return 1.0 + 0.1 * jax.random.normal(k, (DEPTH_2, n), f32)

    def dense(k, fan_in, fan_out):
        return jax.random.normal(k, (DEPTH_2, fan_in, fan_out), f32) * fan_in ** -0.5

    return {
        'x': jax.random.normal(ks[0], (BATCH, SEQ, D_MODEL), f32),
        'meta_tokens': jax.random.normal(ks[1], (N_META, D_MODEL), f32),
        'pre_norm_g': gain(ks[2], D_MODEL),
        'w_in': dense(ks[3], D_MODEL, IN_WIDTH),
        'fox_forget_b': jax.random.uniform(ks[4], (DEPTH_2, FOX_HEADS), f32, 1.0, 4.0),
        'mla_q_norm_g': gain(ks[5], MLA_Q_RANK),
        'mla_kv_norm_g': gain(ks[6], MLA_KV_RANK),
        'w_uq': dense(ks[7], MLA_Q_RANK, MLA_HEADS * (MLA_NOPE_DIM + MLA_ROPE_DIM)),
        'w_ukv': dense(ks[8], MLA_KV_RANK, MLA_HEADS * (MLA_NOPE_DIM + MLA_V_DIM)),
        'w_br_mla': dense(ks[9], MLA_WIDTH, D_MODEL),
        'w_br_fox': dense(ks[10], FOX_WIDTH, D_MODEL),
        'w_out': dense(ks[11], D_MODEL, D_MODEL),
        'post_norm_g': gain(ks[12], D_MODEL),
    }

def second_block(x, meta_tokens, pre_norm_g, w_in, fox_forget_b, mla_q_norm_g, mla_kv_norm_g,
              w_uq, w_ukv, w_br_mla, w_br_fox, w_out, post_norm_g):
    B, S, D = x.shape
    L = S + N_META
    pos = jnp.arange(L)
    h = jnp.concatenate([jnp.broadcast_to(meta_tokens[None].astype(x.dtype), (B, N_META, D)), x], axis=1)
    split_idx = np.cumsum(IN_SPLITS)[:-1].tolist()

    def fox_heads(t):
        return t.reshape(B, L, FOX_HEADS, FOX_HEAD_DIM).transpose(0, 2, 1, 3)

    for l in range(DEPTH_2):
        u = rmsnorm_2(h, pre_norm_g[l])
        proj = u @ w_in[l]
        (cq, ckv, k_pe_raw, z_mla, fq, fk, fv, f_logit, z_fox, gate_a, gate_b) = jnp.split(proj, split_idx, axis=-1)

        q = (rmsnorm_2(cq, mla_q_norm_g[l]) @ w_uq[l]).reshape(B, L, MLA_HEADS, MLA_NOPE_DIM + MLA_ROPE_DIM).transpose(0, 2, 1, 3)
        kv = (rmsnorm_2(ckv, mla_kv_norm_g[l]) @ w_ukv[l]).reshape(B, L, MLA_HEADS, MLA_NOPE_DIM + MLA_V_DIM).transpose(0, 2, 1, 3)
        q_nope, q_pe = q[..., :MLA_NOPE_DIM], q[..., MLA_NOPE_DIM:]
        k_nope, v_mla = kv[..., :MLA_NOPE_DIM], kv[..., MLA_NOPE_DIM:]
        k_pe = rope_2(k_pe_raw, pos)[:, None]
        q_m = jnp.concatenate([q_nope, rope_2(q_pe, pos)], axis=-1)
        k_m = jnp.concatenate([k_nope, jnp.broadcast_to(k_pe, (B, MLA_HEADS, L, MLA_ROPE_DIM))], axis=-1)
        o_mla = causal_block_attention(q_m, k_m, v_mla, MLA_SCALE)
        o_mla = o_mla.transpose(0, 2, 1, 3).reshape(B, L, MLA_WIDTH)
        y_mla = (o_mla * jax.nn.silu(z_mla)) @ w_br_mla[l]

        log_f = jax.nn.log_sigmoid((f_logit + fox_forget_b[l]).astype(jnp.float32)).transpose(0, 2, 1)
        cum = jnp.cumsum(log_f, axis=-1)
        o_fox = causal_block_attention(fox_heads(fq), fox_heads(fk), fox_heads(fv), FOX_SCALE, cum)
        o_fox = o_fox.transpose(0, 2, 1, 3).reshape(B, L, FOX_WIDTH)
        y_fox = (o_fox * jax.nn.silu(z_fox)) @ w_br_fox[l]

        mixed = (jax.nn.sigmoid(gate_a) * y_mla + jax.nn.sigmoid(gate_b) * y_fox) @ w_out[l]
        h = h + rmsnorm_2(mixed, post_norm_g[l])

    return h[:, N_META:]


def setup_inputs(seed=0):
    out = dict(first_inputs(seed))
    for name, value in second_inputs(seed + 1).items():
        if name != "x":
            out[name + "_2"] = value
    return out


def reference(
    x, positions, norm_mix_w, norm_ffn_w, norm_final_w, mlstm_w_in, mlstm_b_gate, mlstm_norm_w,
    mlstm_w_out, attn_w_in, attn_sink, attn_w_out, ffn_w_in, ffn_w_out, meta_tokens_2,
    pre_norm_g_2, w_in_2, fox_forget_b_2, mla_q_norm_g_2, mla_kv_norm_g_2, w_uq_2, w_ukv_2,
    w_br_mla_2, w_br_fox_2, w_out_2, post_norm_g_2,
):
    x = first_block(
        x, positions, norm_mix_w, norm_ffn_w, norm_final_w, mlstm_w_in, mlstm_b_gate,
        mlstm_norm_w, mlstm_w_out, attn_w_in, attn_sink, attn_w_out, ffn_w_in, ffn_w_out,
    )
    return second_block(
        x, meta_tokens_2, pre_norm_g_2, w_in_2, fox_forget_b_2, mla_q_norm_g_2, mla_kv_norm_g_2,
        w_uq_2, w_ukv_2, w_br_mla_2, w_br_fox_2, w_out_2, post_norm_g_2,
    )


_drawn_inputs = setup_inputs


def setup_inputs(seed=0):
    import zlib

    import numpy as np

    out = dict(_drawn_inputs(seed))
    spreads = {}
    factors = {'mlstm_norm_w': 3.129, 'attn_sink': 40.634, 'norm_ffn_w': 3.12}
    for name, (base, spread) in spreads.items():
        noise = np.random.default_rng([zlib.crc32(name.encode()), seed]).standard_normal(out[name].shape)
        drawn = base * np.exp(spread * noise) if base else spread * noise
        out[name] = __import__('jax').numpy.asarray(drawn.astype(out[name].dtype))
    for name, factor in factors.items():
        out[name] = (out[name] * factor).astype(out[name].dtype)
    return out
```

```python
from contextlib import ExitStack

import numpy as np

import concourse.bass as bass
from concourse import mybir
from concourse.alu_op_type import AluOpType as ALU

F32 = mybir.dt.float32
F32R = mybir.dt.float32r
I32 = mybir.dt.int32
ACT = mybir.ActivationFunctionType
AX = mybir.AxisListType.X

P = 128
R = 2
S = P * R
M = 16
L = M + S
D = 1024
KT = D // P
CH = 512
EPS = 1e-6
NEG = -1e30

H0, DK, DV = 4, 128, 256
VW = DV + 2
HD = 64
NH = 16
FB = 11
TWO_PI = 2.0 * np.pi

C_MQ, C_MK, C_MV, C_MO, C_MOUT = 0, 1, 2, 4, 6
C_FFN = (8, 24)
C_AKV, C_AQ, C_AOUT = 19, 20, 22
C_C0, C_FK, C_FQ, C_FV, C_ZM, C_BRM, C_GA, C_ZF, C_BRF, C_GB, C_OUT = 35, 36, 38, 40, 42, 44, 46, 48, 50, 52, 54
N_CHUNKS = 56
U_GATES, U_DOWN, U_K, U_V, U_Q = 0, (1, 23), 45, 46, 47
N_UNITS = 51

PC = {}
_at = 0
for _name, _n in (("norm_mix0", 8), ("norm_mix1", 8), ("norm_ffn0", 8), ("norm_ffn1", 8), ("mlstm_norm", 8),
                  ("pre_norm", 8), ("q_norm", 2), ("kv_norm", 1), ("b_gate", 4), ("fox_b", 1), ("inv_freq", 1),
                  ("sign", 1), ("sink", 16)):
    PC[_name] = _at
    _at += _n
N_PC = _at

L0_CONST = 2 * P + H0 * P
L1_CONST = R * S
B2_CONST = L + S + L + P
KC0 = 464


def acc_plan():
    keys = [("gates",)]
    keys += [("mq", b) for b in range(4)] + [("mk", b) for b in range(4)]
    keys += [(n, c, r) for n in ("mv", "mo", "mout") for c in range(2) for r in range(R)]
    keys += [("ffn0", f, r) for f in range(FB) for r in range(R)]
    keys += [("ak", b) for b in range(2)] + [("av", r) for r in range(R)]
    keys += [("aq", b) for b in range(8)]
    keys += [("aout", c, r) for c in range(2) for r in range(R)]
    keys += [("ffn1", f, r) for f in range(FB) for r in range(R)]
    keys += [("c0", t) for t in range(3)]
    keys += [("uk", p) for p in range(8)] + [("uv", t, c) for t in range(3) for c in range(2)]
    keys += [("uq", 0)]
    for n in range(NH):
        if n + 1 < NH:
            keys.append(("uq", n + 1))
        keys += MLA_RIDERS[n]
    for n in range(NH):
        keys += FOX_RIDERS[n]
    keys += [("zf", 1, r) for r in range(R)]
    keys += [(n, c, r) for n in ("brf", "gb", "out") for c in range(2) for r in range(R)]
    assert len(set(keys)) == len(keys)
    return {k: n for n, k in enumerate(keys)}


MLA_RIDERS = [[("fk", 2 * n), ("fk", 2 * n + 1)] for n in range(4)]
MLA_RIDERS += [[("fq", 2 * n), ("fq", 2 * n + 1)] for n in range(4)]
MLA_RIDERS += [[("fv", c, t)] for c in range(2) for t in range(3)]
MLA_RIDERS += [[("zm", 0, r)] for r in range(R)]
FOX_RIDERS = [[("zm", 1, r)] for r in range(R)]
FOX_RIDERS += [[("brm", c, r)] for c in range(2) for r in range(R)]
FOX_RIDERS += [[("ga", c, r)] for c in range(2) for r in range(R)]
FOX_RIDERS += [[("zf", 0, r)] for r in range(R)]
FOX_RIDERS += [[], [], [], []]
USE = acc_plan()

ST_TILES = {"x0": 8, "m_out": 8, "f0": 8, "x1": 8, "a_out": 8, "f1": 8, "u": 8, "cqkv": 3, "o_mla": 8, "o_fox": 8, "mixed": 8}
LAST = {("mq", 3): C_MQ, ("mk", 3): C_MK, ("av", 1): C_AKV, ("aq", 3): C_AQ, ("aq", 7): C_AQ + 1, ("c0", 2): C_C0,
        ("fk", 3): C_FK, ("fk", 7): C_FK + 1, ("fq", 3): C_FQ, ("fq", 7): C_FQ + 1}
for _name, _c in (("mv", C_MV), ("mo", C_MO), ("mout", C_MOUT), ("aout", C_AOUT), ("zm", C_ZM), ("brm", C_BRM),
                  ("ga", C_GA), ("zf", C_ZF), ("brf", C_BRF), ("gb", C_GB), ("out", C_OUT)):
    for _j in range(2):
        LAST[(_name, _j, 1)] = _c + _j
for _j in range(2):
    LAST[("fv", _j, 2)] = C_FV + _j
ZN = {k: i for i, k in enumerate([("zm", c, r) for c in range(2) for r in range(R)] + [("ga", c, r) for c in range(2) for r in range(R)]
                                 + [("zf", c, r) for c in range(2) for r in range(R)] + [("gb", c, r) for c in range(2) for r in range(R)])}
ST = {}
_at = 0
for _name, _n in ST_TILES.items():
    ST[_name] = _at
    _at += _n
Z_FINAL = 18
RMS = {n: i for i, n in enumerate(("x0", "hs", "f0", "x1", "f1", "fin", "u", "cqkv", "post"))}


def two_blocks(nc, w_main, w_side, params, rows, c_l0, c_l1, c_b2, ident_d, x_d, meta_d, pos_d, negcum_d, out_d):
    ctx = ExitStack()
    with ctx:
        def sb(name, shape, dt=F32):
            return ctx.enter_context(nc.sbuf_tensor(name, shape, dt))

        def sem(name):
            return ctx.enter_context(nc.semaphore(name))

        bank = [ctx.enter_context(nc.psum_tensor(f"bank{i}", [P, 512], F32)) for i in range(8)]
        acc, tp = bank[0:2], bank[2:4]

        w_raw = sb("w_raw", [P, 2, 4, CH])
        w_hi = sb("w_hi", [P, 2, KT, CH], F32R)
        w_lo = sb("w_lo", [P, 2, KT, CH], F32R)
        s_raw = sb("s_raw", [P, 2, D])
        s_hi = sb("s_hi", [P, 2, D], F32R)
        s_lo = sb("s_lo", [P, 2, D], F32R)
        h = sb("h", [P, R, D])
        x_hi = sb("x_hi", [P, KT, L], F32R)
        x_lo = sb("x_lo", [P, KT, L], F32R)
        g_hi = sb("g_hi", [P, 3 * L], F32R)
        g_lo = sb("g_lo", [P, 3 * L], F32R)
        ident = sb("ident", [P, P])
        par = sb("par", [P, N_PC])
        stat = sb("stat", [P, 40])
        small = sb("small", [P, 42])
        ffn_nat = sb("ffn_nat", [P, 2, R, 256])
        zero_r = g_hi[:, 512:512 + P]
        arena = sb("arena", [P, 17232])

        def ar(off, *shape):
            n = int(np.prod(shape))
            v = arena[:, off:off + n]
            names = "abcd"[:len(shape)]
            if len(shape) == 1:
                return v
            return v.rearrange(f"p ({' '.join(names)}) -> p {' '.join(names)}", **dict(zip(names[1:], shape[1:])))

        def pcol(name, k=0, n=1):
            return par[:, PC[name] + k:PC[name] + k + n]

        y_hi = s_hi[:, :, :].rearrange("p a b -> p (a b)").rearrange("p (k t) -> p k t", k=KT)
        y_lo = s_lo[:, :, :].rearrange("p a b -> p (a b)").rearrange("p (k t) -> p k t", k=KT)
        ffh = g_hi[:, 0:512].rearrange("p (k t) -> p k t", k=2)
        ffl = g_lo[:, 0:512].rearrange("p (k t) -> p k t", k=2)
        cst_h = g_hi[:, :].rearrange("p (k t) -> p k t", k=3)
        cst_l = g_lo[:, :].rearrange("p (k t) -> p k t", k=3)

        XN = ar(4224, R, D)
        mqT, mkT, m_kn = ar(0, H0, S), ar(1024, H0, S), ar(2048, R, H0, DK)
        v_aug, o_gate = ar(6272, R, H0, VW), ar(8336, R, D)
        l0c = ar(10384, L0_CONST)
        m_mask = l0c[:, 0:2 * P].rearrange("p (a b) -> p a b", a=2)
        m_sel = l0c[:, 2 * P:].rearrange("p (a b) -> p a b", a=H0)
        g_rows = ar(11152, 4, S)
        row_a, row_b, row_c, row_m, row_n = (ar(12176 + 512 * i, 2, S) for i in range(5))
        row_i, row_e, row_w = ar(14736, 2, P), ar(14992, 2, S), ar(15504, 2, P)
        row_1 = ar(3072, 2, S)
        mcol = ar(15760, 40)
        m_t = ar(15800, 2, R, P)
        m_sd = ar(16312, 2, R, P)
        m_qi = ar(16824, 2, P)
        m_kw = ar(3328, P)
        m_ei, m_sq = ar(3072, 2, P), ar(15800, DV)
        m_c = ar(3584, 2, VW)
        aqT, akT, a_v, a_mask = ar(0, 8, S), ar(2048, 2, S), ar(2560, R, S), ar(3072, R, S)
        cosT, sinT, a_o = ar(3584, S), ar(3840, S), ar(6272, R, D)
        a_sw, a_tmp, ang = ar(8320, 2, S), ar(8832, 2, S), ar(9344, 3, S)
        pos_i = ar(11648, S).bitcast(I32)
        a_sm, a_pt = ar(10112, 2, R, S), ar(11136, 4, P)
        fkT, fqT, f_v, f_vm = ar(0, 8, L), ar(2176, 8, S), s_raw[:, :, :], ar(6272, D)
        kT, v_m, v_mm = ar(7296, NH, L), ar(11648, R, D), ar(13696, D)
        o_fox, y_mix = ar(7296, R, D), ar(9344, R, D)
        q_h, sm, pt = ar(14720, 2, S), ar(15232, 2, 416), ar(16064, 640)
        b2c, b2k = ar(16704, L + S), ar(15232, L + P)
        c_mask, q_tab, k_tab, k_sum = b2c[:, 0:L], b2c[:, L:], b2k[:, 0:L], b2k[:, L:]
        cn, cqn = ar(0, 3, KC0), ar(1392, 3, 384)
        hm, um = ar(13696, D), ar(11648, D)
        kp, f_row = ar(2560, L), ar(2832, 4, L)
        o_mla = XN
        cum, mc = ar(11648, 2, 2, L), ar(12736, 2, 2, 416)
        z_t = ffn_nat[:, :, :, :].rearrange("p a r n -> p a (r n)")
        row_g = ar(6272, D)

        w_landed = [sem("w_landed0"), sem("w_landed1")]
        w_hi_ok, w_lo_ok = sem("w_hi_ok"), sem("w_lo_ok")
        s_landed = [sem("s_landed0"), sem("s_landed1")]
        s_hi_ok, s_lo_ok, s_used = sem("s_hi_ok"), sem("s_lo_ok"), sem("s_used")
        acc_ready = [sem("acc_ready0"), sem("acc_ready1")]
        acc_free = [sem("acc_free0"), sem("acc_free1")]
        tp_ready, st_hi_ok, st_lo_ok = sem("tp_ready"), sem("st_hi_ok"), sem("st_lo_ok")
        xn_ready = sem("xn_ready")
        h_ready = sem("h_ready")
        ss_ok, var_ok, root_ok, rstd_ok = sem("ss_ok"), sem("var_ok"), sem("root_ok"), sem("rstd_ok")
        in_landed, meta_landed, c0_landed, c1_landed, c2_landed = (
            sem("in_landed"), sem("meta_landed"), sem("c0_landed"), sem("c1_landed"), sem("c2_landed"))
        pos_landed, rowg_landed = sem("pos_landed"), [sem("rowg_landed0"), sem("rowg_landed1")]
        silu_ok, g_tp, g_hi_ok, g_lo_ok = sem("silu_ok"), sem("g_tp"), sem("g_hi_ok"), sem("g_lo_ok")
        zero_ok = sem("zero_ok")
        out_landed = sem("out_landed")

        def landed(i):
            return 16 * (i + 1)

        block = ctx.enter_context(nc.Block())

        gr_ok, fa_ok, fe_ok, rows_ok, mc_ps, mc_ok = (sem(n) for n in ("gr_ok", "fa_ok", "fe_ok", "rows_ok", "mc_ps", "mc_ok"))
        kn_ps, kn_ok, bc_ps, t_ok, in_ps, ei_ok = (sem(n) for n in ("kn_ps", "kn_ok", "bc_ps", "t_ok", "in_ps", "ei_ok"))
        s0_ps, wt_ok, sd_ok, kw_ok, c_ps, c_ok, qi_ok = (sem(n) for n in ("s0_ps", "wt_ok", "sd_ok", "kw_ok", "c_ps", "c_ok", "qi_ok"))
        n_ps, rd_ok, hf_ok, n_done, hs_ok, va_ok = (sem(n) for n in ("n_ps", "rd_ok", "hf_ok", "n_done", "hs_ok", "va_ok"))
        ang_ok, tab_ok, sw_ok, rot_ok = (sem(n) for n in ("ang_ok", "tab_ok", "sw_ok", "rot_ok"))
        sc_ps, nm_ok, p_ok, pt_ps, pt_ok, ptm_ok, o_ps, o_ok = (
            sem(n) for n in ("sc_ps", "nm_ok", "p_ok", "pt_ps", "pt_ok", "ptm_ok", "o_ps", "o_ok"))
        k_ok = sem("k_ok")
        f_ps, f1_ok, f2_ok, ncum_ok, ncum_stored, kpe_ps, kp_ok, kr_ps = (
            sem(n) for n in ("f_ps", "f1_ok", "f2_ok", "ncum_ok", "ncum_stored", "kpe_ps", "kp_ok", "kr_ps"))
        cum_landed = [sem("cum_landed0"), sem("cum_landed1")]
        mc_made, th_ok, z_ok = sem("mc_made"), sem("th_ok"), sem("z_ok")
        A1, A2, A3 = 0, NH, 2 * NH

        @block.sync
        def _(sp):
            def main_half(c, g):
                dst = w_raw[:, g, :, :].rearrange("p k n -> p (k n)")
                sp.dma_start(dst, w_main[c, g]).then_inc(w_landed[g], 16)

            def main(c):
                for g in range(2):
                    sp.wait_ge(w_lo_ok, 2 * c - 1 + g)
                    main_half(c, g)

            def side(u, slot):
                sp.wait_ge(s_lo_ok, u - 1)
                sp.dma_start(s_raw[:, slot, :], w_side[u]).then_inc(s_landed[slot], 16)

            sp.dma_start(h[:, :, :], x_d.rearrange("(r p) d -> p r d", p=P)).then_inc(in_landed, 16)
            sp.dma_start(par[:, :], params).then_inc(in_landed, 16)
            sp.dma_start(ident[:, :], ident_d).then_inc(in_landed, 16)
            for g in range(2):
                main_half(0, g)
            for u in range(2):
                sp.dma_start(s_raw[:, u, :], w_side[u]).then_inc(s_landed[u], 16)
            main(1)
            main(2)
            side(2, 0)
            with sp.Fori(3, C_FFN[0] + 2) as c:
                main(c)

            def ffn(layer):
                c0, u0 = C_FFN[layer] + 2, U_DOWN[layer] + 2
                with sp.Fori(0, FB - 1) as i:
                    main(c0 + i)
                    for s in range(2):
                        side(u0 + 2 * i + s, (u0 + s) % 2)

            ffn(0)
            main(C_AKV + 1)
            for u in (U_DOWN[1], U_DOWN[1] + 1):
                side(u, u % 2)
            with sp.Fori(C_AKV + 2, C_FFN[1] + 2) as c:
                main(c)
            ffn(1)
            for c, units in ((C_FK, (U_K, U_V)), (C_FK + 1, (U_Q, U_Q + 1)), (C_FQ, (U_Q + 2,)), (C_FQ + 1, (U_Q + 3,))):
                main(c)
                for u in units:
                    side(u, u % 2)
            with sp.Fori(C_FV, N_CHUNKS) as c:
                main(c)
            sp.wait_ge(z_ok, Z_FINAL)
            sp.dma_start(out_d.rearrange("(r p) d -> p r d", p=P), XN).then_inc(out_landed, 16)
            sp.wait_ge(out_landed, 16)

        @block.gpsimd
        def _(pool):
            pool.memset(stat[:, :], 1.0)
            pool.memset(zero_r.bitcast(F32), 0.0).then_inc(zero_ok, 1)
            pool.memset(row_1[0:H0, :, :], 1.0)
            pool.memset(v_aug[:, :, :, DV:DV + 1], 1.0)
            pool.memset(v_aug[:, :, :, DV + 1:VW], 0.0).then_inc(va_ok, 1)
            pool.dma_start(l0c, c_l0).then_inc(c0_landed, 16)
            pool.wait_ge(h_ready, 1)
            pool.dma_start(a_mask, c_l1.rearrange("p (r s) -> p r s", r=R)).then_inc(c1_landed, 16)
            pool.dma_start(pos_i[:, :], pos_d.to_broadcast([P, S])).then_inc(pos_landed, 16)
            pool.wait_ge(h_ready, 3)
            pool.dma_start(b2c, c_b2[:, 0:L + S]).then_inc(c2_landed, 16)
            pool.dma_start(b2k, c_b2[:, L + S:]).then_inc(c2_landed, 16)
            pool.dma_start(hm[0:M, :], meta_d).then_inc(meta_landed, 16)
            pool.dma_start(row_g, rows[0]).then_inc(rowg_landed[0], 16)
            pool.wait_ge(ncum_ok, 1)
            pool.dma_start(negcum_d, f_row[0:NH, 3, :]).then_inc(ncum_stored, 16)
            pool.wait_ge(ncum_stored, 16)
            pool.wait_ge(o_ok, A3)
            for p in range(8):
                if p >= 2:
                    pool.wait_ge(nm_ok, A3 + 2 * (p - 2) + 2)
                pool.dma_start(cum[:, p % 2, :, :],
                               negcum_d[2 * p:2 * p + 2, :].rearrange("(a b) l -> a b l", a=1).to_broadcast([P, 2, L])
                               ).then_inc(cum_landed[p % 2], 16)
                pool.wait_ge(cum_landed[p % 2], landed(p // 2))
                for t, (a, b, k0) in enumerate(((0, M + P, P), (M + P, 416, 0))):
                    pool.tensor_tensor(mc[:, p % 2, :, a:b], cum[:, p % 2, :, 0:b - a],
                                       c_mask[:, k0:L].rearrange("p (a l) -> p a l", a=1).to_broadcast([P, 2, b - a]),
                                       ALU.add).then_inc(mc_made, 1)
            pool.wait_ge(o_ok, 3 * NH)
            pool.dma_start(row_g, rows[1]).then_inc(rowg_landed[1], 16)

        @block.tensor
        def _(pe):
            def mm3(out, ah, al, bh, bl, first, last):
                pe.matmul(out, ah, bh, start=first, stop=False)
                pe.matmul(out, ah, bl, start=False, stop=False)
                return pe.matmul(out, al, bh, start=False, stop=last)

            def acc_wait(key):
                n = USE[key]
                if n >= 2:
                    pe.wait_ge(acc_free[n % 2], n // 2)
                return acc[n % 2]

            def done(ins, key):
                ins.then_inc(acc_ready[USE[key] % 2], 1)

            def tok_cols(t):
                return slice(0, P) if t == 2 else slice(M + t * P, M + (t + 1) * P)

            def part_a(c, key, t, k0, k1, sh=x_hi, sl=x_lo, n0=0, n1=CH, moved=0):
                bank_ = acc_wait(key) if k0 == 0 else acc[USE[key] % 2]
                cols = tok_cols(t)
                if moved:
                    cols = slice(cols.start - moved, cols.stop - moved)
                for k in range(k0, k1):
                    if k % 4 == 0:
                        pe.wait_ge(w_lo_ok, 2 * c + k // 4 + 1)
                    ins = mm3(bank_[:, 0:n1 - n0], sh[:, k, cols], sl[:, k, cols],
                              w_hi[:, c % 2, k, n0:n1], w_lo[:, c % 2, k, n0:n1], k == 0, k == KT - 1)
                if k1 == KT:
                    done(ins, key)

            def part_b(c, key, b, t0):
                bank_ = acc_wait(key)
                for k in range(KT):
                    if k % 4 == 0:
                        pe.wait_ge(w_lo_ok, 2 * c + k // 4 + 1)
                    ins = mm3(bank_[:, 0:L - t0], w_hi[:, c % 2, k, b * P:(b + 1) * P], w_lo[:, c % 2, k, b * P:(b + 1) * P],
                              x_hi[:, k, t0:L], x_lo[:, k, t0:L], k == 0, k == KT - 1)
                done(ins, key)

            def evacuated(*keys):
                for key in keys:
                    pe.wait_ge(acc_free[USE[key] % 2], USE[key] // 2 + 1)

            def to_stationary(name, src, sem_, value, meta=None):
                pe.wait_ge(sem_, value)
                for k in range(ST_TILES[name]):
                    n = ST[name] + k
                    if n >= 2:
                        pe.wait_ge(st_lo_ok, n - 1)
                    b = tp[n % 2]
                    if meta is not None:
                        pe.transpose(b[:, 0:M], meta(k), ident[0:M, 0:M])
                    for r in range(R):
                        ins = pe.transpose(b[:, M + r * P:M + (r + 1) * P], src(r, k), ident[:, :])
                    ins.then_inc(tp_ready, 1)

            def st_wait(name, k=None):
                pe.wait_ge(st_lo_ok, ST[name] + (ST_TILES[name] if k is None else k + 1))

            def xn(r, k):
                return XN[:, r, k * P:(k + 1) * P]

            pe.wait_ge(in_landed, 48)
            to_stationary("x0", xn, xn_ready, 1)
            st_wait("x0")
            b = acc_wait(("gates",))
            pe.wait_ge(s_lo_ok, U_GATES + 1)
            for k in range(KT):
                ins = mm3(b[:, 0:S], s_hi[:, 0, k * P:(k + 1) * P], s_lo[:, 0, k * P:(k + 1) * P],
                          x_hi[:, k, M:L], x_lo[:, k, M:L], k == 0, k == KT - 1)
            done(ins, ("gates",))
            for b in range(4):
                part_b(C_MQ, ("mq", b), b, M)
            for b in range(4):
                part_b(C_MK, ("mk", b), b, M)
            for c in range(2):
                for r in range(R):
                    part_a(C_MV + c, ("mv", c, r), r, 0, KT)

            for r in range(R):
                if r == 0:
                    evacuated(("mk", 2), ("mk", 3))
                if r:
                    pe.wait_ge(kn_ok, 1)
                for hh in range(H0):
                    ins = pe.transpose(bank[4][:, hh * P:(hh + 1) * P], mkT[:, hh, r * P:(r + 1) * P], ident[:, :])
                ins.then_inc(kn_ps, 1)
            pe.wait_ge(rows_ok, 1)
            for d in range(2):
                for r in range(R):
                    a = (d * R + r) * H0
                    pe.transpose(bank[5][:, a:a + H0], row_c[0:H0, d, r * P:(r + 1) * P], ident[0:H0, 0:H0])
                    pe.transpose(bank[5][:, 16 + a:16 + a + H0], row_e[0:H0, d, r * P:(r + 1) * P], ident[0:H0, 0:H0])
            for d in range(2):
                ins = pe.transpose(bank[5][:, 32 + d * H0:32 + (d + 1) * H0], row_w[0:H0, d, :], ident[0:H0, 0:H0])
            ins.then_inc(mc_ps, 1)
            for c in range(2):
                for r in range(R):
                    part_a(C_MO + c, ("mo", c, r), r, 0, KT)

            pe.wait_ge(c0_landed, 16)
            for hh in range(H0):
                if hh:
                    pe.wait_ge(t_ok, hh)
                    pe.wait_ge(ei_ok, hh)
                pe.matmul(bank[3][:, :], m_sel[0:H0, hh, :], row_n[0:H0, :, :].rearrange("p a b -> p (a b)"),
                          start=True, stop=True).then_inc(bc_ps, 1)
                pe.matmul(bank[2][:, 0:2 * P], m_sel[0:H0, hh, :], row_i[0:H0, :, :].rearrange("p a b -> p (a b)"),
                          start=True, stop=True).then_inc(in_ps, 1)
                if hh:
                    pe.wait_ge(sd_ok, hh)
                pe.wait_ge(kn_ok, 2)
                for r in range(R):
                    ins = pe.matmul(bank[4][:, r * P:(r + 1) * P], mkT[:, hh, r * P:(r + 1) * P],
                                    mqT[:, hh, r * P:(r + 1) * P], start=True, stop=True)
                ins.then_inc(s0_ps, 1)
                for d in range(2):
                    n = 2 * hh + d
                    pe.wait_ge(kw_ok, n + 1)
                    if n:
                        pe.wait_ge(c_ok, n)
                    else:
                        pe.wait_ge(va_ok, 1)
                        evacuated(("mv", 1, 0), ("mv", 1, 1))
                    pe.matmul(bank[5][:, 0:VW], m_kw[:, :], v_aug[:, d, hh, :], start=True, stop=True).then_inc(c_ps, 1)
                pe.wait_ge(sd_ok, hh + 1)
                for r in range(R):
                    for d in range(2):
                        n = 4 * hh + 2 * r + d
                        if n >= 2:
                            pe.wait_ge(n_done if d else hf_ok, n // 2)
                        second = (r == 1 - d)
                        ins = pe.matmul(bank[6 + n % 2][:, 0:VW], m_sd[:, d, r, :], v_aug[:, r, hh, :], start=True,
                                        stop=not second)
                        if second:
                            pe.wait_ge(c_ok, 2 * hh + d + 1)
                            pe.wait_ge(qi_ok, hh + 1)
                            ins = pe.matmul(bank[6 + n % 2][:, 0:VW], m_qi[:, d, :], m_c[:, d, :], start=False, stop=True)
                        ins.then_inc(n_ps, 1)

            to_stationary("m_out", xn, xn_ready, 2)
            st_wait("m_out")
            for c in range(2):
                for r in range(R):
                    part_a(C_MOUT + c, ("mout", c, r), r, 0, KT)

            def ffn(layer, n_xn):
                name, c0, u0 = f"ffn{layer}", C_FFN[layer], U_DOWN[layer]
                n0 = USE[(name, 0, 0)]
                to_stationary(f"f{layer}", xn, xn_ready, n_xn)
                st_wait(f"f{layer}")

                def up(f, j, transposes):
                    slot = (c0 + j) % 2
                    for r in range(R):
                        b_ = (n0 + r) % 2
                        pe.wait_ge(acc_free[b_], (n0 + r) // 2 + f)
                        for k in range(KT):
                            if r == 0 and k % 4 == 0:
                                pe.wait_ge(w_lo_ok, 2 * (c0 + f) + k // 4 + 1)
                            if transposes and r == 0 and k == 4:
                                turn(f - 1)
                            cols = tok_cols(r)
                            ins = mm3(acc[b_][:, :], x_hi[:, k, cols], x_lo[:, k, cols],
                                      w_hi[:, slot, k, :], w_lo[:, slot, k, :], k == 0, k == KT - 1)
                        ins.then_inc(acc_ready[b_], 1)

                def turn(f):
                    for r in range(R):
                        pe.wait_ge(acc_free[(n0 + r) % 2], (n0 + r) // 2 + f + 1)
                    for ks in range(2):
                        for r in range(R):
                            ins = pe.transpose(bank[2][:, ks * S + r * P:ks * S + (r + 1) * P],
                                               ffn_nat[:, 1, r, ks * P:(ks + 1) * P], ident[:, :])
                    ins.then_inc(g_tp, 1)

                def down(f, first=False, final=False):
                    pe.wait_ge(g_lo_ok, FB * layer + f + 1)
                    for ks in range(2):
                        slot = (u0 + ks) % 2
                        pe.wait_ge(s_lo_ok, u0 + 2 * f + ks + 1)
                        for r in range(R):
                            for cc in range(2):
                                ins = mm3(bank[4 + 2 * r + cc][:, :], ffh[:, ks, r * P:(r + 1) * P],
                                          ffl[:, ks, r * P:(r + 1) * P], s_hi[:, slot, cc * CH:(cc + 1) * CH],
                                          s_lo[:, slot, cc * CH:(cc + 1) * CH], False, final and ks == 1)
                        ins.then_inc(s_used, 1)

                pe.wait_ge(zero_ok, 1)
                for i in range(4):
                    for q in range(4):
                        pe.matmul(bank[4 + i][:, q * P:(q + 1) * P], zero_r, zero_r,
                                  start=(q == 0), stop=False)
                up(0, 0, False)
                with pe.Fori(0, (FB - 1) // 2) as i:
                    up(2 * i + 1, 1, True)
                    down(2 * i)
                    up(2 * i + 2, 2, True)
                    down(2 * i + 1)
                turn(FB - 1)
                down(FB - 1, final=True)

            ffn(0, 3)

            to_stationary("x1", xn, xn_ready, 4)
            st_wait("x1")
            for b in range(2):
                part_b(C_AKV, ("ak", b), b, M)
            for r in range(R):
                part_a(C_AKV, ("av", r), r, 0, KT, n0=256, n1=512)
            for b in range(8):
                part_b(C_AQ + b // 4, ("aq", b), b % 4, M)

            def a_scores(n):
                a = 64 * (n % 2)
                if n == 0:
                    pe.wait_ge(rot_ok, 10)
                if n:
                    pe.wait_ge(nm_ok, n)
                for r in range(R):
                    ins = pe.matmul(bank[4][:, r * S:(r + 1) * S], aqT[a:a + HD, n // 2, r * P:(r + 1) * P],
                                    akT[a:a + HD, n // 8, :], start=True, stop=True)
                ins.then_inc(sc_ps, 1)

            def a_turn(n):
                pe.wait_ge(p_ok, n + 1)
                if n:
                    pe.wait_ge(pt_ok, n)
                for r in range(R):
                    for kt in range(2):
                        ins = pe.transpose(bank[5][:, (kt * 2 + r) * P:(kt * 2 + r + 1) * P],
                                           a_sm[:, n % 2, r, kt * P:(kt + 1) * P], ident[:, :])
                ins.then_inc(pt_ps, 1)

            def a_values(n):
                pe.wait_ge(pt_ok, n + 1)
                if n:
                    pe.wait_ge(o_ok, n)
                else:
                    evacuated(("av", 0), ("av", 1))
                g = 2 * (n // 8) + n % 2
                for r in range(R):
                    for kt in range(2):
                        ins = pe.matmul(bank[7][:, r * HD:(r + 1) * HD], a_pt[:, kt * 2 + r, :],
                                        a_v[:, kt, g * HD:(g + 1) * HD], start=(kt == 0), stop=(kt == 1))
                ins.then_inc(o_ps, 1)

            for n in range(NH + 1):
                if n < NH:
                    a_scores(n)
                if n:
                    a_turn(n - 1)
                    a_values(n - 1)

            to_stationary("a_out", lambda r, k: a_o[:, r, k * P:(k + 1) * P], o_ok, NH)
            st_wait("a_out")
            for c in range(2):
                for r in range(R):
                    part_a(C_AOUT + c, ("aout", c, r), r, 0, KT)
            ffn(1, 5)

            to_stationary("u", xn, xn_ready, 6, meta=lambda k: um[0:M, k * P:(k + 1) * P])
            st_wait("u")
            for i, t in enumerate((2, 0, 1)):
                part_a(C_C0, ("c0", i), t, 0, KT, n1=KC0)
            evacuated(("c0", 1), ("c0", 2))
            pe.wait_ge(c2_landed, 32)
            for t, a, n in ((0, 0, M), (1, M, P), (2, M + P, P)):
                ins = pe.transpose(bank[4][0:NH, a:a + n], cn[0:n, t, 448:464], ident[0:n, 0:n])
            ins.then_inc(f_ps, 1)
            for t, a, n in ((0, 0, M), (1, M, P), (2, M + P, P)):
                ins = pe.transpose(bank[5][0:64, a:a + n], cn[0:n, t, 384:448], ident[0:n, 0:n])
            ins.then_inc(kpe_ps, 1)
            to_stationary("cqkv", lambda r, k: cqn[:, 1 + r, k * P:(k + 1) * P], xn_ready, 7,
                          meta=lambda k: cqn[0:M, 0, k * P:(k + 1) * P])
            pe.wait_ge(kp_ok, 1)
            pe.matmul(bank[6][:, 0:L], k_sum[0:64, :], kp[0:64, :], start=True, stop=True).then_inc(kr_ps, 1)
            st_wait("cqkv")
            for p in range(8):
                b = acc_wait(("uk", p))
                pe.wait_ge(s_lo_ok, U_K + 1)
                sl = U_K % 2
                done(mm3(b[:, 0:L], s_hi[:, sl, p * P:(p + 1) * P], s_lo[:, sl, p * P:(p + 1) * P],
                         cst_h[:, 2, :], cst_l[:, 2, :], True, True), ("uk", p))
            for i, t in enumerate((2, 0, 1)):
                for cc in range(2):
                    b = acc_wait(("uv", i, cc))
                    pe.wait_ge(s_lo_ok, U_V + 1)
                    sl = U_V % 2
                    done(mm3(b[:, :], cst_h[:, 2, tok_cols(t)], cst_l[:, 2, tok_cols(t)],
                             s_hi[:, sl, cc * CH:(cc + 1) * CH], s_lo[:, sl, cc * CH:(cc + 1) * CH], True, True),
                         ("uv", i, cc))

            def mla_query(n):
                b = acc_wait(("uq", n))
                u = U_Q + n // 4
                pe.wait_ge(s_lo_ok, u + 1)
                for ks in range(2):
                    a = ks * CH + (n % 4) * P
                    ins = mm3(b[:, 0:S], s_hi[:, u % 2, a:a + P], s_lo[:, u % 2, a:a + P],
                              cst_h[:, ks, M:L], cst_l[:, ks, M:L], ks == 0, ks == 1)
                done(ins, ("uq", n))

            def scores(n, q, k):
                pe.wait_ge(nm_ok, n)
                pe.matmul(bank[4][:, 0:M + P], q(0), k(M + P), start=True, stop=True)
                pe.matmul(bank[4][:, M + P:416], q(1), k(L), start=True, stop=True).then_inc(sc_ps, 1)

            def turn(n):
                pe.wait_ge(p_ok, n + 1)
                pe.wait_ge(pt_ok, n)
                if n > A2:
                    pe.wait_ge(ptm_ok, n - A2)
                s_ = sm[:, n % 2, :]
                pe.transpose(bank[5][:, 0:P], s_[:, M:M + P], ident[:, :])
                pe.transpose(bank[5][:, P:2 * P], s_[:, 2 * M + P:2 * M + 2 * P], ident[:, :])
                pe.transpose(bank[5][:, 2 * P:3 * P], s_[:, 2 * M + 2 * P:416], ident[:, :])
                pe.transpose(bank[6][0:M, 0:P], s_[:, 0:M], ident[:, :])
                pe.transpose(bank[6][0:M, P:2 * P], s_[:, M + P:2 * M + P], ident[:, :]).then_inc(pt_ps, 1)

            def values(n, v, vm):
                pe.wait_ge(pt_ok, n + 1)
                pe.wait_ge(ptm_ok, n - A2 + 1)
                pe.wait_ge(o_ok, n)
                pe.matmul(bank[7][:, 0:HD], pt[0:M, 384:384 + P], vm, start=True, stop=False)
                pe.matmul(bank[7][:, 0:HD], pt[:, 0:P], v(0), start=False, stop=True)
                pe.matmul(bank[7][:, HD:2 * HD], pt[0:M, 384 + P:640], vm, start=True, stop=False)
                pe.matmul(bank[7][:, HD:2 * HD], pt[:, P:2 * P], v(0), start=False, stop=False)
                pe.matmul(bank[7][:, HD:2 * HD], pt[:, 2 * P:3 * P], v(1), start=False, stop=True).then_inc(o_ps, 1)

            def rider(key, half):
                kind = key[0]
                if kind in ("fk", "fq"):
                    b = key[1]
                    c = (C_FK if kind == "fk" else C_FQ) + b // 4
                    part_b(c, key, b % 4, 0 if kind == "fk" else M)
                    return
                c = {"fv": C_FV, "zm": C_ZM, "brm": C_BRM, "ga": C_GA, "zf": C_ZF, "brf": C_BRF, "gb": C_GB,
                     "out": C_OUT}[kind] + key[1]
                t = (2, 0, 1)[key[2]] if kind == "fv" else key[2]
                y = kind in ("brm", "brf", "out")
                part_a(c, key, t, 4 * half, 4 * half + 4, sh=y_hi if y else x_hi, sl=y_lo if y else x_lo,
                       moved=M if y else 0)

            def riders(keys, half):
                if len(keys) == 2:
                    rider(keys[half], 0)
                elif keys:
                    rider(keys[0], half)

            mla_query(0)
            for n in range(NH):
                if n == 0:
                    pe.wait_ge(k_ok, 1)
                    evacuated(("uk", 6), ("uk", 7))
                evacuated(("uq", n))
                scores(A2 + n, lambda r: q_h[:, n % 2, r * P:(r + 1) * P], lambda e: kT[:, n, 0:e])
                if n + 1 < NH:
                    mla_query(n + 1)
                riders(MLA_RIDERS[n], 0)
                turn(A2 + n)
                riders(MLA_RIDERS[n], 1)
                if n == 0:
                    evacuated(("uv", 2, 0), ("uv", 2, 1))
                values(A2 + n, lambda r: v_m[:, r, n * HD:(n + 1) * HD], v_mm[0:M, n * HD:(n + 1) * HD])

            for n in range(NH):
                a = 64 * (n % 2)
                if n == 0:
                    evacuated(("fv", 1, 1), ("fv", 1, 2))
                if n == 2:
                    to_stationary("o_mla", lambda r, k: o_mla[:, r, k * P:(k + 1) * P], z_ok, 4)
                    st_wait("o_mla")
                scores(A3 + n, lambda r: fqT[a:a + HD, n // 2, r * P:(r + 1) * P], lambda e: fkT[a:a + HD, n // 2, 0:e])
                riders(FOX_RIDERS[n], 0)
                turn(A3 + n)
                riders(FOX_RIDERS[n], 1)
                values(A3 + n, lambda r: f_v[:, r, n * HD:(n + 1) * HD], f_vm[0:M, n * HD:(n + 1) * HD])

            for r in range(R):
                for half in range(2):
                    rider(("zf", 1, r), half)
            to_stationary("o_fox", lambda r, k: o_fox[:, r, k * P:(k + 1) * P], z_ok, 12)
            st_wait("o_fox")
            for name in ("brf", "gb", "out"):
                if name == "out":
                    to_stationary("mixed", lambda r, k: y_mix[:, r, k * P:(k + 1) * P], z_ok, 16)
                    st_wait("mixed")
                for c in range(2):
                    for r in range(R):
                        for half in range(2):
                            rider((name, c, r), half)

        @block.scalar
        def _(act):
            def split_main(c, slot):
                for g in range(2):
                    act.wait_ge(w_landed[g], 16 * c + 16)
                    act.activation(w_hi[:, slot, 4 * g:4 * g + 4, :], w_raw[:, g, :, :], ACT.Copy).then_inc(w_hi_ok, 1)

            def split_side(u, after=None):
                act.wait_ge(s_landed[u % 2], 16 * (u // 2 + 1))
                if after is not None:
                    act.wait_ge(acc_ready[USE[after] % 2], USE[after] // 2 + 1)
                act.activation(s_hi[:, u % 2, :], s_raw[:, u % 2, :], ACT.Copy).then_inc(s_hi_ok, 1)

            def acc_in(key):
                n = USE[key]
                act.wait_ge(acc_ready[n % 2], n // 2 + 1)
                return acc[n % 2]

            def freed(ins, key):
                ins.then_inc(acc_free[USE[key] % 2], 1)
                if key in LAST and LAST[key] + 2 < N_CHUNKS:
                    split_main(LAST[key] + 2, LAST[key] % 2)

            def carry(out, key, width=CH, scale=1.0, rows=P):
                b = acc_in(key)
                freed(act.activation(out, b[0:rows, 0:width], ACT.Copy, scale=scale), key)

            def split_st(name, hi, scale=None, a=M):
                for k in range(ST_TILES[name]):
                    n = ST[name] + k
                    act.wait_ge(tp_ready, n + 1)
                    sc = 1.0 if scale is None else scale(k)
                    act.activation(hi(k), tp[n % 2][:, a:L], ACT.Copy, scale=sc).then_inc(st_hi_ok, 1)

            def root(name, n):
                act.wait_ge(var_ok, RMS[name] + 1)
                act.activation(stat[:, 16:16 + n], stat[:, 8:8 + n], ACT.Ln)
                act.drain()
                act.activation(stat[:, 16:16 + n], stat[:, 16:16 + n], ACT.Exp, scale=-0.5).then_inc(root_ok, 1)

            def sums(name, src, after, value, meta=None):
                act.wait_ge(after, value)
                if meta is not None:
                    act.activation(um[0:M, :], meta, ACT.Square, accum_out=stat[0:M, R:R + 1])
                for r in range(R):
                    ins = act.activation(XN[:, r, :], src[:, r, :], ACT.Square, accum_out=stat[:, r:r + 1])
                ins.then_inc(ss_ok, 1)
                root(name, R + (meta is not None))

            def x_tile(t, a=M):
                return lambda k: t[:, k, a:L]

            act.wait_ge(zero_ok, 1)
            sums("x0", h, in_landed, 48)
            split_side(0)
            for c in range(2):
                split_main(c, c)
            split_side(1)
            split_st("x0", x_tile(x_hi), lambda k: pcol("norm_mix0", k))
            b = acc_in(("gates",))
            for g in range(4):
                ins = act.activation(g_rows[0:H0, g, :], b[32 * g:32 * g + H0, 0:S], ACT.Copy)
            freed(ins, ("gates",))
            split_side(2, after=("gates",))
            for b in range(4):
                carry(mqT[:, b, :], ("mq", b), S, DK ** -0.5)
            act.wait_ge(fa_ok, 1)
            act.activation(row_b[0:H0, :, :], row_a[0:H0, :, :], ACT.Exp, scale=-1.0)
            act.drain()
            act.activation(row_b[0:H0, :, :], row_b[0:H0, :, :], ACT.Ln, bias=1.0).then_inc(fe_ok, 1)
            for b in range(4):
                carry(mkT[:, b, :], ("mk", b), S)
            for c in range(2):
                for r in range(R):
                    carry(v_aug[:, r, 2 * c:2 * c + 2, 0:DV], ("mv", c, r))
            for r in range(R):
                act.wait_ge(kn_ps, r + 1)
                act.activation(m_kn[:, r, :, :], bank[4][:, :].rearrange("p (a b) -> p a b", a=H0), ACT.Copy).then_inc(kn_ok, 1)
            act.wait_ge(mc_ps, 1)
            act.activation(mcol[:, 0:16], bank[5][:, 0:16], ACT.Copy)
            act.activation(mcol[:, 16:40], bank[5][:, 16:40], ACT.Exp).then_inc(mc_ok, 1)
            for c in range(2):
                for r in range(R):
                    key = ("mo", c, r)
                    b = acc_in(key)
                    freed(act.activation(o_gate[:, r, c * CH:(c + 1) * CH], b[:, :], ACT.Sigmoid), key)

            for hh in range(H0):
                act.wait_ge(in_ps, hh + 1)
                if hh:
                    act.wait_ge(qi_ok, hh)
                act.activation(m_ei[:, :, :], bank[2][:, 0:2 * P], ACT.Exp).then_inc(ei_ok, 1)
                act.wait_ge(t_ok, hh + 1)
                for d in range(2):
                    for r in range(R):
                        a = (d * R + r) * H0 + hh
                        ins = act.activation(m_t[:, d, r, :], m_t[:, d, r, :], ACT.Exp, bias=mcol[:, a:a + 1])
                ins.then_inc(wt_ok, 1)
                for d in range(2):
                    n = 2 * hh + d
                    act.wait_ge(c_ps, n + 1)
                    if hh:
                        act.wait_ge(n_ps, 4 * hh)
                    act.activation(m_c[:, d, :], bank[5][:, 0:VW], ACT.Copy).then_inc(c_ok, 1)
                for r in range(R):
                    n = 4 * hh + 2 * r
                    act.wait_ge(rd_ok, 2 * hh + r + 1)
                    act.activation(XN[:, r, hh * DV:(hh + 1) * DV], bank[6 + n % 2][:, 0:DV], ACT.Copy,
                                   scale=small[:, 2:3]).then_inc(hf_ok, 1)
            act.wait_ge(n_done, 8)
            for r in range(R):
                for hh in range(H0):
                    if r + hh:
                        act.drain()
                    ins = act.activation(m_sq, XN[:, r, hh * DV:(hh + 1) * DV], ACT.Square,
                                         accum_out=stat[:, 4 * r + hh:4 * r + hh + 1])
            ins.then_inc(ss_ok, 1)
            root("hs", 8)
            split_st("m_out", x_tile(x_hi), lambda k: pcol("mlstm_norm", k))
            for c in range(2):
                act.wait_ge(acc_ready[USE[("mout", c, 1)] % 2], USE[("mout", c, 1)] // 2 + 1)
                split_main(8 + c, c)

            def ffn(layer):
                c0, u0, n0 = C_FFN[layer], U_DOWN[layer], USE[(f"ffn{layer}", 0, 0)]

                def gate(f):
                    for r in range(R):
                        act.wait_ge(acc_ready[(n0 + r) % 2], (n0 + r) // 2 + f + 1)
                        act.activation(ffn_nat[:, 0, r, :], acc[(n0 + r) % 2][:, 0:256], ACT.Silu).then_inc(silu_ok, 1)

                def turned(f):
                    act.wait_ge(g_tp, FB * layer + f + 1)
                    act.activation(ffh, bank[2][:, :], ACT.Copy).then_inc(g_hi_ok, 1)

                def block_(f, j):
                    turned(f - 1)
                    gate(f)
                    split_main(c0 + f + 2, (c0 + j) % 2)
                    for s in range(2):
                        slot = (u0 + s) % 2
                        act.wait_ge(s_used, u0 + 2 * f + s - 2)
                        act.wait_ge(s_landed[slot], 16 * (f + (u0 + s) // 2 + 1))
                        act.activation(s_hi[:, slot, :], s_raw[:, slot, :], ACT.Copy).then_inc(s_hi_ok, 1)

                gate(0)
                split_main(c0 + 2, c0 % 2)
                with act.Fori(0, (FB - 1) // 2) as i:
                    block_(2 * i + 1, 1)
                    block_(2 * i + 2, 2)
                turned(FB - 1)
                for u in (u0 + 2 * FB, u0 + 2 * FB + 1):
                    act.wait_ge(s_used, u - 2)
                    split_side(u)

            sums("f0", h, h_ready, 1)
            split_st("f0", x_tile(x_hi), lambda k: pcol("norm_ffn0", k))
            ffn(0)

            act.wait_ge(ang_ok, 1)
            act.activation(sinT, ang[:, 0, :], ACT.Sin)
            act.activation(cosT, ang[:, 1, :], ACT.Sin).then_inc(tab_ok, 1)
            sums("x1", h, h_ready, 2)
            split_st("x1", x_tile(x_hi), lambda k: pcol("norm_mix1", k))

            def swapped(i, key):
                b = acc_in(key)
                if i >= 2:
                    act.wait_ge(rot_ok, i - 1)
                for q in range(4):
                    ins = act.activation(a_sw[32 * (q ^ 1):32 * (q ^ 1) + 32, i % 2, :], b[32 * q:32 * q + 32, 0:S], ACT.Copy)
                ins.then_inc(sw_ok, 1)
                if key in LAST:
                    split_main(LAST[key] + 2, LAST[key] % 2)

            for b in range(2):
                swapped(b, ("ak", b))
            for r in range(R):
                carry(a_v[:, r, :], ("av", r), S)
            for b in range(8):
                swapped(2 + b, ("aq", b))

            def exps(n, tiles, s0, sink=None):
                act.wait_ge(nm_ok, n + 1)
                for r in range(R):
                    ins = act.activation(tiles(r), tiles(r), ACT.Exp, bias=small[:, s0 + 2 + r:s0 + 3 + r],
                                         accum_out=small[:, s0 + 4 + r:s0 + 5 + r])
                if sink is not None:
                    ins = act.activation(small[:, s0 + 6:s0 + 8], small[:, s0 + 2:s0 + 4], ACT.Exp, bias=sink)
                ins.then_inc(p_ok, 1)

            for n in range(NH):
                exps(n, lambda r: a_sm[:, n % 2, r, :], 8 * (n % 2), pcol("sink", n))
            split_st("a_out", x_tile(x_hi))
            for c in range(2):
                act.wait_ge(acc_ready[USE[("aout", c, 1)] % 2], USE[("aout", c, 1)] // 2 + 1)
                split_main(C_AOUT + 2 + c, C_AOUT % 2 if c == 0 else (C_AOUT + 1) % 2)
            sums("f1", h, h_ready, 3)
            split_st("f1", x_tile(x_hi), lambda k: pcol("norm_ffn1", k))
            ffn(1)

            sums("fin", h, h_ready, 4)
            act.wait_ge(meta_landed, 16)
            sums("u", h, h_ready, 5, meta=hm[0:M, :])
            split_st("u", x_tile(x_hi, 0), lambda k: pcol("pre_norm", k), a=0)
            for i in range(3):
                carry(cn[:, i, :], ("c0", i), KC0)
            act.drain()
            for i in range(3):
                act.activation(cqn[:, i, 0:256], cn[:, i, 0:256], ACT.Square, accum_out=stat[:, i:i + 1])
                ins = act.activation(cqn[:, i, 256:384], cn[:, i, 256:384], ACT.Square, accum_out=stat[:, 3 + i:4 + i])
            ins.then_inc(ss_ok, 1)
            root("cqkv", 6)
            act.wait_ge(f1_ok, 1)
            act.activation(f_row[0:NH, 2, :], f_row[0:NH, 1, :], ACT.Exp, scale=-1.0)
            act.drain()
            act.activation(f_row[0:NH, 2, :], f_row[0:NH, 2, :], ACT.Ln, bias=1.0).then_inc(f2_ok, 1)
            split_st("cqkv", x_tile(cst_h, 0), lambda k: pcol("q_norm", k), a=0)
            act.wait_ge(kr_ps, 1)
            act.activation(kT[64:P, :, :], bank[6][64:P, 0:L].rearrange("p (a l) -> p a l", a=1).to_broadcast([64, NH, L]),
                           ACT.Copy).then_inc(k_ok, 1)
            for p in range(0, 8):
                if USE[("uk", p)] % 2 == 0:
                    b = acc_in(("uk", p))
                    act.activation(kT[0:64, 2 * p, :], b[0:64, 0:L], ACT.Copy)
                    freed(act.activation(kT[0:64, 2 * p + 1, :], b[64:P, 0:L], ACT.Copy), ("uk", p))
            split_side(U_Q, after=("uk", 7))
            for i, t in enumerate((2, 0, 1)):
                for cc in range(2):
                    if t == 2:
                        carry(v_mm[0:M, cc * CH:(cc + 1) * CH], ("uv", i, cc), rows=M)
                    else:
                        carry(v_m[:, t, cc * CH:(cc + 1) * CH], ("uv", i, cc))
            split_side(U_Q + 1, after=("uv", 2, 1))

            def gate_in(key):
                i = ZN[key]
                b = acc_in(key)
                if i >= 2:
                    act.wait_ge(z_ok, i - 1)
                act.activation(z_t[:, i % 2, :], b[:, :], ACT.Tanh, scale=0.5).then_inc(th_ok, 1)
                if key in LAST and LAST[key] + 2 < N_CHUNKS:
                    split_main(LAST[key] + 2, LAST[key] % 2)

            def rider(key):
                kind = key[0]
                if kind == "fk":
                    carry(fkT[:, key[1], :], key, L)
                elif kind == "fq":
                    if key[1] == 0:
                        act.wait_ge(ncum_stored, 16)
                    carry(fqT[:, key[1], :], key, S, HD ** -0.5)
                elif kind == "fv":
                    if key[1:] == (0, 0):
                        act.wait_ge(s_lo_ok, N_UNITS)
                    cols = slice(key[1] * CH, (key[1] + 1) * CH)
                    if key[2] == 0:
                        carry(f_vm[0:M, cols], key, rows=M)
                    else:
                        carry(f_v[:, key[2] - 1, cols], key)
                elif kind == "brm":
                    carry(y_mix[:, key[2], key[1] * CH:(key[1] + 1) * CH], key, scale=0.5)
                elif kind == "brf":
                    carry(XN[:, key[2], key[1] * CH:(key[1] + 1) * CH], key, scale=0.5)
                elif kind == "out":
                    carry(o_fox[:, key[2], key[1] * CH:(key[1] + 1) * CH], key)
                else:
                    gate_in(key)

            def meta_turned(n):
                act.wait_ge(pt_ps, n + 1)
                act.wait_ge(o_ps, n)
                act.activation(pt[0:M, 384:640], bank[6][0:M, 0:2 * P], ACT.Copy).then_inc(ptm_ok, 1)

            for n in range(2 * NH):
                keys = MLA_RIDERS[n] if n < NH else FOX_RIDERS[n - NH]
                s_ = sm[:, n % 2, :]
                exps(A2 + n, lambda r: s_[:, 0:M + P] if r == 0 else s_[:, M + P:416], 8 * (n % 2))
                if n == NH + 2:
                    pass
                if len(keys) == 2:
                    rider(keys[0])
                meta_turned(A2 + n)
                if keys:
                    rider(keys[-1])
                if n in (3, 7):
                    split_side(U_Q + 2 + n // 4, after=("uq", n))
                if n == NH + 1:
                    split_st("o_mla", lambda k: y_hi[:, k, :])
            for r in range(R):
                rider(("zf", 1, r))
            split_st("o_fox", lambda k: y_hi[:, k, :])
            for name in ("brf", "gb", "out"):
                if name == "out":
                    split_st("mixed", lambda k: y_hi[:, k, :])
                for c in range(2):
                    for r in range(R):
                        rider((name, c, r))
            act.drain()
            for r in range(R):
                ins = act.activation(XN[:, r, :], o_fox[:, r, :], ACT.Square, accum_out=stat[:, r:r + 1])
            ins.then_inc(ss_ok, 1)
            root("post", R)

        @block.vector
        def _(dve):
            def rest_main(c, slot):
                for g in range(2):
                    dve.wait_ge(w_hi_ok, 2 * c + g + 1)
                    dve.tensor_tensor(w_lo[:, slot, 4 * g:4 * g + 4, :], w_raw[:, g, :, :],
                                      w_hi[:, slot, 4 * g:4 * g + 4, :], ALU.subtract).then_inc(w_lo_ok, 1)

            def rest_side(u):
                dve.wait_ge(s_hi_ok, u + 1)
                dve.tensor_tensor(s_lo[:, u % 2, :], s_raw[:, u % 2, :], s_hi[:, u % 2, :], ALU.subtract).then_inc(s_lo_ok, 1)

            def after_key(key):
                if key in LAST and LAST[key] + 2 < N_CHUNKS:
                    rest_main(LAST[key] + 2, LAST[key] % 2)

            def acc_in(key):
                n = USE[key]
                dve.wait_ge(acc_ready[n % 2], n // 2 + 1)
                return acc[n % 2]

            def rest_st(name, hi, lo, scale=None, a=M):
                for k in range(ST_TILES[name]):
                    n = ST[name] + k
                    dve.wait_ge(st_hi_ok, n + 1)
                    src = tp[n % 2][:, a:L]
                    if scale is None:
                        ins = dve.tensor_tensor(lo(k), src, hi(k), ALU.subtract)
                    else:
                        ins = dve.scalar_tensor_tensor(out=lo(k), in0=src, scalar=scale(k), in1=hi(k),
                                                       op0=ALU.mult, op1=ALU.subtract)
                    ins.then_inc(st_lo_ok, 1)

            def rstd(name, parts):
                i, n = RMS[name], sum(w for w, _ in parts)
                dve.wait_ge(ss_ok, i + 1)
                at = 0
                for w, width in parts:
                    ins = dve.tensor_scalar(stat[:, 8 + at:8 + at + w], stat[:, at:at + w], 1.0 / width, EPS, ALU.mult, ALU.add)
                    at += w
                ins.then_inc(var_ok, 1)
                dve.wait_ge(root_ok, i + 1)
                x, y, t = stat[:, 8:8 + n], stat[:, 16:16 + n], stat[:, 24:24 + n]
                dve.drain()
                dve.tensor_tensor(t, y, y, ALU.mult)
                dve.drain()
                dve.tensor_tensor(t, t, x, ALU.mult)
                dve.drain()
                dve.tensor_scalar(t, t, -0.5, 1.5, ALU.mult, ALU.add)
                dve.drain()
                dve.tensor_tensor(stat[:, 32:32 + n], y, t, ALU.mult)
                dve.drain()

            def root_col(k):
                return stat[:, 32 + k:33 + k]

            def x_tile(t, a=M):
                return lambda k: t[:, k, a:L]

            def scaled_rows(src):
                for r in range(R):
                    ins = dve.tensor_scalar(XN[:, r, :], src[:, r, :], root_col(r), None, ALU.mult)
                return ins

            dve.wait_ge(in_landed, 48)
            rstd("x0", [(R, D)])
            scaled_rows(h).then_inc(xn_ready, 1)
            rest_side(0)
            for c in range(2):
                rest_main(c, c)
            rest_side(1)
            rest_st("x0", x_tile(x_hi), x_tile(x_lo), lambda k: pcol("norm_mix0", k))
            n = USE[("gates",)]
            dve.wait_ge(acc_free[n % 2], n // 2 + 1)
            gr = g_rows[0:H0, :, :]
            dve.tensor_tensor(gr, gr, par[0:H0, PC["b_gate"]:PC["b_gate"] + 4].rearrange("p (a b) -> p a b", b=1)
                              .to_broadcast([H0, 4, S]), ALU.add)
            dve.drain()
            f2 = g_rows[0:H0, :, :].rearrange("p (d k) s -> p d k s", k=2)
            ig, fg = f2[:, :, 0, :], f2[:, :, 1, :]
            ra, rb, rc, rm, rn, re_ = (t[0:H0, :, :] for t in (row_a, row_b, row_c, row_m, row_n, row_e))
            dve.scalar_tensor_tensor(out=ra, in0=fg, scalar=-1.0, in1=fg, op0=ALU.mult, op1=ALU.max).then_inc(fa_ok, 1)
            rest_side(2)
            dve.wait_ge(fe_ok, 1)
            dve.drain()
            dve.scalar_tensor_tensor(out=ra, in0=fg, scalar=0.0, in1=rb, op0=ALU.min, op1=ALU.subtract)
            dve.drain()
            dve.wait_ge(va_ok, 1)

            def tile(t, d, r):
                v = t[:, d, r * P:(r + 1) * P]
                return v if d == 0 else v[:, ::-1]

            ones = row_1[0:H0, :, :]
            for d in range(2):
                for r in range(R):
                    dve.tensor_tensor_scan(tile(rb, d, r), tile(ones, d, r), tile(ra, d, r), 0.0, ALU.mult, ALU.add)
            dve.drain()
            dve.tensor_tensor(rc, ig, rb, ALU.subtract)
            dve.drain()
            last = [P - 1, P]
            for d in range(2):
                dve.tensor_tensor_scan(tile(rm, d, d), tile(rc, d, d), tile(rc, d, d), 0.0, ALU.max, ALU.max)
            dve.drain()
            for d in range(2):
                e = last[d]
                dve.tensor_tensor(small[0:H0, 40 + d:41 + d], rb[:, d, e:e + 1], rm[:, d, e:e + 1], ALU.add)
            dve.drain()
            for d in range(2):
                dve.tensor_tensor_scan(tile(rm, d, 1 - d), tile(rc, d, 1 - d), tile(rc, d, 1 - d), small[0:H0, 40 + d:41 + d],
                                       ALU.max, ALU.max)
            dve.drain()
            dve.tensor_scalar(rn, rm, -1.0, None, ALU.mult)
            dve.drain()
            dve.tensor_tensor(re_, rn, rb, ALU.subtract)
            for d in range(2):
                e = last[d]
                dve.tensor_scalar(row_i[0:H0, d, :], rn[:, d, (1 - d) * P:(2 - d) * P], small[0:H0, 40 + d:41 + d], None, ALU.add)
                ins = dve.tensor_scalar(row_w[0:H0, d, :], rc[:, d, d * P:(d + 1) * P], rn[:, d, e:e + 1], None, ALU.add)
            ins.then_inc(rows_ok, 1)
            for c in range(2, 8):
                rest_main(c, c % 2)

            dve.wait_ge(c0_landed, 16)
            dve.wait_ge(mc_ok, 1)
            dve.wait_ge(kn_ok, 2)
            for hh in range(H0):
                def state_keys(d):
                    n = 2 * hh + d
                    if n:
                        dve.wait_ge(c_ps, n)
                    a = 32 + d * H0 + hh
                    dve.tensor_scalar(m_kw, m_kn[:, d, hh, :], mcol[:, a:a + 1], None, ALU.mult).then_inc(kw_ok, 1)

                dve.wait_ge(bc_ps, hh + 1)
                for d in range(2):
                    ins = dve.tensor_tensor(m_t[:, d, :, :], bank[3][:, d * S:(d + 1) * S].rearrange("p (r l) -> p r l", r=R),
                                            m_mask[:, d, :].rearrange("p (a l) -> p a l", a=1).to_broadcast([P, R, P]), ALU.add)
                ins.then_inc(t_ok, 1)
                if hh:
                    dve.wait_ge(n_ps, 4 * hh)
                dve.wait_ge(ei_ok, hh + 1)
                for d in range(2):
                    ins = dve.tensor_tensor(m_qi[:, d, :], mqT[:, hh, (1 - d) * P:(2 - d) * P], m_ei[:, d, :], ALU.mult)
                ins.then_inc(qi_ok, 1)
                state_keys(0)
                dve.wait_ge(wt_ok, hh + 1)
                dve.wait_ge(s0_ps, hh + 1)
                for d in range(2):
                    ins = dve.tensor_tensor(m_sd[:, d, :, :], m_t[:, d, :, :], bank[4][:, 0:S].rearrange("p (r l) -> p r l", r=R),
                                            ALU.mult)
                ins.then_inc(sd_ok, 1)
                state_keys(1)
                dve.drain()
                for r in range(R):
                    for d in range(2):
                        n = 4 * hh + 2 * r + d
                        b = bank[6 + n % 2]
                        dve.wait_ge(n_ps, n + 1)
                        t = small[:, 0:1]
                        a = 16 + (d * R + r) * H0 + hh
                        dve.tensor_scalar(t, b[:, DV:DV + 1], -1.0, None, ALU.mult)
                        dve.drain()
                        dve.scalar_tensor_tensor(out=small[:, 1:2], in0=b[:, DV:DV + 1], scalar=mcol[:, a:a + 1], in1=t,
                                                 op0=ALU.max, op1=ALU.max)
                        dve.drain()
                        if d == 0:
                            dve.reciprocal(small[:, 2:3], small[:, 1:2]).then_inc(rd_ok, 1)
                        else:
                            dve.reciprocal(small[:, 3:4], small[:, 1:2])
                            dve.wait_ge(hf_ok, 2 * hh + r + 1)
                            dve.drain()
                            xs = XN[:, r, hh * DV:(hh + 1) * DV]
                            dve.scalar_tensor_tensor(out=xs, in0=b[:, 0:DV], scalar=small[:, 3:4], in1=xs,
                                                     op0=ALU.mult, op1=ALU.add).then_inc(n_done, 1)
            rstd("hs", [(8, DV)])
            for r in range(R):
                for hh in range(H0):
                    xs = XN[:, r, hh * DV:(hh + 1) * DV]
                    ins = dve.scalar_tensor_tensor(out=xs, in0=xs, scalar=root_col(4 * r + hh),
                                                   in1=o_gate[:, r, hh * DV:(hh + 1) * DV], op0=ALU.mult, op1=ALU.mult)
            ins.then_inc(xn_ready, 1)
            rest_st("m_out", x_tile(x_hi), x_tile(x_lo), lambda k: pcol("mlstm_norm", k))

            def residual(name):
                for c in range(2):
                    for r in range(R):
                        key = (name, c, r)
                        b = acc_in(key)
                        hs = h[:, r, c * CH:(c + 1) * CH]
                        dve.tensor_tensor(hs, hs, b[:, :], ALU.add).then_inc(acc_free[USE[key] % 2], 1)
                        if (c, r) == (1, 1):
                            dve.drain().then_inc(h_ready, 1)
                        after_key(key)

            residual("mout")

            def ffn(layer):
                c0, u0, n0 = C_FFN[layer], U_DOWN[layer], USE[(f"ffn{layer}", 0, 0)]

                def product(f):
                    for r in range(R):
                        b_ = (n0 + r) % 2
                        dve.wait_ge(silu_ok, 2 * FB * layer + 2 * f + r + 1)
                        dve.tensor_tensor(ffn_nat[:, 1, r, :], acc[b_][:, 256:512], ffn_nat[:, 0, r, :],
                                          ALU.mult).then_inc(acc_free[b_], 1)

                def turned(f):
                    dve.wait_ge(g_hi_ok, FB * layer + f + 1)
                    dve.tensor_tensor(ffl, bank[2][:, :].rearrange("p (k t) -> p k t", k=2), ffh,
                                      ALU.subtract).then_inc(g_lo_ok, 1)

                def block_(f, j):
                    turned(f - 1)
                    product(f)
                    rest_main(c0 + f + 2, (c0 + j) % 2)
                    for s in range(2):
                        slot = (u0 + s) % 2
                        dve.wait_ge(s_hi_ok, u0 + 2 * f + s + 1)
                        dve.tensor_tensor(s_lo[:, slot, :], s_raw[:, slot, :], s_hi[:, slot, :],
                                          ALU.subtract).then_inc(s_lo_ok, 1)

                product(0)
                rest_main(c0 + 2, c0 % 2)
                with dve.Fori(0, (FB - 1) // 2) as i:
                    block_(2 * i + 1, 1)
                    block_(2 * i + 2, 2)
                turned(FB - 1)
                dve.wait_ge(s_used, u0 + 2 * FB - 1)
                for r in range(R):
                    for cc in range(2):
                        hs = h[:, r, cc * CH:(cc + 1) * CH]
                        ins = dve.tensor_tensor(hs, hs, bank[4 + 2 * r + cc][:, :], ALU.add)
                ins.then_inc(h_ready, 1)
                dve.drain()
                for u in (u0 + 2 * FB, u0 + 2 * FB + 1):
                    rest_side(u)

            rstd("f0", [(R, D)])
            scaled_rows(h).then_inc(xn_ready, 1)
            rest_st("f0", x_tile(x_hi), x_tile(x_lo), lambda k: pcol("norm_ffn0", k))
            c1 = 6.28125
            c2 = float(np.float32(round((TWO_PI - c1) * 2 ** 21) / 2 ** 21))
            c3 = TWO_PI - c1 - c2
            big, lim = float(1.5 * 2 ** 23), 3.1415925
            dve.wait_ge(pos_landed, 16)
            dve.tensor_copy(ang[:, 0, :], pos_i[:, :])
            dve.drain()
            dve.tensor_scalar(ang[:, 0, :], ang[:, 0, :], pcol("inv_freq"), None, ALU.mult)
            dve.drain()
            dve.tensor_scalar(ang[:, 1, :], ang[:, 0, :], 1.0 / TWO_PI, big, ALU.mult, ALU.add)
            dve.drain()
            dve.tensor_scalar(ang[:, 1, :], ang[:, 1, :], big, None, ALU.subtract)
            for cw in (c1, c2, c3):
                dve.drain()
                dve.scalar_tensor_tensor(out=ang[:, 0, :], in0=ang[:, 1, :], scalar=-cw, in1=ang[:, 0, :],
                                         op0=ALU.mult, op1=ALU.add)
            dve.drain()
            dve.tensor_scalar(ang[:, 1, :], ang[:, 0, :], float(np.pi / 2), None, ALU.add)
            dve.drain()
            dve.tensor_scalar(ang[:, 2, :], ang[:, 1, :], float(np.pi), -TWO_PI, ALU.is_gt, ALU.mult)
            dve.drain()
            dve.tensor_tensor(ang[:, 1, :], ang[:, 1, :], ang[:, 2, :], ALU.add)
            dve.drain()
            dve.tensor_scalar(ang[:, 0:2, :], ang[:, 0:2, :], lim, -lim, ALU.min, ALU.max).then_inc(ang_ok, 1)
            ffn(0)

            rstd("x1", [(R, D)])
            scaled_rows(h).then_inc(xn_ready, 1)
            rest_st("x1", x_tile(x_hi), x_tile(x_lo), lambda k: pcol("norm_mix1", k))
            dve.wait_ge(tab_ok, 1)
            dve.tensor_scalar(sinT, sinT, pcol("sign"), None, ALU.mult)
            dve.drain()

            def rotated(i, key, out):
                n = USE[key]
                dve.wait_ge(sw_ok, i + 1)
                dve.tensor_tensor(a_tmp[:, i % 2, :], acc[n % 2][:, 0:S], cosT, ALU.mult).then_inc(acc_free[n % 2], 1)
                dve.tensor_tensor(a_sw[:, i % 2, :], a_sw[:, i % 2, :], sinT, ALU.mult)
                dve.drain()
                dve.tensor_tensor(out, a_tmp[:, i % 2, :], a_sw[:, i % 2, :], ALU.add).then_inc(rot_ok, 1)
                after_key(key)

            for b in range(2):
                rotated(b, ("ak", b), akT[:, b, :])
            after_key(("av", 1))
            for b in range(8):
                rotated(2 + b, ("aq", b), aqT[:, b, :])

            def masked(n, tiles, sources, masks, s0, scale=1.0, sink=None):
                dve.wait_ge(sc_ps, n + 1)
                if n >= 2:
                    dve.wait_ge(pt_ps, n - 1)
                for r in range(R):
                    dve.tensor_tensor_reduce(tiles(r), sources(r), masks(r), scale, float(np.finfo(np.float32).min), ALU.add, ALU.max,
                                             small[:, s0 + r:s0 + r + 1])
                dve.drain()
                mx, nm = small[:, s0:s0 + 2], small[:, s0 + 2:s0 + 4]
                if sink is None:
                    dve.tensor_scalar(nm, mx, -1.0, None, ALU.mult).then_inc(nm_ok, 1)
                else:
                    dve.tensor_scalar(nm, mx, sink, -1.0, ALU.max, ALU.mult).then_inc(nm_ok, 1)

            def attended(n, out, s0, sink=False):
                dve.wait_ge(p_ok, n + 1)
                den = small[:, s0 + 4:s0 + 6]
                if sink:
                    dve.tensor_tensor(den, den, small[:, s0 + 6:s0 + 8], ALU.add)
                    dve.drain()
                dve.reciprocal(small[:, s0 + 6:s0 + 8], den)
                dve.wait_ge(o_ps, n + 1)
                dve.drain()
                dve.tensor_tensor(out, bank[7][:, 0:R * HD].rearrange("p (r e) -> p r e", r=R),
                                  small[:, s0 + 6:s0 + 8].rearrange("p (r e) -> p r e", e=1).to_broadcast([P, R, HD]),
                                  ALU.mult).then_inc(o_ok, 1)

            dve.wait_ge(c1_landed, 16)
            for n in range(NH + 1):
                if n < NH:
                    masked(n, lambda r: a_sm[:, n % 2, r, :], lambda r: bank[4][:, r * S:(r + 1) * S],
                           lambda r: a_mask[:, r, :], 8 * (n % 2), HD ** -0.5, pcol("sink", n))
                if n:
                    m = n - 1
                    dve.wait_ge(pt_ps, m + 1)
                    if m:
                        dve.wait_ge(o_ps, m)
                    dve.tensor_copy(a_pt[:, :, :], bank[5][:, :].rearrange("p (a b) -> p a b", a=4)).then_inc(pt_ok, 1)
                    attended(m, a_o[:, :, m * HD:(m + 1) * HD], 8 * (m % 2), sink=True)
            rest_st("a_out", x_tile(x_hi), x_tile(x_lo))
            residual("aout")
            rstd("f1", [(R, D)])
            scaled_rows(h).then_inc(xn_ready, 1)
            rest_st("f1", x_tile(x_hi), x_tile(x_lo), lambda k: pcol("norm_ffn1", k))
            ffn(1)

            rstd("fin", [(R, D)])
            dve.wait_ge(rowg_landed[0], 16)
            for r in range(R):
                ins = dve.scalar_tensor_tensor(out=h[:, r, :], in0=h[:, r, :], scalar=root_col(r), in1=row_g,
                                               op0=ALU.mult, op1=ALU.mult)
            ins.then_inc(h_ready, 1)
            rstd("u", [(3, D)])
            dve.tensor_scalar(um[0:M, :], hm[0:M, :], stat[0:M, 34:35], None, ALU.mult)
            scaled_rows(h).then_inc(xn_ready, 1)
            rest_st("u", x_tile(x_hi, 0), x_tile(x_lo, 0), lambda k: pcol("pre_norm", k), a=0)
            after_key(("c0", 2))
            rstd("cqkv", [(3, 256), (3, 128)])
            for i in range(3):
                dve.tensor_scalar(cqn[:, i, 0:256], cn[:, i, 0:256], root_col(i), None, ALU.mult)
                ins = dve.tensor_scalar(cqn[:, i, 256:384], cn[:, i, 256:384], root_col(3 + i), None, ALU.mult)
            ins.then_inc(xn_ready, 1)
            dve.wait_ge(f_ps, 1)
            fr = [f_row[0:NH, i, :] for i in range(4)]
            dve.tensor_scalar(fr[0], bank[4][0:NH, 0:L], par[0:NH, PC["fox_b"]:PC["fox_b"] + 1], None, ALU.add)
            dve.drain()
            dve.scalar_tensor_tensor(out=fr[1], in0=fr[0], scalar=-1.0, in1=fr[0], op0=ALU.mult, op1=ALU.max).then_inc(f1_ok, 1)
            dve.memset(fr[3], 1.0)
            dve.wait_ge(kpe_ps, 1)
            dve.wait_ge(c2_landed, 32)
            dve.tensor_tensor(kp[0:64, :], bank[5][0:64, 0:L], k_tab[0:64, :], ALU.mult).then_inc(kp_ok, 1)
            dve.wait_ge(f2_ok, 1)
            dve.drain()
            dve.scalar_tensor_tensor(out=fr[1], in0=fr[0], scalar=0.0, in1=fr[2], op0=ALU.min, op1=ALU.subtract)
            dve.drain()
            dve.tensor_tensor_scan(fr[2], fr[3], fr[1], 0.0, ALU.mult, ALU.add)
            dve.drain()
            dve.tensor_scalar(fr[3], fr[2], -1.0, None, ALU.mult).then_inc(ncum_ok, 1)
            rest_st("cqkv", x_tile(cst_h, 0), x_tile(cst_l, 0), lambda k: pcol("q_norm", k), a=0)
            for p in range(8):
                if USE[("uk", p)] % 2 == 1:
                    b = acc_in(("uk", p))
                    dve.tensor_copy(kT[0:64, 2 * p, :], b[0:64, 0:L])
                    dve.tensor_copy(kT[0:64, 2 * p + 1, :], b[64:P, 0:L]).then_inc(acc_free[USE[("uk", p)] % 2], 1)
            rest_side(U_Q)
            rest_side(U_Q + 1)

            def query(n):
                b = acc_in(("uq", n))
                dve.wait_ge(sc_ps, A2 + n - 1)
                dve.tensor_tensor(q_h[:, n % 2, :], b[:, 0:S], q_tab, ALU.mult).then_inc(acc_free[USE[("uq", n)] % 2], 1)

            def gate(key):
                if key[0] not in ("zm", "zf", "ga", "gb"):
                    return
                i, c, r = ZN[key], key[1], key[2]
                cols = slice(c * CH, (c + 1) * CH)
                z, t = acc[USE[key] % 2], z_t[:, i % 2, :]
                dve.wait_ge(th_ok, i + 1)
                if key[0] in ("zm", "zf"):
                    out = (o_mla if key[0] == "zm" else o_fox)[:, r, cols]
                    dve.scalar_tensor_tensor(out=t, in0=t, scalar=1.0, in1=z[:, :], op0=ALU.add,
                                             op1=ALU.mult).then_inc(acc_free[USE[key] % 2], 1)
                    dve.drain()
                    dve.scalar_tensor_tensor(out=out, in0=t, scalar=0.5, in1=out, op0=ALU.mult, op1=ALU.mult).then_inc(z_ok, 1)
                    return
                dve.engine_nop().then_inc(acc_free[USE[key] % 2], 1)
                if key[0] == "ga":
                    out = y_mix[:, r, cols]
                    dve.scalar_tensor_tensor(out=out, in0=t, scalar=1.0, in1=out, op0=ALU.add, op1=ALU.mult).then_inc(z_ok, 1)
                else:
                    out = y_mix[:, r, cols]
                    dve.scalar_tensor_tensor(out=t, in0=t, scalar=1.0, in1=XN[:, r, cols], op0=ALU.add, op1=ALU.mult)
                    dve.drain()
                    dve.tensor_tensor(out, out, t, ALU.add).then_inc(z_ok, 1)

            query(0)
            for n in range(2 * NH):
                mla = n < NH
                keys = MLA_RIDERS[n] if mla else FOX_RIDERS[n - NH]
                s_ = sm[:, n % 2, :]
                if mla:
                    masks = lambda r: c_mask[:, P:L] if r == 0 else c_mask
                else:
                    p, e = (n - NH) // 2, n % 2
                    dve.wait_ge(mc_made, 2 * p + 2)
                    masks = lambda r: mc[:, p % 2, e, 0:M + P] if r == 0 else mc[:, p % 2, e, M + P:416]
                masked(A2 + n, lambda r: s_[:, 0:M + P] if r == 0 else s_[:, M + P:416],
                       lambda r: bank[4][:, 0:M + P] if r == 0 else bank[4][:, M + P:416], masks, 8 * (n % 2))
                if n + 1 < NH:
                    query(n + 1)
                dve.wait_ge(pt_ps, A2 + n + 1)
                dve.wait_ge(o_ps, A2 + n)
                dve.tensor_copy(pt[:, 0:384], bank[5][:, 0:384]).then_inc(pt_ok, 1)
                if len(keys) == 2:
                    after_key(keys[0])
                out = o_mla[:, :, n * HD:(n + 1) * HD] if mla else o_fox[:, :, (n - NH) * HD:(n - NH + 1) * HD]
                attended(A2 + n, out, 8 * (n % 2))
                if keys:
                    gate(keys[-1])
                    after_key(keys[-1])
                if n in (3, 7):
                    rest_side(U_Q + 2 + n // 4)
                if n == NH + 1:
                    rest_st("o_mla", lambda k: y_hi[:, k, :], lambda k: y_lo[:, k, :])
            for r in range(R):
                gate(("zf", 1, r))
                after_key(("zf", 1, r))
            rest_st("o_fox", lambda k: y_hi[:, k, :], lambda k: y_lo[:, k, :])
            for name in ("brf", "gb", "out"):
                if name == "out":
                    rest_st("mixed", lambda k: y_hi[:, k, :], lambda k: y_lo[:, k, :])
                for c in range(2):
                    for r in range(R):
                        gate((name, c, r))
                        after_key((name, c, r))
            rstd("post", [(R, D)])
            dve.wait_ge(rowg_landed[1], 16)
            for r in range(R):
                dve.scalar_tensor_tensor(out=XN[:, r, :], in0=o_fox[:, r, :], scalar=root_col(r), in1=row_g,
                                         op0=ALU.mult, op1=ALU.mult)
                dve.drain()
                dve.tensor_tensor(XN[:, r, :], XN[:, r, :], h[:, r, :], ALU.add).then_inc(z_ok, 1)


def k_tiles(w):
    return w.reshape(-1, P, w.shape[1]).transpose(1, 0, 2)


def main_chunks(i):
    def cols(w, idx=None):
        w = w if idx is None else w[:, idx]
        n = w.shape[1]
        for a in range(0, n, CH):
            part = w[:, a:a + CH]
            if part.shape[1] < CH:
                part = np.concatenate([part, np.zeros((D, CH - part.shape[1]), part.dtype)], 1)
            yield part

    parts = [*cols(i["mlstm_w_in"][0][:, 0:3072]), *cols(i["mlstm_w_out"][0])]
    ff = 2816

    def ffn(j):
        w = i["ffn_w_in"][j]
        for f in range(FB):
            yield np.concatenate([w[:, f * 256:(f + 1) * 256], w[:, ff + f * 256:ff + (f + 1) * 256]], 1)

    parts += ffn(0)
    aw = i["attn_w_in"][0]
    parts += cols(aw[:, 1024:1536])
    parts += cols(aw, np.concatenate([np.arange(hd * HD, (hd + 1) * HD) for hd in HEADS]))
    parts += cols(i["attn_w_out"][0][np.concatenate([np.arange(hd * HD, (hd + 1) * HD) for hd in HEADS])])
    parts += ffn(1)
    w = i["w_in_2"][0]
    o = np.cumsum([0, 256, 128, 32, 1024, 1024, 1024, 1024, 16, 1024, 1024, 1024])
    seg = [w[:, o[j]:o[j + 1]] for j in range(11)]
    cq, ckv, kpe, zm, fq, fk, fv, fl, zf, ga, gb = seg
    swap = np.concatenate([np.arange(16, 32), np.arange(16)])
    parts += cols(np.concatenate([cq, ckv, kpe, kpe[:, swap], fl], 1))
    for m in (fk, fq, fv, zm, i["w_br_mla_2"][0], ga, zf, i["w_br_fox_2"][0], gb, i["w_out_2"][0]):
        parts += cols(m)
    assert len(parts) == N_CHUNKS
    return np.stack([k_tiles(p).reshape(P, 2, 4 * CH).transpose(1, 0, 2) for p in parts])


HEADS = [8 * g + j + 4 * e for g in range(2) for j in range(4) for e in range(2)]


def side_units(i):
    g = i["mlstm_w_in"][0][:, 3072:]
    gates = np.zeros((D, P), g.dtype)
    for q in range(4):
        gates[:, 32 * q:32 * q + H0] = g[:, q * H0:(q + 1) * H0]
    units = [k_tiles(gates).reshape(P, D)]
    for j in range(2):
        units += list(i["ffn_w_out"][j].reshape(2 * FB, P, D))
    kv = i["w_ukv_2"][0].reshape(P, NH, 2, HD)
    units += [kv[:, :, 0].reshape(P, D), kv[:, :, 1].reshape(P, D)]
    q = i["w_uq_2"][0].reshape(256, NH, 96)
    pe = q[:, :, 64:]
    swap = np.concatenate([np.arange(16, 32), np.arange(16)])
    q = np.concatenate([q, pe[:, :, swap]], 2)
    for j in range(4):
        units.append(k_tiles(q[:, 4 * j:4 * j + 4].reshape(256, CH)).reshape(P, D))
    return np.stack(units)


def param_tile(i):
    t = np.zeros((P, N_PC), np.float32)

    def put(name, v):
        t[:v.shape[0], PC[name]:PC[name] + v.shape[1]] = v

    for j in range(2):
        put(f"norm_mix{j}", i["norm_mix_w"][j].reshape(KT, P).T)
        put(f"norm_ffn{j}", i["norm_ffn_w"][j].reshape(KT, P).T)
    put("mlstm_norm", i["mlstm_norm_w"][0].reshape(KT, P).T)
    put("pre_norm", i["pre_norm_g_2"][0].reshape(KT, P).T)
    put("q_norm", i["mla_q_norm_g_2"][0].reshape(2, P).T)
    put("kv_norm", i["mla_kv_norm_g_2"][0].reshape(1, P).T)
    put("b_gate", i["mlstm_b_gate"][0].reshape(4, H0).T)
    put("fox_b", i["fox_forget_b_2"][0].reshape(NH, 1))
    put("inv_freq", np.tile(np.float32(10000.0) ** (-np.arange(32, dtype=np.float32) / np.float32(32)), 4)[:, None])
    put("sign", np.where(np.arange(P) % 64 < 32, -1.0, 1.0)[:, None])
    put("sink", np.broadcast_to(i["attn_sink"][0][HEADS], (P, NH)))
    return t


def constants():
    a = np.arange(P)
    fwd = np.where(a[:, None] <= a[None, :], 0.0, NEG)
    sel = np.zeros((P, H0, P))
    for j in range(H0):
        sel[j, j] = 1.0
    l0 = np.concatenate([fwd, fwd.T, sel.reshape(P, -1)], 1)
    q = np.arange(S).reshape(R, P).T[:, :, None]
    l1 = np.where(np.abs(np.arange(S) - q) <= P, 0.0, NEG).reshape(P, -1)
    causal = np.where(np.arange(L)[None, :] - (M + P) <= a[:, None], 0.0, NEG)
    inv = np.float32(10000.0) ** (-np.arange(16, dtype=np.float32) / np.float32(16))
    ang = np.arange(L, dtype=np.float32)[None, :] * inv[:, None]
    cos, sin = np.cos(ang), np.sin(ang)
    k_tab = np.zeros((P, L))
    k_tab[0:64] = np.concatenate([cos, cos, -sin, sin])
    q_tab = np.concatenate([np.ones((64, L)), cos, cos, -sin, sin])[:, M:] * (1.0 / np.sqrt(96.0))
    k_sum = np.zeros((P, P))
    for j in range(64):
        k_sum[j, [64 + j % 32, 96 + j % 32]] = 1.0
    b2 = np.concatenate([causal, q_tab, k_tab, k_sum], 1)
    return [np.ascontiguousarray(t, np.float32) for t in (l0, l1, b2, np.eye(P))]


def kernel(**inputs):
    import concourse.bacc as bacc
    from concourse.bass_utils import run_bass_kernel_spmd

    i = {k: np.asarray(v) for k, v in inputs.items()}
    l0, l1, b2, eye = constants()
    rows = np.stack([np.broadcast_to(i["norm_final_w"], (P, D)), np.broadcast_to(i["post_norm_g_2"][0], (P, D))])
    arrays = {
        "w_main_dram": main_chunks(i), "w_side_dram": side_units(i), "params_dram": param_tile(i), "rows_dram": rows,
        "c_l0_dram": l0, "c_l1_dram": l1, "c_b2_dram": b2, "ident_dram": eye, "x_dram": i["x"][0],
        "meta_dram": i["meta_tokens_2"], "pos_dram": i["positions"].reshape(1, S),
    }
    arrays = {k: np.ascontiguousarray(v) for k, v in arrays.items()}
    nc = bacc.Bacc("TRN2", target_bir_lowering=False, num_devices=1)
    aps = [nc.dram_tensor(k, v.shape, mybir.dt.from_np(v.dtype), kind="ExternalInput").ap() for k, v in arrays.items()]
    negcum = nc.dram_tensor("negcum_dram", (NH, L), F32, kind="Internal").ap()
    out = nc.dram_tensor("out_dram", (S, D), F32, kind="ExternalOutput").ap()
    two_blocks(nc, *aps, negcum, out)
    r = run_bass_kernel_spmd(nc, [arrays], core_ids=[0])
    return r.results[0]["out_dram"].reshape(1, S, D)
```

```python
from contextlib import ExitStack

import numpy as np

import concourse.bass as bass
from concourse import mybir
from concourse.alu_op_type import AluOpType as ALU

F32 = mybir.dt.float32
F32R = mybir.dt.float32r
I32 = mybir.dt.int32
ACT = mybir.ActivationFunctionType
AX = mybir.AxisListType.X

P = 128
R = 2
S = P * R
M = 16
L = M + S
D = 1024
KT = D // P
CH = 512
EPS = 1e-6
NEG = -1e30

H0, DK, DV = 4, 128, 256
VW = DV + 2
HD = 64
NH = 16
FB = 11
TWO_PI = 2.0 * np.pi

C_MQ, C_MK, C_MV, C_MO, C_MOUT = 0, 1, 2, 4, 6
C_FFN = (8, 24)
C_AKV, C_AQ, C_AOUT = 19, 20, 22
C_C0, C_FK, C_FQ, C_FV, C_ZM, C_GA, C_BRM, C_ZF, C_GB, C_BRF, C_OUT = 35, 36, 38, 40, 42, 43, 46, 48, 49, 52, 54
N_CHUNKS = 56
STRIDE = {"zm": 2, "ga": 2, "zf": 2, "gb": 2}
U_GATES, U_DOWN, U_K, U_V, U_Q = 0, (1, 23), 45, 46, 47
N_UNITS = 51

PC = {}
_at = 0
for _name, _n in (("norm_mix0", 8), ("norm_mix1", 8), ("norm_ffn0", 8), ("norm_ffn1", 8), ("mlstm_norm", 8),
                  ("pre_norm", 8), ("norm_final", 8), ("q_norm", 2), ("kv_norm", 1), ("b_gate", 4), ("fox_b", 1), ("inv_freq", 1),
                  ("sign", 1), ("sink", 16)):
    PC[_name] = _at
    _at += _n
N_PC = _at

L0_CONST = 2 * P + H0 * P
L1_CONST = R * S
B2_CONST = L + S + L + P
KC0 = 464


FK_EARLY = 4


def token_major(name, cs=(0, 1), ts=(0, 1)):
    return [[(name, c, t)] for c in cs for t in ts]


RIDERS = [[("fk", b), ("fk", b + 1)] for b in range(FK_EARLY, 8, 2)]
RIDERS += [[("fq", 2 * n), ("fq", 2 * n + 1)] for n in range(4)]
RIDERS += token_major("fv", ts=(0, 1, 2)) + token_major("zm", (0,)) + token_major("ga", (0,))
RIDERS += token_major("zm", (1,)) + token_major("ga", (1,)) + token_major("brm") + token_major("zf", (0,)) + token_major("gb", (0,))
RIDERS += [[] for _ in range(2 * NH - len(RIDERS))]
MLA_TURNS = {RIDERS.index([("zm", j // 2, 1)]) + 1 + j % 2: (2 * j, 2 * j + 1) for j in range(4)}
TAIL_KEYS = [("zf", 1, r) for r in range(R)] + [("gb", 1, r) for r in range(R)] + [("brf", c, r) for c in range(2) for r in range(R)]


def acc_plan():
    keys = [("gates",)]
    keys += [("mq", b) for b in range(4)] + [("mk", b) for b in range(4)]
    keys += [(n, c, r) for n in ("mv", "mo", "mout") for c in range(2) for r in range(R)]
    keys += [("ffn0", f, r) for f in range(FB) for r in range(R)]
    keys += [("av", r) for r in range(R)] + [("ak", b) for b in range(2)]
    keys += [("aq", b) for b in range(8)]
    keys += [("aout", c, r) for c in range(2) for r in range(R)]
    keys += [("ffn1", f, r) for f in range(FB) for r in range(R)]
    keys += [("c0", t) for t in range(3)] + [("fk", b) for b in range(FK_EARLY)]
    keys += [("uk", p) for p in range(8)] + [("uv", t, c) for t in range(3) for c in range(2)]
    keys += [("uq", 0)]
    keys += [("uq", 1), ("uq", 2)]
    for n in range(2 * NH):
        if n + 3 < NH:
            keys.append(("uq", n + 3))
        keys += RIDERS[n]
    keys += TAIL_KEYS + [("out", c, r) for c in range(2) for r in range(R)]
    assert len(set(keys)) == len(keys)
    return {k: n for n, k in enumerate(keys)}


TAIL_TURNS = {0: (0, 1), 1: (2, 3), 3: (4, 5)}
USE = acc_plan()
AQ_RIDERS = (1, 4, 7, 10)
AOUT_SPLITS = (1, 4)

ST_TILES = {"x0": 8, "m_out": 8, "f0": 8, "x1": 8, "a_out": 8, "f1": 8, "u": 8, "cqkv": 3, "o_mla": 8, "o_fox": 8, "mixed": 8}
LAST = {("mq", 3): C_MQ, ("mk", 3): C_MK,
        ("fk", 3): C_FK, ("fk", 7): C_FK + 1, ("fq", 3): C_FQ, ("fq", 7): C_FQ + 1}
for _name, _c in (("mv", C_MV), ("mout", C_MOUT), ("aout", C_AOUT), ("zm", C_ZM), ("brm", C_BRM),
                  ("ga", C_GA), ("zf", C_ZF), ("brf", C_BRF), ("gb", C_GB), ("out", C_OUT)):
    for _j in range(2):
        LAST[(_name, _j, 1)] = _c + _j * STRIDE.get(_name, 1)
for _j in range(2):
    LAST[("fv", _j, 2)] = C_FV + _j
del LAST[("brf", 1, 1)]
ZN = {k: i for i, k in enumerate([("zm", c, r) for c in range(2) for r in range(R)] + [("zf", c, r) for c in range(2) for r in range(R)])}


def z_count(i):
    return i + 1 + (4 if i >= 4 else 0)


ST = {}
_at = 0
for _name, _n in ST_TILES.items():
    ST[_name] = _at
    _at += _n
Z_FINAL = 18
RMS = {n: i for i, n in enumerate(("x0", "hs", "f0", "x1", "meta", "f1", "fin", "u", "cqkv", "post"))}


def two_blocks(nc, w_main, w_side, params, rows, c_l0, c_l1, c_b2, ident_d, x_d, meta_d, pos_d, out_d):
    ctx = ExitStack()
    with ctx:
        def sb(name, shape, dt=F32):
            return ctx.enter_context(nc.sbuf_tensor(name, shape, dt))

        def sem(name):
            return ctx.enter_context(nc.semaphore(name))

        bank = [ctx.enter_context(nc.psum_tensor(f"bank{i}", [P, 512], F32)) for i in range(8)]
        acc, tp = bank[0:2], bank[2:4]
        sc_bank, o_bank = (bank[4], bank[3]), (bank[7], bank[2])

        def tp_bank(n):
            return bank[2] if ST["o_mla"] <= n < ST["o_fox"] else tp[n % 2]

        w_raw = sb("w_raw", [P, 2, 4, CH])
        w_hi = sb("w_hi", [P, 2, KT, CH], F32R)
        w_lo = sb("w_lo", [P, 2, KT, CH], F32R)
        s_raw = sb("s_raw", [P, 2, D])
        s_hi = sb("s_hi", [P, 2, D], F32R)
        s_lo = sb("s_lo", [P, 2, D], F32R)
        h = sb("h", [P, R, D])
        x_hi = sb("x_hi", [P, KT, L], F32R)
        x_lo = sb("x_lo", [P, KT, L], F32R)
        g_hi = sb("g_hi", [P, 3 * L], F32R)
        g_lo = sb("g_lo", [P, 3 * L], F32R)
        ident = sb("ident", [P, P])
        par = sb("par", [P, N_PC])
        stat = sb("stat", [P, 32])
        small = sb("small", [P, 42])
        ffn_nat = sb("ffn_nat", [P, 2, R, 256])
        zero_r = g_hi[:, 512:512 + P]
        arena = sb("arena", [P, 17232])

        def ar(off, *shape):
            n = int(np.prod(shape))
            v = arena[:, off:off + n]
            names = "abcd"[:len(shape)]
            if len(shape) == 1:
                return v
            return v.rearrange(f"p ({' '.join(names)}) -> p {' '.join(names)}", **dict(zip(names[1:], shape[1:])))

        def pcol(name, k=0, n=1):
            return par[:, PC[name] + k:PC[name] + k + n]

        y_hi = s_hi[:, :, :].rearrange("p a b -> p (a b)").rearrange("p (k t) -> p k t", k=KT)
        y_lo = s_lo[:, :, :].rearrange("p a b -> p (a b)").rearrange("p (k t) -> p k t", k=KT)
        ffh = g_hi[:, 0:512].rearrange("p (k t) -> p k t", k=2)
        ffl = g_lo[:, 0:512].rearrange("p (k t) -> p k t", k=2)
        cst_h = g_hi[:, :].rearrange("p (k t) -> p k t", k=3)
        cst_l = g_lo[:, :].rearrange("p (k t) -> p k t", k=3)

        XN = ar(4224, R, D)
        mqT, mkT, m_kn = ar(0, H0, S), ar(1024, H0, S), ar(2048, R, H0, DK)
        v_aug, o_gate = ar(6272, R, H0, VW), ar(8336, R, D)
        l0c = ar(10384, L0_CONST)
        m_mask = l0c[:, 0:2 * P].rearrange("p (a b) -> p a b", a=2)
        m_sel = l0c[:, 2 * P:].rearrange("p (a b) -> p a b", a=H0)
        g_rows = ar(11152, 4, S)
        row_a, row_b, row_c, row_m, row_n = (ar(12176 + 512 * i, 2, S) for i in range(5))
        row_i, row_e, row_w = ar(14736, 2, P), ar(14992, 2, S), ar(15504, 2, P)
        row_1 = ar(3072, 2, S)
        mcol = ar(15760, 40)
        m_t = ar(15800, 2, R, P)
        m_sd = ar(16312, 2, R, P)
        m_qi = ar(16824, 2, P)
        m_kw = ar(3328, 2, P)
        m_ei, m_sq = ar(3072, 2, P), ar(11152, R * H0, DV)
        m_c = ar(3584, 2, VW)
        aqT, akT, a_v, a_mask = ar(0, 8, S), ar(2048, 2, S), ar(2560, R, S), ar(14208, R, S)
        cosT, sinT, a_o = ar(14720, S), ar(14976, S), ar(6272, R, D)
        a_sw, a_tmp, ang = ar(8320, 2, S), ar(8832, 2, S), ar(9344, 3, S)
        pos_i = ar(11648, S).bitcast(I32)
        a_sm, a_pt = ar(10112, 2, R, S), ar(11136, 4, P)
        fkT, fqT, f_v, f_vm = ar(0, 8, L), ar(2176, 8, S), s_raw[:, :, :], ar(6272, D)
        kT, v_m, v_mm = ar(7296, NH, L), ar(11648, R, D), ar(13696, D)
        o_fox, y_mix = ar(7296, R, D), ar(9344, R, D)
        q_h, sm, pt = ar(14720, 2, S), ar(15232, 2, 416), ar(16064, 640)
        b2c, b2k = ar(16704, L + S), ar(15232, L + P)
        c_mask, q_tab, k_tab, k_sum = b2c[:, 0:L], b2c[:, L:], b2k[:, 0:L], b2k[:, L:]
        cn, cqn = ar(7296, 3, KC0), ar(7296 + 3 * KC0, 3, 384)
        hm, um, m_tmp = ar(11904, D), ar(12928, D), ar(3328, KT, M)
        sq = ar(11648, R, D)
        gain_u, scale_u, half_u = pcol("norm_mix0", 0, KT), small[:, 32:34], small[:, 34:36]
        kp, f_row = ar(2560, L), ar(2832, 4, L)
        o_mla = XN
        ncum = v_mm[64:64 + NH, 0:L]
        r_row = ffn_nat[:, :, :, :].rearrange("p a r n -> p (a r n)")[:, 0:L]
        z_t = ffn_nat[:, :, :, :].rearrange("p a r n -> p a (r n)")
        row_g = ar(6272, D)

        w_landed = [sem("w_landed0"), sem("w_landed1")]
        w_hi_ok, w_lo_ok = sem("w_hi_ok"), sem("w_lo_ok")
        s_landed = [sem("s_landed0"), sem("s_landed1")]
        s_hi_ok, s_lo_ok, s_used = sem("s_hi_ok"), sem("s_lo_ok"), sem("s_used")
        acc_ready = [sem("acc_ready0"), sem("acc_ready1")]
        acc_free = [sem("acc_free0"), sem("acc_free1")]
        tp_ready, st_hi_ok, st_lo_ok = sem("tp_ready"), sem("st_hi_ok"), sem("st_lo_ok")
        xn_ready = sem("xn_ready")
        h_ready, h_half = sem("h_ready"), sem("h_half")
        av_ok = sem("av_ok")
        um_ok, um_ps, um_g, um_hi, um_lo, ru_ok, ru_ps, rrow_ok = (
            sem(n) for n in ("um_ok", "um_ps", "um_g", "um_hi", "um_lo", "ru_ok", "ru_ps", "rrow_ok"))
        hg_ok = sem("hg_ok")
        rs_ok, rb_ps = sem("rs_ok"), sem("rb_ps")
        ss_ok = sem("ss_ok")
        in_landed, meta_landed, c0_landed, c1_landed, c2_landed = (
            sem("in_landed"), sem("meta_landed"), sem("c0_landed"), sem("c1_landed"), sem("c2_landed"))
        pos_landed, rowg_landed = sem("pos_landed"), [sem("rowg_landed0"), sem("rowg_landed1")]
        silu_ok, g_tp, g_hi_ok, g_lo_ok = sem("silu_ok"), sem("g_tp"), sem("g_hi_ok"), sem("g_lo_ok")
        zero_ok = sem("zero_ok")
        out_landed = sem("out_landed")

        def landed(i):
            return 16 * (i + 1)

        block = ctx.enter_context(nc.Block())

        gr_ok, fa_ok, fe_ok, rows_ok, mc_ps, mc_ok = (sem(n) for n in ("gr_ok", "fa_ok", "fe_ok", "rows_ok", "mc_ps", "mc_ok"))
        kn_ps, kn_ok, bc_ps, t_ok, in_ps, ei_ok = (sem(n) for n in ("kn_ps", "kn_ok", "bc_ps", "t_ok", "in_ps", "ei_ok"))
        s0_ps, wt_ok, sd_ok, kw_ok, c_ps, c_ok, qi_ok = (sem(n) for n in ("s0_ps", "wt_ok", "sd_ok", "kw_ok", "c_ps", "c_ok", "qi_ok"))
        n_ps, rd_ok, hf_ok, n_done, hs_ok, va_ok = (sem(n) for n in ("n_ps", "rd_ok", "hf_ok", "n_done", "hs_ok", "va_ok"))
        og1_ok = sem("og1_ok")
        n_bank = (bank[6], bank[7], bank[4], bank[6])
        ang_ok, tab_ok, sw_ok, rot_ok = (sem(n) for n in ("ang_ok", "tab_ok", "sw_ok", "rot_ok"))
        sc_ps, nm_ok, p_ok, pt_ps, pt_ok, ptm_ok, o_ps, o_ok = (
            sem(n) for n in ("sc_ps", "nm_ok", "p_ok", "pt_ps", "pt_ok", "ptm_ok", "o_ps", "o_ok"))
        k_ok = sem("k_ok")
        f_ps, f1_ok, f2_ok, ncum_ok, kpe_ps, kp_ok, kr_ps = (
            sem(n) for n in ("f_ps", "f1_ok", "f2_ok", "ncum_ok", "kpe_ps", "kp_ok", "kr_ps"))
        th_ok, z_ok = sem("th_ok"), sem("z_ok")
        A1, A2, A3 = 0, NH, 2 * NH

        @block.sync
        def _(sp):
            def main_half(c, g):
                dst = w_raw[:, g, :, :].rearrange("p k n -> p (k n)")
                sp.dma_start(dst, w_main[c, g]).then_inc(w_landed[g], 16)

            def main(c):
                for g in range(2):
                    sp.wait_ge(w_lo_ok, 2 * c - 1 + g)
                    main_half(c, g)

            def side(u, slot):
                sp.wait_ge(s_lo_ok, u - 1)
                sp.dma_start(s_raw[:, slot, :], w_side[u]).then_inc(s_landed[slot], 16)

            sp.dma_start(h[:, :, :], x_d.rearrange("(r p) d -> p r d", p=P)).then_inc(in_landed, 16)
            sp.dma_start(par[:, :], params).then_inc(in_landed, 16)
            sp.dma_start(ident[:, :], ident_d).then_inc(in_landed, 16)
            for g in range(2):
                main_half(0, g)
            for u in range(2):
                sp.dma_start(s_raw[:, u, :], w_side[u]).then_inc(s_landed[u], 16)
            main(1)
            main(2)
            side(2, 0)
            with sp.Fori(3, C_FFN[0] + 2) as c:
                main(c)

            def ffn(layer):
                c0, u0 = C_FFN[layer] + 2, U_DOWN[layer] + 2
                with sp.Fori(0, FB - 1) as i:
                    main(c0 + i)
                    for s in range(2):
                        side(u0 + 2 * i + s, (u0 + s) % 2)

            ffn(0)
            main(C_AKV + 1)
            for u in (U_DOWN[1], U_DOWN[1] + 1):
                side(u, u % 2)
            with sp.Fori(C_AKV + 2, C_FFN[1] + 2) as c:
                main(c)
            ffn(1)
            for c, units in ((C_FK, (U_K, U_V)), (C_FK + 1, (U_Q, U_Q + 1)), (C_FQ, (U_Q + 2,)), (C_FQ + 1, (U_Q + 3,))):
                main(c)
                for u in units:
                    side(u, u % 2)
            with sp.Fori(C_FV, N_CHUNKS) as c:
                main(c)
            sp.wait_ge(z_ok, Z_FINAL)
            sp.dma_start(out_d.rearrange("(r p) d -> p r d", p=P), XN).then_inc(out_landed, 16)
            sp.wait_ge(out_landed, 16)

        @block.gpsimd
        def _(pool):
            pool.memset(stat[:, :], 1.0)
            pool.memset(zero_r.bitcast(F32), 0.0).then_inc(zero_ok, 1)
            pool.memset(row_1[0:H0, :, :], 1.0)
            pool.memset(v_aug[:, :, :, DV:DV + 1], 1.0)
            pool.memset(v_aug[:, :, :, DV + 1:VW], 0.0).then_inc(va_ok, 1)
            pool.dma_start(l0c, c_l0).then_inc(c0_landed, 16)
            pool.wait_ge(mc_ok, 1)
            pool.wait_ge(kn_ok, 2)
            for hh in range(H0):
                for d in range(2):
                    if hh:
                        pool.wait_ge(c_ps, 2 * hh + d - 1)
                    a = 32 + d * H0 + hh
                    pool.tensor_scalar(m_kw[:, d, :], m_kn[:, d, hh, :], mcol[:, a:a + 1], None, ALU.mult).then_inc(kw_ok, 1)
                if hh:
                    pool.wait_ge(n_ps, 4 * hh)
                pool.wait_ge(ei_ok, hh + 1)
                for d in range(2):
                    ins = pool.tensor_tensor(m_qi[:, d, :], mqT[:, hh, (1 - d) * P:(2 - d) * P], m_ei[:, d, :], ALU.mult)
                ins.then_inc(qi_ok, 1)
                n = USE[("mo", hh // 2, hh % 2)]
                pool.wait_ge(acc_free[n % 2], n // 2 + 1)
                og = o_gate[:, hh % 2, hh // 2 * CH:(hh // 2 + 1) * CH]
                pool.tensor_scalar(og, og, 1.0, None, ALU.add).then_inc(og1_ok, 1)
            pool.wait_ge(h_ready, 1)
            pool.dma_start(hm[0:M, :], meta_d).then_inc(meta_landed, 16)
            pool.dma_start(a_mask, c_l1.rearrange("p (r s) -> p r s", r=R)).then_inc(c1_landed, 16)
            pool.dma_start(pos_i[:, :], pos_d.to_broadcast([P, S])).then_inc(pos_landed, 16)
            pool.wait_ge(h_ready, 3)
            pool.dma_start(b2c, c_b2[:, 0:L + S]).then_inc(c2_landed, 16)
            pool.dma_start(b2k, c_b2[:, L + S:]).then_inc(c2_landed, 16)
            pool.dma_start(row_g, rows[0]).then_inc(rowg_landed[0], 16)
            pool.wait_ge(o_ok, 3 * NH)
            pool.dma_start(row_g, rows[1]).then_inc(rowg_landed[1], 16)

        @block.tensor
        def _(pe):
            def mm3(out, ah, al, bh, bl, first, last):
                pe.matmul(out, ah, bh, start=first, stop=False)
                pe.matmul(out, ah, bl, start=False, stop=False)
                return pe.matmul(out, al, bh, start=False, stop=last)

            def acc_wait(key):
                n = USE[key]
                if n >= 2:
                    pe.wait_ge(acc_free[n % 2], n // 2)
                return acc[n % 2]

            def done(ins, key):
                ins.then_inc(acc_ready[USE[key] % 2], 1)

            def tok_cols(t):
                return slice(0, P) if t == 2 else slice(M + t * P, M + (t + 1) * P)

            def part_a(c, key, t, k0, k1, sh=x_hi, sl=x_lo, n0=0, n1=CH, moved=0):
                bank_ = acc_wait(key) if k0 == 0 else acc[USE[key] % 2]
                cols = tok_cols(t)
                if moved:
                    cols = slice(cols.start - moved, cols.stop - moved)
                for k in range(k0, k1):
                    if k % 4 == 0:
                        pe.wait_ge(w_lo_ok, 2 * c + k // 4 + 1)
                    ins = mm3(bank_[:, 0:n1 - n0], sh[:, k, cols], sl[:, k, cols],
                              w_hi[:, c % 2, k, n0:n1], w_lo[:, c % 2, k, n0:n1], k == 0, k == KT - 1)
                if k1 == KT:
                    done(ins, key)

            def part_b(c, key, b, t0, k0=0, k1=KT):
                bank_ = acc_wait(key) if k0 == 0 else acc[USE[key] % 2]
                for k in range(k0, k1):
                    if k % 4 == 0:
                        pe.wait_ge(w_lo_ok, 2 * c + k // 4 + 1)
                    ins = mm3(bank_[:, 0:L - t0], w_hi[:, c % 2, k, b * P:(b + 1) * P], w_lo[:, c % 2, k, b * P:(b + 1) * P],
                              x_hi[:, k, t0:L], x_lo[:, k, t0:L], k == 0, k == KT - 1)
                if k1 == KT:
                    done(ins, key)

            def evacuated(*keys):
                for key in keys:
                    pe.wait_ge(acc_free[USE[key] % 2], USE[key] // 2 + 1)

            def to_stationary(name, src, sem_, value, meta=None, ks=None):
                if sem_ is not None:
                    pe.wait_ge(sem_, value)
                for k in range(ST_TILES[name]) if ks is None else ks:
                    n = ST[name] + k
                    if n >= 2:
                        pe.wait_ge(st_lo_ok, n if tp_bank(n) is tp_bank(n - 1) else n - 1)
                    b = tp_bank(n)
                    if meta is not None:
                        pe.transpose(b[:, 0:M], meta(k), ident[0:M, 0:M])
                    for r in range(R):
                        ins = pe.transpose(b[:, M + r * P:M + (r + 1) * P], src(r, k), ident[:, :])
                    ins.then_inc(tp_ready, 1)

            def streamed(name, src, ready, products, meta=None):
                def turn_(k):
                    if k in ready:
                        ready[k]()
                    to_stationary(name, src, None, 0, meta, ks=(k,))

                turn_(0)
                turn_(1)
                for k in range(ST_TILES[name]):
                    st_wait(name, k)
                    if k + 2 < ST_TILES[name]:
                        turn_(k + 2)
                    for product in products:
                        product(k)

            def st_wait(name, k=None):
                pe.wait_ge(st_lo_ok, ST[name] + (ST_TILES[name] if k is None else k + 1))

            def xn(r, k):
                return XN[:, r, k * P:(k + 1) * P]

            pe.wait_ge(in_landed, 48)
            def gates_product(k):
                b = acc[USE[("gates",)] % 2]
                if k == 0:
                    pe.wait_ge(s_lo_ok, U_GATES + 1)
                ins = mm3(b[:, 0:S], s_hi[:, 0, k * P:(k + 1) * P], s_lo[:, 0, k * P:(k + 1) * P],
                          x_hi[:, k, M:L], x_lo[:, k, M:L], k == 0, k == KT - 1)
                if k == KT - 1:
                    done(ins, ("gates",))

            def rows_ready(value):
                return {0: lambda: pe.wait_ge(xn_ready, value)}

            def tiles_a(c, key, r, n0=0, n1=CH):
                return lambda k: part_a(c, key, r, k, k + 1, n0=n0, n1=n1)

            def tiles_b(c, key, b):
                return lambda k: part_b(c, key, b, M, k, k + 1)

            streamed("x0", xn, rows_ready(1), [gates_product, tiles_b(C_MQ, ("mq", 0), 0)])
            for b in range(1, 4):
                part_b(C_MQ, ("mq", b), b, M)
            for b in range(4):
                part_b(C_MK, ("mk", b), b, M)
            for c in range(2):
                for r in range(R):
                    part_a(C_MV + c, ("mv", c, r), r, 0, KT)
                    if c == 0:
                        if r == 0:
                            evacuated(("mk", 2), ("mk", 3))
                        else:
                            pe.wait_ge(kn_ok, 1)
                        for hh in range(H0):
                            ins = pe.transpose(bank[4][:, hh * P:(hh + 1) * P], mkT[:, hh, r * P:(r + 1) * P], ident[:, :])
                        ins.then_inc(kn_ps, 1)

            pe.wait_ge(rows_ok, 1)
            for d in range(2):
                for r in range(R):
                    a = (d * R + r) * H0
                    pe.transpose(bank[5][:, a:a + H0], row_c[0:H0, d, r * P:(r + 1) * P], ident[0:H0, 0:H0])
                    pe.transpose(bank[5][:, 16 + a:16 + a + H0], row_e[0:H0, d, r * P:(r + 1) * P], ident[0:H0, 0:H0])
            for d in range(2):
                ins = pe.transpose(bank[5][:, 32 + d * H0:32 + (d + 1) * H0], row_w[0:H0, d, :], ident[0:H0, 0:H0])
            ins.then_inc(mc_ps, 1)
            pe.wait_ge(c0_landed, 16)
            for hh in range(H0):
                if hh:
                    pe.wait_ge(t_ok, hh)
                    pe.wait_ge(ei_ok, hh)
                pe.matmul(bank[3][:, :], m_sel[0:H0, hh, :], row_n[0:H0, :, :].rearrange("p a b -> p (a b)"),
                          start=True, stop=True).then_inc(bc_ps, 1)
                pe.matmul(bank[2][:, 0:2 * P], m_sel[0:H0, hh, :], row_i[0:H0, :, :].rearrange("p a b -> p (a b)"),
                          start=True, stop=True).then_inc(in_ps, 1)
                if hh:
                    pe.wait_ge(hf_ok, 2 * hh)
                else:
                    pe.wait_ge(kn_ok, 2)
                for r in range(R):
                    ins = pe.matmul(bank[4][:, r * P:(r + 1) * P], mkT[:, hh, r * P:(r + 1) * P],
                                    mqT[:, hh, r * P:(r + 1) * P], start=True, stop=True)
                ins.then_inc(s0_ps, 1)
                part_a(C_MO + hh // 2, ("mo", hh // 2, hh % 2), hh % 2, 0, KT)
                for d in range(2):
                    n = 2 * hh + d
                    pe.wait_ge(kw_ok, n + 1)
                    if n:
                        pe.wait_ge(c_ok, n)
                    else:
                        pe.wait_ge(va_ok, 1)
                        evacuated(("mv", 1, 0), ("mv", 1, 1))
                    pe.matmul(bank[5][:, 0:VW], m_kw[:, d, :], v_aug[:, d, hh, :], start=True, stop=True).then_inc(c_ps, 1)
                pe.wait_ge(sd_ok, hh + 1)
                for r in range(R):
                    for d in range(2):
                        if (r, d) == (1, 1):
                            pe.wait_ge(hf_ok, 2 * hh + 1)
                        elif r == 0 and hh:
                            pe.wait_ge(n_done, 2 * hh - d)
                        b = n_bank[2 * r + d]
                        second = (r == 1 - d)
                        ins = pe.matmul(b[:, 0:VW], m_sd[:, d, r, :], v_aug[:, r, hh, :], start=True, stop=not second)
                        if second:
                            pe.wait_ge(c_ok, 2 * hh + d + 1)
                            pe.wait_ge(qi_ok, hh + 1)
                            ins = pe.matmul(b[:, 0:VW], m_qi[:, d, :], m_c[:, d, :], start=False, stop=True)
                        ins.then_inc(n_ps, 1)

            def residual_rows(r, k):
                return h[:, r, k * P:(k + 1) * P]

            def mixer_out(name, c, st, src, value, ffn_st, sem_):
                streamed(st, src, {0: lambda: pe.wait_ge(sem_, value)}, [tiles_a(c, (name, 0, r), r) for r in range(R)])
                part_a(c + 1, (name, 1, 0), 0, 0, KT)
                evacuated((name, 0, 1))
                to_stationary(ffn_st, residual_rows, None, 0, ks=range(2))
                part_a(c + 1, (name, 1, 1), 1, 0, KT)

            mixer_out("mout", C_MOUT, "m_out", xn, 2, "f0", xn_ready)

            def ffn(layer, mixer):
                name, c0, u0 = f"ffn{layer}", C_FFN[layer], U_DOWN[layer]
                n0 = USE[(name, 0, 0)]

                def up(f, j, transposes):
                    slot = (c0 + j) % 2
                    for r in range(R):
                        b_ = (n0 + r) % 2
                        pe.wait_ge(acc_free[b_], (n0 + r) // 2 + f)
                        for k in range(KT):
                            if r == 0 and k % 4 == 0:
                                pe.wait_ge(w_lo_ok, 2 * (c0 + f) + k // 4 + 1)
                            if transposes and r == 0 and k == 4:
                                turn(f - 1)
                            cols = tok_cols(r)
                            ins = mm3(acc[b_][:, :], x_hi[:, k, cols], x_lo[:, k, cols],
                                      w_hi[:, slot, k, :], w_lo[:, slot, k, :], k == 0, k == KT - 1)
                        ins.then_inc(acc_ready[b_], 1)

                def turn(f):
                    for r in range(R):
                        pe.wait_ge(acc_free[(n0 + r) % 2], (n0 + r) // 2 + f + 1)
                    for ks in range(2):
                        for r in range(R):
                            ins = pe.transpose(bank[2][:, ks * S + r * P:ks * S + (r + 1) * P],
                                               ffn_nat[:, 1, r, ks * P:(ks + 1) * P], ident[:, :])
                    ins.then_inc(g_tp, 1)

                def down(f, first=False, final=False):
                    pe.wait_ge(g_lo_ok, FB * layer + f + 1)
                    if final:
                        pe.wait_ge(s_lo_ok, u0 + 2 * f + 2)
                        for cc in range(2):
                            for ks in range(2):
                                slot = (u0 + ks) % 2
                                for r in range(R):
                                    ins = mm3(bank[4 + 2 * r + cc][:, :], ffh[:, ks, r * P:(r + 1) * P],
                                              ffl[:, ks, r * P:(r + 1) * P], s_hi[:, slot, cc * CH:(cc + 1) * CH],
                                              s_lo[:, slot, cc * CH:(cc + 1) * CH], False, ks == 1)
                            ins.then_inc(s_used, 1)
                        return
                    for ks in range(2):
                        slot = (u0 + ks) % 2
                        pe.wait_ge(s_lo_ok, u0 + 2 * f + ks + 1)
                        for r in range(R):
                            for cc in range(2):
                                ins = mm3(bank[4 + 2 * r + cc][:, :], ffh[:, ks, r * P:(r + 1) * P],
                                          ffl[:, ks, r * P:(r + 1) * P], s_hi[:, slot, cc * CH:(cc + 1) * CH],
                                          s_lo[:, slot, cc * CH:(cc + 1) * CH], False, False)
                        ins.then_inc(s_used, 1)

                pe.wait_ge(zero_ok, 1)
                for i in range(4):
                    for q in range(4):
                        pe.matmul(bank[4 + i][:, q * P:(q + 1) * P], zero_r, zero_r,
                                  start=(q == 0), stop=False)
                for k in range(KT):
                    if k == 0:
                        for r in range(R):
                            pe.wait_ge(acc_free[(n0 + r) % 2], (n0 + r) // 2)
                    st_wait(f"f{layer}", k)
                    if k + 2 < KT:
                        if k == 2:
                            evacuated((mixer, 1, 0), (mixer, 1, 1))
                        to_stationary(f"f{layer}", residual_rows, None, 0, ks=(k + 2,))
                    if k % 4 == 0:
                        pe.wait_ge(w_lo_ok, 2 * c0 + k // 4 + 1)
                    for r in range(R):
                        cols = tok_cols(r)
                        ins = mm3(acc[(n0 + r) % 2][:, :], x_hi[:, k, cols], x_lo[:, k, cols],
                                  w_hi[:, c0 % 2, k, :], w_lo[:, c0 % 2, k, :], k == 0, k == KT - 1)
                        if k == KT - 1:
                            ins.then_inc(acc_ready[(n0 + r) % 2], 1)
                with pe.Fori(0, (FB - 1) // 2) as i:
                    up(2 * i + 1, 1, True)
                    down(2 * i)
                    up(2 * i + 2, 2, True)
                    down(2 * i + 1)
                turn(FB - 1)
                down(FB - 1, final=True)

            ffn(0, "mout")

            streamed("x1", residual_rows, {0: lambda: pe.wait_ge(h_half, 1), 4: lambda: pe.wait_ge(h_ready, 2)},
                     [tiles_a(C_AKV, ("av", r), r, 256, 512) for r in range(R)])
            part_b(C_AKV, ("ak", 0), 0, M)
            pe.wait_ge(rs_ok, 2)
            for r in range(R):
                ins = pe.transpose(bank[6][:, r * P:(r + 1) * P], stat[:, 24 + r:25 + r].to_broadcast([P, P]), ident[:, :])
            ins.then_inc(rb_ps, 1)
            part_b(C_AKV, ("ak", 1), 1, M)
            for b in range(4):
                part_b(C_AQ, ("aq", b), b, M)

            def a_scores(n):
                a = 64 * (n % 2)
                pe.wait_ge(rot_ok, 3 + n // 2)
                if n >= 2:
                    pe.wait_ge(nm_ok, n - 1)
                for r in range(R):
                    ins = pe.matmul(sc_bank[n % 2][:, r * S:(r + 1) * S], aqT[a:a + HD, n // 2, r * P:(r + 1) * P],
                                    akT[a:a + HD, n // 8, :], start=True, stop=True)
                ins.then_inc(sc_ps, 1)

            def a_turn(n):
                pe.wait_ge(p_ok, n + 1)
                if n:
                    pe.wait_ge(pt_ok, n)
                for r in range(R):
                    for kt in range(2):
                        ins = pe.transpose(bank[5][:, (kt * 2 + r) * P:(kt * 2 + r + 1) * P],
                                           a_sm[:, n % 2, r, kt * P:(kt + 1) * P], ident[:, :])
                ins.then_inc(pt_ps, 1)

            def a_values(n):
                pe.wait_ge(pt_ok, n + 1)
                if n >= 2:
                    pe.wait_ge(o_ok, n - 1)
                else:
                    pe.wait_ge(av_ok, 1)
                g = 2 * (n // 8) + n % 2
                for r in range(R):
                    for kt in range(2):
                        ins = pe.matmul(o_bank[n % 2][:, r * HD:(r + 1) * HD], a_pt[:, kt * 2 + r, :],
                                        a_v[:, kt, g * HD:(g + 1) * HD], start=(kt == 0), stop=(kt == 1))
                ins.then_inc(o_ps, 1)

            a_scores(0)
            a_scores(1)
            for n in range(NH + 1):
                if n + 2 < NH:
                    a_scores(n + 2)
                if n == 2:
                    pe.wait_ge(um_ok, 1)
                    for k in range(KT):
                        ins = pe.transpose(bank[6][:, k * M:(k + 1) * M], um[0:M, k * P:(k + 1) * P], ident[0:M, 0:M])
                    ins.then_inc(um_ps, 1)
                if n in AQ_RIDERS:
                    j = AQ_RIDERS.index(n)
                    part_b(C_AQ + 1, ("aq", 4 + j), j, M)
                if n < NH:
                    a_turn(n)
                if n:
                    a_values(n - 1)

            mixer_out("aout", C_AOUT, "a_out", lambda r, k: a_o[:, r, k * P:(k + 1) * P], NH, "f1", o_ok)
            ffn(1, "aout")

            def tile_c0(i, t):
                return lambda k: part_a(C_C0, ("c0", i), t, k, k + 1, n1=KC0)

            pe.wait_ge(um_lo, 1)
            streamed("u", residual_rows, {0: lambda: pe.wait_ge(h_half, 2), 4: lambda: pe.wait_ge(h_ready, 4)},
                     [tile_c0(0, 2), tile_c0(1, 0)])
            part_a(C_C0, ("c0", 2), 1, 0, KT, n1=KC0)
            pe.wait_ge(ru_ok, 1)
            for r in range(R):
                ins = pe.transpose(bank[6][:, r * P:(r + 1) * P], scale_u[:, r:r + 1].to_broadcast([P, P]), ident[:, :])
            ins.then_inc(ru_ps, 1)
            for b in range(2):
                part_b(C_FK, ("fk", b), b, 0)
            evacuated(("c0", 1), ("c0", 2))
            pe.wait_ge(c2_landed, 32)
            for t, a, n in ((0, 0, M), (1, M, P), (2, M + P, P)):
                ins = pe.transpose(bank[4][0:NH, a:a + n], cn[0:n, t, 448:464], ident[0:n, 0:n])
            ins.then_inc(f_ps, 1)
            for t, a, n in ((0, 0, M), (1, M, P), (2, M + P, P)):
                ins = pe.transpose(bank[5][0:64, a:a + n], cn[0:n, t, 384:448], ident[0:n, 0:n])
            ins.then_inc(kpe_ps, 1)
            for b in range(2, FK_EARLY):
                part_b(C_FK, ("fk", b), b, 0)
            to_stationary("cqkv", lambda r, k: cqn[:, 1 + r, k * P:(k + 1) * P], xn_ready, 3,
                          meta=lambda k: cqn[0:M, 0, k * P:(k + 1) * P])
            pe.wait_ge(kp_ok, 1)
            pe.matmul(bank[6][:, 0:L], k_sum[0:64, :], kp[0:64, :], start=True, stop=True).then_inc(kr_ps, 1)
            st_wait("cqkv")
            for p in range(8):
                b = acc_wait(("uk", p))
                pe.wait_ge(s_lo_ok, U_K + 1)
                sl = U_K % 2
                done(mm3(b[:, 0:L], s_hi[:, sl, p * P:(p + 1) * P], s_lo[:, sl, p * P:(p + 1) * P],
                         cst_h[:, 2, :], cst_l[:, 2, :], True, True), ("uk", p))
            for i, t in enumerate((2, 0, 1)):
                for cc in range(2):
                    b = acc_wait(("uv", i, cc))
                    pe.wait_ge(s_lo_ok, U_V + 1)
                    sl = U_V % 2
                    done(mm3(b[:, :], cst_h[:, 2, tok_cols(t)], cst_l[:, 2, tok_cols(t)],
                             s_hi[:, sl, cc * CH:(cc + 1) * CH], s_lo[:, sl, cc * CH:(cc + 1) * CH], True, True),
                         ("uv", i, cc))

            def mla_query(n):
                b = acc_wait(("uq", n))
                u = U_Q + n // 4
                pe.wait_ge(s_lo_ok, u + 1)
                for ks in range(2):
                    a = ks * CH + (n % 4) * P
                    ins = mm3(b[:, 0:S], s_hi[:, u % 2, a:a + P], s_lo[:, u % 2, a:a + P],
                              cst_h[:, ks, M:L], cst_l[:, ks, M:L], ks == 0, ks == 1)
                done(ins, ("uq", n))

            def scores(n, q, k, gates=False):
                pe.wait_ge(nm_ok, n - 1)
                b = sc_bank[n % 2]
                for r, (a, e) in enumerate(((0, M + P), (M + P, 416))):
                    ins = pe.matmul(b[:, a:e], q(r), k(e - a), start=True, stop=not gates)
                    if gates:
                        ins = pe.matmul(b[:, a:e], ident[64:64 + NH, 64 + n - A3:65 + n - A3].to_broadcast([NH, P]),
                                        ncum[:, 0:e - a], start=False, stop=True)
                ins.then_inc(sc_ps, 1)

            def turn(n):
                pe.wait_ge(p_ok, n + 1)
                s_ = sm[:, n % 2, :]
                pe.transpose(bank[5][:, 0:P], s_[:, M:M + P], ident[:, :])
                pe.transpose(bank[5][:, P:2 * P], s_[:, 2 * M + P:2 * M + 2 * P], ident[:, :])
                pe.transpose(bank[5][:, 2 * P:3 * P], s_[:, 2 * M + 2 * P:416], ident[:, :])
                pe.transpose(bank[6][0:M, 0:P], s_[:, 0:M], ident[:, :])
                pe.transpose(bank[6][0:M, P:2 * P], s_[:, M + P:2 * M + P], ident[:, :]).then_inc(pt_ps, 1)

            def values(n, v, vm):
                pe.wait_ge(pt_ok, n + 1)
                pe.wait_ge(ptm_ok, n - A2 + 1)
                pe.wait_ge(o_ok, n)
                pe.matmul(bank[7][:, 0:HD], pt[0:M, 384:384 + P], vm, start=True, stop=False)
                pe.matmul(bank[7][:, 0:HD], pt[:, 0:P], v(0), start=False, stop=True)
                pe.matmul(bank[7][:, HD:2 * HD], pt[0:M, 384 + P:640], vm, start=True, stop=False)
                pe.matmul(bank[7][:, HD:2 * HD], pt[:, P:2 * P], v(0), start=False, stop=False)
                pe.matmul(bank[7][:, HD:2 * HD], pt[:, 2 * P:3 * P], v(1), start=False, stop=True).then_inc(o_ps, 1)

            def rider(key, half):
                kind = key[0]
                if kind in ("fk", "fq"):
                    b = key[1]
                    c = (C_FK if kind == "fk" else C_FQ) + b // 4
                    part_b(c, key, b % 4, 0 if kind == "fk" else M)
                    return
                c = {"fv": C_FV, "zm": C_ZM, "brm": C_BRM, "ga": C_GA, "zf": C_ZF, "brf": C_BRF, "gb": C_GB,
                     "out": C_OUT}[kind] + key[1] * STRIDE.get(kind, 1)
                t = (2, 0, 1)[key[2]] if kind == "fv" else key[2]
                y = kind in ("brm", "brf")
                part_a(c, key, t, 4 * half, 4 * half + 4, sh=y_hi if y else x_hi, sl=y_lo if y else x_lo,
                       moved=M if y else 0)

            def riders(keys, half):
                if len(keys) == 2:
                    rider(keys[half], 0)
                elif keys:
                    rider(keys[0], half)

            def head_scores(n):
                if n < NH:
                    evacuated(("uq", n))
                    scores(A2 + n, lambda r: q_h[:, n % 2, r * P:(r + 1) * P], lambda e: kT[:, n, 0:e])
                else:
                    a, i = 64 * (n % 2), (n - NH) // 2
                    scores(A2 + n, lambda r: fqT[a:a + HD, i, r * P:(r + 1) * P], lambda e: fkT[a:a + HD, i, 0:e], True)

            def head_values(n):
                cols = slice(n % NH * HD, (n % NH + 1) * HD)
                if n < NH:
                    values(A2 + n, lambda r: v_m[:, r, cols], v_mm[0:M, cols])
                else:
                    values(A2 + n, lambda r: f_v[:, r, cols], f_vm[0:M, cols])

            def o_mla_turn(k):
                to_stationary("o_mla", lambda r, k: o_mla[:, r, k * P:(k + 1) * P], z_ok, 2 + k // 4 * 2, ks=(k,))

            for n in range(3):
                mla_query(n)
            pe.wait_ge(k_ok, 1)
            evacuated(("uk", 6), ("uk", 7))
            for n in range(2):
                head_scores(n)
            evacuated(("uv", 2, 0), ("uv", 2, 1))
            for n in range(2 * NH):
                if n == NH - 2:
                    pe.wait_ge(ncum_ok, 1)
                if n + 2 < 2 * NH:
                    head_scores(n + 2)
                if n + 3 < NH:
                    mla_query(n + 3)
                if n == min(j for j in range(2 * NH) if RIDERS[j] and RIDERS[j][0][0] == "brm"):
                    st_wait("o_mla")
                riders(RIDERS[n], 0)
                if n:
                    head_values(n - 1)
                turn(A2 + n)
                if n in MLA_TURNS:
                    o_mla_turn(MLA_TURNS[n][0])
                riders(RIDERS[n], 1)
                if n in MLA_TURNS:
                    o_mla_turn(MLA_TURNS[n][1])
            head_values(2 * NH - 1)

            def y_tiles(name, src, ready, c, keys, st_hi, st_lo, moved, first):
                for k in range(KT):
                    st_wait(name, k)
                    if first <= k + 2 < KT:
                        if k + 2 in ready:
                            pe.wait_ge(z_ok, ready[k + 2])
                        to_stationary(name, src, None, 0, ks=(k + 2,))
                    for key in keys:
                        part_a(c, key, key[2], k, k + 1, sh=st_hi, sl=st_lo, moved=moved)

            def o_fox_rows(r, k):
                return o_fox[:, r, k * P:(k + 1) * P]

            def mixed_rows(r, k):
                return y_mix[:, r, k * P:(k + 1) * P]

            for i, key in enumerate(TAIL_KEYS[:4]):
                if i == 3:
                    pe.wait_ge(z_ok, 12)
                elif i == 0:
                    pe.wait_ge(z_ok, 10)
                if i != 2:
                    to_stationary("o_fox", o_fox_rows, None, 0, ks=TAIL_TURNS[i])
                for half in range(2):
                    rider(key, half)
            y_tiles("o_fox", o_fox_rows, {}, C_BRF, [("brf", 0, r) for r in range(R)], y_hi, y_lo, M, 6)
            for half in range(2):
                rider(("brf", 1, 0), half)
            to_stationary("mixed", mixed_rows, z_ok, 14, ks=range(2))
            for half in range(2):
                rider(("brf", 1, 1), half)
            y_tiles("mixed", mixed_rows, {4: 16}, C_OUT, [("out", 0, r) for r in range(R)], x_hi, x_lo, 0, 2)
            for r in range(R):
                for half in range(2):
                    rider(("out", 1, r), half)
        @block.scalar
        def _(act):
            def split_main(c, slot):
                for g in range(2):
                    act.wait_ge(w_landed[g], 16 * c + 16)
                    act.activation(w_hi[:, slot, 4 * g:4 * g + 4, :], w_raw[:, g, :, :], ACT.Copy).then_inc(w_hi_ok, 1)

            def split_side(u, after=None):
                act.wait_ge(s_landed[u % 2], 16 * (u // 2 + 1))
                if after is not None:
                    act.wait_ge(acc_ready[USE[after] % 2], USE[after] // 2 + 1)
                act.activation(s_hi[:, u % 2, :], s_raw[:, u % 2, :], ACT.Copy).then_inc(s_hi_ok, 1)

            def acc_in(key):
                n = USE[key]
                act.wait_ge(acc_ready[n % 2], n // 2 + 1)
                return acc[n % 2]

            def freed(ins, key):
                ins.then_inc(acc_free[USE[key] % 2], 1)
                if key in LAST and LAST[key] + 2 < N_CHUNKS:
                    split_main(LAST[key] + 2, LAST[key] % 2)

            def carry(out, key, width=CH, scale=1.0, rows=P):
                b = acc_in(key)
                freed(act.activation(out, b[0:rows, 0:width], ACT.Copy, scale=scale), key)

            def split_st(name, hi, scale=None, a=M, ks=None, after=None):
                for k in range(ST_TILES[name]) if ks is None else ks:
                    n = ST[name] + k
                    act.wait_ge(tp_ready, n + 1)
                    if after is not None and k == 0:
                        act.wait_ge(*after)
                    sc = 1.0 if scale is None else scale(k)
                    act.activation(hi(k), tp_bank(n)[:, a:L], ACT.Copy, scale=sc).then_inc(st_hi_ok, 1)

            def sums(name, src, after, value, scratch=XN):
                act.wait_ge(after, value)
                for r in range(R):
                    ins = act.activation(scratch[:, r, :], src[:, r, :], ACT.Square, accum_out=stat[:, r:r + 1])
                ins.then_inc(ss_ok, 1)

            def x_tile(t, a=M):
                return lambda k: t[:, k, a:L]

            def split_both(name, scale, c, slot, first=0):
                for k in range(KT):
                    if k >= first:
                        split_st(name, x_tile(x_hi), scale, ks=(k,))
                    act.wait_ge(w_landed[k // 4], 16 * c + 16)
                    ins = act.activation(w_hi[:, slot, k, :], w_raw[:, k // 4, k % 4, :], ACT.Copy)
                    if k % 4 == 3:
                        ins.then_inc(w_hi_ok, 1)

            act.wait_ge(zero_ok, 1)
            sums("x0", h, in_landed, 48)
            split_side(0)
            split_main(0, 0)
            split_st("x0", x_tile(x_hi), lambda k: pcol("norm_mix0", k))
            b = acc_in(("gates",))
            for g in range(4):
                ins = act.activation(g_rows[0:H0, g, :], b[32 * g:32 * g + H0, 0:S], ACT.Copy)
            freed(ins, ("gates",))
            carry(mqT[:, 0, :], ("mq", 0), S, DK ** -0.5)
            split_main(1, 1)
            for b in range(1, 4):
                carry(mqT[:, b, :], ("mq", b), S, DK ** -0.5)
            split_side(1)
            split_side(2, after=("gates",))
            for b in range(4):
                carry(mkT[:, b, :], ("mk", b), S)
                if b == 1:
                    act.wait_ge(fa_ok, 1)
                    act.activation(row_b[0:H0, :, :], row_a[0:H0, :, :], ACT.Exp, scale=-1.0)
                    act.drain()
                    act.activation(row_b[0:H0, :, :], row_b[0:H0, :, :], ACT.Ln, bias=1.0).then_inc(fe_ok, 1)
            for c in range(2):
                for r in range(R):
                    if c == 0:
                        carry(v_aug[:, r, 0:2, 0:DV], ("mv", c, r))
                        act.wait_ge(kn_ps, r + 1)
                        act.activation(m_kn[:, r, :, :], bank[4][:, :].rearrange("p (a b) -> p a b", a=H0), ACT.Copy).then_inc(kn_ok, 1)
                    else:
                        carry(v_aug[:, r, 2 * c:2 * c + 2, 0:DV], ("mv", c, r))
            act.wait_ge(mc_ps, 1)
            act.activation(mcol[:, 0:16], bank[5][:, 0:16], ACT.Copy)
            act.activation(mcol[:, 16:40], bank[5][:, 16:40], ACT.Exp).then_inc(mc_ok, 1)
            def squares(hh, last=False):
                act.wait_ge(n_done, 2 * hh + 2)
                for r in range(R):
                    ins = act.activation(m_sq[:, 4 * r + hh, :], XN[:, r, hh * DV:(hh + 1) * DV], ACT.Square,
                                         accum_out=stat[:, 4 * r + hh:4 * r + hh + 1])
                if last:
                    ins.then_inc(ss_ok, 1)

            for hh in range(H0):
                act.wait_ge(in_ps, hh + 1)
                if hh:
                    act.wait_ge(qi_ok, hh)
                act.activation(m_ei[:, :, :], bank[2][:, 0:2 * P], ACT.Exp).then_inc(ei_ok, 1)
                act.wait_ge(t_ok, hh + 1)
                for d in range(2):
                    for r in range(R):
                        a = (d * R + r) * H0 + hh
                        ins = act.activation(m_t[:, d, r, :], m_t[:, d, r, :], ACT.Exp, bias=mcol[:, a:a + 1])
                ins.then_inc(wt_ok, 1)
                if hh:
                    squares(hh - 1)
                key = ("mo", hh // 2, hh % 2)
                b = acc_in(key)
                freed(act.activation(o_gate[:, hh % 2, hh // 2 * CH:(hh // 2 + 1) * CH], b[:, :], ACT.Tanh, scale=0.5), key)
                for d in range(2):
                    n = 2 * hh + d
                    act.wait_ge(c_ps, n + 1)
                    if hh:
                        act.wait_ge(n_ps, 4 * hh)
                    act.activation(m_c[:, d, :], bank[5][:, 0:VW], ACT.Copy).then_inc(c_ok, 1)
                for r in range(R):
                    n = 4 * hh + 2 * r
                    act.wait_ge(rd_ok, 2 * hh + r + 1)
                    act.activation(XN[:, r, hh * DV:(hh + 1) * DV], n_bank[2 * r][:, 0:DV], ACT.Copy,
                                   scale=small[:, 2:3]).then_inc(hf_ok, 1)
                if hh == 1:
                    split_main(C_MO + 2, 0)
            squares(H0 - 1, True)
            split_both("m_out", lambda k: pcol("mlstm_norm", k), C_MO + 3, 1)

            def mixer_out(name, c, ffn_st, gain):
                acc_in((name, 0, 1))
                split_main(c + 2, c % 2)
                if name == "aout":
                    next_sides(0)
                scale = lambda k: pcol(gain, k)
                acc_in((name, 1, 1))
                split_both(ffn_st, scale, c + 3, (c + 1) % 2)
                sums(ffn_st, h, h_ready, 1 if ffn_st == "f0" else 3)

            mixer_out("mout", C_MOUT, "f0", "norm_ffn0")

            def ffn(layer, after):
                c0, u0, n0 = C_FFN[layer], U_DOWN[layer], USE[(f"ffn{layer}", 0, 0)]

                def gate(f):
                    for r in range(R):
                        act.wait_ge(acc_ready[(n0 + r) % 2], (n0 + r) // 2 + f + 1)
                        act.activation(ffn_nat[:, 0, r, :], acc[(n0 + r) % 2][:, 0:256], ACT.Silu,
                                       scale=stat[:, 24 + r:25 + r]).then_inc(silu_ok, 1)

                def turned(f):
                    act.wait_ge(g_tp, FB * layer + f + 1)
                    act.activation(ffh, bank[2][:, :], ACT.Copy).then_inc(g_hi_ok, 1)

                def block_(f, j, last=False):
                    turned(f - 1)
                    gate(f)
                    if not last:
                        split_main(c0 + f + 2, (c0 + j) % 2)
                    for s in range(2):
                        slot = (u0 + s) % 2
                        act.wait_ge(s_used, u0 + 2 * f + s - 2)
                        act.wait_ge(s_landed[slot], 16 * (f + (u0 + s) // 2 + 1))
                        act.activation(s_hi[:, slot, :], s_raw[:, slot, :], ACT.Copy).then_inc(s_hi_ok, 1)

                act.wait_ge(rs_ok, 1 + 2 * layer)
                gate(0)
                split_main(c0 + 2, c0 % 2)
                with act.Fori(0, (FB - 1) // 2 - 1) as i:
                    block_(2 * i + 1, 1)
                    block_(2 * i + 2, 2)
                if layer == 0:
                    act.wait_ge(ang_ok, 1)
                    act.activation(sinT, ang[:, 0, :], ACT.Sin)
                    act.activation(cosT, ang[:, 1, :], ACT.Sin).then_inc(tab_ok, 1)
                block_(FB - 2, 1)
                block_(FB - 1, 2, last=True)
                turned(FB - 1)
                after()
                if layer == 1:
                    split_main(c0 + FB + 1, (c0 + 2) % 2)

            def next_sides(layer):
                u = U_DOWN[layer] + 2 * FB
                act.wait_ge(s_used, u - 1)
                for s in range(2):
                    split_side(u + s)


            def swapped(i, key):
                b = acc_in(key)
                if i >= 2:
                    act.wait_ge(rot_ok, i - 1)
                for q in range(4):
                    ins = act.activation(a_sw[32 * (q ^ 1):32 * (q ^ 1) + 32, i % 2, :], b[32 * q:32 * q + 32, 0:S], ACT.Copy)
                ins.then_inc(sw_ok, 1)
                if key in LAST:
                    split_main(LAST[key] + 2, LAST[key] % 2)

            def x1():
                split_both("x1", lambda k: pcol("norm_mix1", k), C_AQ, C_AQ % 2)
                sums("x1", h, h_ready, 2)
                for r in range(R):
                    carry(a_v[:, r, :], ("av", r), S)
                for b in range(2):
                    swapped(b, ("ak", b))

            ffn(0, x1)
            def split_half(c, slot, g):
                act.wait_ge(w_landed[g], 16 * c + 16)
                act.activation(w_hi[:, slot, 4 * g:4 * g + 4, :], w_raw[:, g, :, :], ACT.Copy).then_inc(w_hi_ok, 1)

            for b in range(4):
                if b == 2:
                    act.wait_ge(meta_landed, 16)
                    act.wait_ge(av_ok, 1)
                    act.activation(um[0:M, :], hm[0:M, :], ACT.Square, accum_out=stat[0:M, 0:1]).then_inc(ss_ok, 1)
                swapped(2 + b, ("aq", b))
                if b in (1, 2):
                    split_half(C_AKV + 2, C_AKV % 2, b - 1)

            def exps(n, tiles, s0, sink=None):
                act.wait_ge(nm_ok, n + 1)
                for r in range(R):
                    ins = act.activation(tiles(r), tiles(r), ACT.Exp, bias=small[:, s0 + 2 + r:s0 + 3 + r],
                                         accum_out=small[:, s0 + 4 + r:s0 + 5 + r])
                if sink is not None:
                    ins = act.activation(small[:, s0 + 6:s0 + 8], small[:, s0 + 2:s0 + 4], ACT.Exp, bias=sink)
                ins.then_inc(p_ok, 1)

            for n in range(-1, NH):
                if n + 1 < NH:
                    m = n + 1
                    exps(m, lambda r: a_sm[:, m % 2, r, :], 8 * (m % 4), pcol("sink", m))
                if n == 3:
                    act.wait_ge(um_g, 1)
                    act.activation(x_hi[:, :, 0:M], m_tmp, ACT.Copy).then_inc(um_hi, 1)
                if n in AOUT_SPLITS:
                    split_half(C_AOUT, C_AOUT % 2, AOUT_SPLITS.index(n))
                if n in AQ_RIDERS:
                    j = AQ_RIDERS.index(n)
                    swapped(6 + j, ("aq", 4 + j))
                if n >= 0:
                    act.wait_ge(pt_ps, n + 1)
                    if n:
                        act.wait_ge(o_ps, n)
                    act.activation(a_pt[:, :, :], bank[5][:, :].rearrange("p (a b) -> p a b", a=4), ACT.Copy).then_inc(pt_ok, 1)
            split_both("a_out", None, C_AOUT + 1, (C_AOUT + 1) % 2)
            mixer_out("aout", C_AOUT, "f1", "norm_ffn1")
            def u_():
                split_st("u", x_tile(x_hi), lambda k: gain_u[:, k:k + 1])
                sums("fin", h, h_ready, 4, scratch=sq)
                act.drain()
                for r in range(R):
                    act.wait_ge(hg_ok, r + 1)
                    if r == 0:
                        act.wait_ge(rs_ok, 4)
                    ins = act.activation(sq[:, r, :], XN[:, r, :], ACT.Square, accum_out=stat[:, r:r + 1])
                ins.then_inc(ss_ok, 1)
                carry(cn[:, 0, :], ("c0", 0), KC0)

            ffn(1, u_)

            act.wait_ge(ru_ok, 1)
            for i in (1, 2):
                carry(cn[:, i, :], ("c0", i), KC0, scale=scale_u[:, i - 1:i])
                if i == 1:
                    next_sides(1)
            act.wait_ge(rs_ok, 5)
            act.drain()
            for i in range(3):
                act.activation(cqn[:, i, 0:256], cn[:, i, 0:256], ACT.Square, accum_out=stat[:, i:i + 1])
                ins = act.activation(cqn[:, i, 256:384], cn[:, i, 256:384], ACT.Square, accum_out=stat[:, 3 + i:4 + i])
            ins.then_inc(ss_ok, 1)
            split_main(C_C0 + 2, C_C0 % 2)
            act.wait_ge(f1_ok, 1)
            act.activation(f_row[0:NH, 2, :], f_row[0:NH, 1, :], ACT.Exp, scale=-1.0)
            act.drain()
            act.activation(f_row[0:NH, 2, :], f_row[0:NH, 2, :], ACT.Ln, bias=1.0).then_inc(f2_ok, 1)
            split_st("cqkv", x_tile(cst_h, 0), lambda k: pcol("q_norm", k), a=0)
            act.wait_ge(kr_ps, 1)
            act.activation(kT[64:P, :, :], bank[6][64:P, 0:L].rearrange("p (a l) -> p a l", a=1).to_broadcast([64, NH, L]),
                           ACT.Copy).then_inc(k_ok, 1)
            for p in range(0, 8):
                if USE[("uk", p)] % 2 == 0:
                    b = acc_in(("uk", p))
                    act.activation(kT[0:64, 2 * p, :], b[0:64, 0:L], ACT.Copy)
                    freed(act.activation(kT[0:64, 2 * p + 1, :], b[64:P, 0:L], ACT.Copy), ("uk", p))
            split_side(U_Q, after=("uk", 7))
            for i, t in enumerate((2, 0, 1)):
                for cc in range(2):
                    if t == 2:
                        carry(v_mm[0:M, cc * CH:(cc + 1) * CH], ("uv", i, cc), rows=M)
                    else:
                        carry(v_m[:, t, cc * CH:(cc + 1) * CH], ("uv", i, cc))
            split_side(U_Q + 1, after=("uv", 2, 1))

            def gate_in(key):
                b = acc_in(key)
                if key in ZN:
                    i = ZN[key]
                    if i >= 2:
                        act.wait_ge(z_ok, z_count(i - 2))
                    act.activation(z_t[:, i % 2, :], b[:, :], ACT.Tanh,
                                   scale=half_u[:, key[2]:key[2] + 1]).then_inc(th_ok, 1)
                    if key in LAST and LAST[key] + 2 < N_CHUNKS:
                        split_main(LAST[key] + 2, LAST[key] % 2)
                    return
                out = y_mix if key[0] == "ga" else XN
                freed(act.activation(out[:, key[2], key[1] * CH:(key[1] + 1) * CH], b[:, :], ACT.Tanh,
                                     scale=half_u[:, key[2]:key[2] + 1]), key)

            def rider(key):
                kind = key[0]
                if kind in ("fk", "fq"):
                    if key in LAST and LAST[key] + 2 < N_CHUNKS:
                        acc_in(key)
                        split_main(LAST[key] + 2, LAST[key] % 2)
                elif kind == "fv":
                    if key[1:] == (0, 0):
                        act.wait_ge(s_lo_ok, N_UNITS)
                    cols = slice(key[1] * CH, (key[1] + 1) * CH)
                    if key[2] == 0:
                        carry(f_vm[0:M, cols], key, rows=M)
                    else:
                        carry(f_v[:, key[2] - 1, cols], key, scale=scale_u[:, key[2] - 1:key[2]])
                elif kind in ("brm", "brf"):
                    if key in LAST and LAST[key] + 2 < N_CHUNKS:
                        acc_in(key)
                        split_main(LAST[key] + 2, LAST[key] % 2)
                elif kind == "out":
                    carry(o_fox[:, key[2], key[1] * CH:(key[1] + 1) * CH], key)
                else:
                    gate_in(key)

            def meta_turned(n):
                act.wait_ge(pt_ps, n + 1)
                act.wait_ge(o_ps, n)
                act.activation(pt[0:M, 384:640], bank[6][0:M, 0:2 * P], ACT.Copy).then_inc(ptm_ok, 1)

            def head_exps(n):
                s_ = sm[:, n % 2, :]
                exps(A2 + n, lambda r: s_[:, 0:M + P] if r == 0 else s_[:, M + P:416], 8 * (n % 4))

            head_exps(0)
            for n in range(2 * NH):
                keys = RIDERS[n]
                if n + 1 < 2 * NH:
                    head_exps(n + 1)
                if len(keys) == 2:
                    rider(keys[0])
                meta_turned(A2 + n)
                if n in MLA_TURNS:
                    split_st("o_mla", lambda k: y_hi[:, k, :], ks=MLA_TURNS[n])
                if keys:
                    rider(keys[-1])
                if n == 0:
                    split_main(C_FK + 2, C_FK % 2)
                if n in (1, 5):
                    split_side(U_Q + 2 + n // 4, after=("uq", 3 + n // 4 * 4))
            for i, key in enumerate(TAIL_KEYS):
                if i in TAIL_TURNS:
                    split_st("o_fox", lambda k: y_hi[:, k, :], ks=TAIL_TURNS[i])
                if i == 4:
                    split_st("o_fox", lambda k: y_hi[:, k, :], ks=(6, 7))
                if i == len(TAIL_KEYS) - 1:
                    split_st("mixed", x_tile(x_hi), lambda k: 0.5, ks=(0, 1))
                rider(key)
            acc_in(TAIL_KEYS[-1])
            split_both("mixed", lambda k: 0.5, C_OUT + 1, (C_OUT + 1) % 2, first=2)
            for c in range(2):
                for r in range(R):
                    rider(("out", c, r))
            act.drain()
            for r in range(R):
                ins = act.activation(XN[:, r, :], o_fox[:, r, :], ACT.Square, accum_out=stat[:, r:r + 1])
            ins.then_inc(ss_ok, 1)

        @block.vector
        def _(dve):
            def rest_main(c, slot):
                for g in range(2):
                    dve.wait_ge(w_hi_ok, 2 * c + g + 1)
                    dve.tensor_tensor(w_lo[:, slot, 4 * g:4 * g + 4, :], w_raw[:, g, :, :],
                                      w_hi[:, slot, 4 * g:4 * g + 4, :], ALU.subtract).then_inc(w_lo_ok, 1)

            def rest_side(u):
                dve.wait_ge(s_hi_ok, u + 1)
                dve.tensor_tensor(s_lo[:, u % 2, :], s_raw[:, u % 2, :], s_hi[:, u % 2, :], ALU.subtract).then_inc(s_lo_ok, 1)

            def after_key(key):
                if key in LAST and LAST[key] + 2 < N_CHUNKS:
                    rest_main(LAST[key] + 2, LAST[key] % 2)

            def acc_in(key):
                n = USE[key]
                dve.wait_ge(acc_ready[n % 2], n // 2 + 1)
                return acc[n % 2]

            def rest_st(name, hi, lo, scale=None, a=M, ks=None):
                for k in range(ST_TILES[name]) if ks is None else ks:
                    n = ST[name] + k
                    dve.wait_ge(st_hi_ok, n + 1)
                    src = tp_bank(n)[:, a:L]
                    if scale is None:
                        ins = dve.tensor_tensor(lo(k), src, hi(k), ALU.subtract)
                    else:
                        ins = dve.scalar_tensor_tensor(out=lo(k), in0=src, scalar=scale(k), in1=hi(k),
                                                       op0=ALU.mult, op1=ALU.subtract)
                    ins.then_inc(st_lo_ok, 1)

            def rstd(name, parts, rows=P):
                i, n = RMS[name], sum(w for w, _ in parts)
                dve.wait_ge(ss_ok, i + 1)
                at = 0
                for w, width in parts:
                    dve.tensor_scalar(stat[0:rows, 8 + at:8 + at + w], stat[0:rows, at:at + w], 1.0 / width, EPS, ALU.mult, ALU.add)
                    at += w
                x, y, t = stat[0:rows, 8:8 + n], stat[0:rows, 16:16 + n], stat[0:rows, 0:n]
                dve.drain()
                dve.tensor_scalar(y.bitcast(I32), x.bitcast(I32), -0.5, float(0x5F3759DF), ALU.mult, ALU.add)
                dve.tensor_scalar(x, x, -0.5, None, ALU.mult)
                for step in range(3):
                    dve.drain()
                    dve.tensor_tensor(t, y, y, ALU.mult)
                    dve.drain()
                    dve.tensor_tensor(t, t, x, ALU.mult)
                    dve.drain()
                    dve.scalar_tensor_tensor(out=y if step < 2 else stat[0:rows, 24:24 + n], in0=t, scalar=1.5, in1=y,
                                             op0=ALU.add, op1=ALU.mult)
                dve.drain()

            def root_col(k):
                return stat[:, 24 + k:25 + k]

            def x_tile(t, a=M):
                return lambda k: t[:, k, a:L]

            def rest_second(c, slot):
                dve.wait_ge(w_hi_ok, 2 * c + 2)
                dve.tensor_tensor(w_lo[:, slot, 4:8, :], w_raw[:, 1, :, :], w_hi[:, slot, 4:8, :], ALU.subtract).then_inc(w_lo_ok, 1)

            def rest_both(name, scale, c, slot, first=0, second=True):
                for k in range(first, KT):
                    rest_st(name, x_tile(x_hi), x_tile(x_lo), scale, ks=(k,))
                    if k >= 4:
                        dve.wait_ge(w_hi_ok, 2 * c + 1)
                        ins = dve.tensor_tensor(w_lo[:, slot, k - 4, :], w_raw[:, 0, k - 4, :], w_hi[:, slot, k - 4, :], ALU.subtract)
                        if k == KT - 1:
                            ins.then_inc(w_lo_ok, 1)
                if second:
                    rest_second(c, slot)

            def scaled_rows(src):
                for r in range(R):
                    ins = dve.tensor_scalar(XN[:, r, :], src[:, r, :], root_col(r), None, ALU.mult)
                return ins

            dve.wait_ge(in_landed, 48)
            rstd("x0", [(R, D)])
            scaled_rows(h).then_inc(xn_ready, 1)
            rest_side(0)
            rest_main(0, 0)
            rest_st("x0", x_tile(x_hi), x_tile(x_lo), lambda k: pcol("norm_mix0", k))
            rest_main(1, 1)
            n = USE[("gates",)]
            dve.wait_ge(acc_free[n % 2], n // 2 + 1)
            gr = g_rows[0:H0, :, :]
            dve.tensor_tensor(gr, gr, par[0:H0, PC["b_gate"]:PC["b_gate"] + 4].rearrange("p (a b) -> p a b", b=1)
                              .to_broadcast([H0, 4, S]), ALU.add)
            dve.drain()
            f2 = g_rows[0:H0, :, :].rearrange("p (d k) s -> p d k s", k=2)
            ig, fg = f2[:, :, 0, :], f2[:, :, 1, :]
            ra, rb, rc, rm, rn, re_ = (t[0:H0, :, :] for t in (row_a, row_b, row_c, row_m, row_n, row_e))
            dve.scalar_tensor_tensor(out=ra, in0=fg, scalar=-1.0, in1=fg, op0=ALU.mult, op1=ALU.max).then_inc(fa_ok, 1)
            rest_side(1)
            rest_side(2)
            dve.wait_ge(fe_ok, 1)
            dve.drain()
            dve.scalar_tensor_tensor(out=ra, in0=fg, scalar=0.0, in1=rb, op0=ALU.min, op1=ALU.subtract)
            dve.drain()
            dve.wait_ge(va_ok, 1)

            def tile(t, d, r):
                v = t[:, d, r * P:(r + 1) * P]
                return v if d == 0 else v[:, ::-1]

            ones = row_1[0:H0, :, :]
            for d in range(2):
                for r in range(R):
                    dve.tensor_tensor_scan(tile(rb, d, r), tile(ones, d, r), tile(ra, d, r), 0.0, ALU.mult, ALU.add)
            dve.drain()
            dve.tensor_tensor(rc, ig, rb, ALU.subtract)
            dve.drain()
            last = [P - 1, P]
            for d in range(2):
                dve.tensor_tensor_scan(tile(rm, d, d), tile(rc, d, d), tile(rc, d, d), 0.0, ALU.max, ALU.max)
            dve.drain()
            for d in range(2):
                e = last[d]
                dve.tensor_tensor(small[0:H0, 40 + d:41 + d], rb[:, d, e:e + 1], rm[:, d, e:e + 1], ALU.add)
            dve.drain()
            for d in range(2):
                dve.tensor_tensor_scan(tile(rm, d, 1 - d), tile(rc, d, 1 - d), tile(rc, d, 1 - d), small[0:H0, 40 + d:41 + d],
                                       ALU.max, ALU.max)
            dve.drain()
            dve.tensor_scalar(rn, rm, -1.0, None, ALU.mult)
            dve.drain()
            dve.tensor_tensor(re_, rn, rb, ALU.subtract)
            for d in range(2):
                e = last[d]
                dve.tensor_scalar(row_i[0:H0, d, :], rn[:, d, (1 - d) * P:(2 - d) * P], small[0:H0, 40 + d:41 + d], None, ALU.add)
                ins = dve.tensor_scalar(row_w[0:H0, d, :], rc[:, d, d * P:(d + 1) * P], rn[:, d, e:e + 1], None, ALU.add)
            ins.then_inc(rows_ok, 1)
            for c in range(2, C_MO + 2):
                rest_main(c, c % 2)

            dve.wait_ge(c0_landed, 16)
            dve.wait_ge(mc_ok, 1)
            for hh in range(H0):
                dve.wait_ge(bc_ps, hh + 1)
                for d in range(2):
                    ins = dve.tensor_tensor(m_t[:, d, :, :], bank[3][:, d * S:(d + 1) * S].rearrange("p (r l) -> p r l", r=R),
                                            m_mask[:, d, :].rearrange("p (a l) -> p a l", a=1).to_broadcast([P, R, P]), ALU.add)
                ins.then_inc(t_ok, 1)
                if hh:
                    dve.wait_ge(n_ps, 4 * hh)
                dve.wait_ge(wt_ok, hh + 1)
                dve.wait_ge(s0_ps, hh + 1)
                for d in range(2):
                    ins = dve.tensor_tensor(m_sd[:, d, :, :], m_t[:, d, :, :], bank[4][:, 0:S].rearrange("p (r l) -> p r l", r=R),
                                            ALU.mult)
                ins.then_inc(sd_ok, 1)
                dve.drain()
                for r in range(R):
                    for d in range(2):
                        n = 4 * hh + 2 * r + d
                        b = n_bank[2 * r + d]
                        dve.wait_ge(n_ps, n + 1)
                        t = small[:, 0:1]
                        a = 16 + (d * R + r) * H0 + hh
                        dve.tensor_scalar(t, b[:, DV:DV + 1], -1.0, None, ALU.mult)
                        dve.drain()
                        dve.scalar_tensor_tensor(out=small[:, 1:2], in0=b[:, DV:DV + 1], scalar=mcol[:, a:a + 1], in1=t,
                                                 op0=ALU.max, op1=ALU.max)
                        dve.drain()
                        if d == 0:
                            dve.reciprocal(small[:, 2:3], small[:, 1:2]).then_inc(rd_ok, 1)
                        else:
                            dve.reciprocal(small[:, 3:4], small[:, 1:2])
                            dve.wait_ge(hf_ok, 2 * hh + r + 1)
                            dve.drain()
                            xs = XN[:, r, hh * DV:(hh + 1) * DV]
                            dve.scalar_tensor_tensor(out=xs, in0=b[:, 0:DV], scalar=small[:, 3:4], in1=xs,
                                                     op0=ALU.mult, op1=ALU.add).then_inc(n_done, 1)
                if hh == 1:
                    rest_main(C_MO + 2, 0)
            rstd("hs", [(8, DV)])
            dve.tensor_scalar(stat[:, 24:32], stat[:, 24:32], 0.5, None, ALU.mult)
            dve.drain()
            dve.wait_ge(og1_ok, H0)
            for r in range(R):
                for hh in range(H0):
                    xs = XN[:, r, hh * DV:(hh + 1) * DV]
                    ins = dve.scalar_tensor_tensor(out=xs, in0=xs, scalar=root_col(4 * r + hh),
                                                   in1=o_gate[:, r, hh * DV:(hh + 1) * DV], op0=ALU.mult, op1=ALU.mult)
            ins.then_inc(xn_ready, 1)
            rest_both("m_out", lambda k: pcol("mlstm_norm", k), C_MO + 3, 1)

            def mixer_out(name, ch, ffn_st, gain):
                for c in range(2):
                    for r in range(R):
                        key = (name, c, r)
                        b = acc_in(key)
                        hs = h[:, r, c * CH:(c + 1) * CH]
                        dve.tensor_tensor(hs, hs, b[:, :], ALU.add).then_inc(acc_free[USE[key] % 2], 1)
                        if (c, r) == (1, 1):
                            dve.drain().then_inc(h_ready, 1)
                        if (c, r) == (0, 1):
                            rest_main(ch + 2, ch % 2)
                            if name == "aout":
                                next_sides(0)
                rest_both(ffn_st, lambda k: pcol(gain, k), ch + 3, (ch + 1) % 2)
                rstd(ffn_st, [(R, D)])
                dve.drain().then_inc(rs_ok, 1)

            mixer_out("mout", C_MOUT, "f0", "norm_ffn0")

            def angles():
                c1 = 6.28125
                c2 = float(np.float32(round((TWO_PI - c1) * 2 ** 21) / 2 ** 21))
                c3 = TWO_PI - c1 - c2
                big, lim = float(1.5 * 2 ** 23), 3.1415925
                dve.wait_ge(pos_landed, 16)
                dve.tensor_copy(ang[:, 0, :], pos_i[:, :])
                dve.drain()
                dve.tensor_scalar(ang[:, 0, :], ang[:, 0, :], pcol("inv_freq"), None, ALU.mult)
                dve.drain()
                dve.tensor_scalar(ang[:, 1, :], ang[:, 0, :], 1.0 / TWO_PI, big, ALU.mult, ALU.add)
                dve.drain()
                dve.tensor_scalar(ang[:, 1, :], ang[:, 1, :], big, None, ALU.subtract)
                for cw in (c1, c2, c3):
                    dve.drain()
                    dve.scalar_tensor_tensor(out=ang[:, 0, :], in0=ang[:, 1, :], scalar=-cw, in1=ang[:, 0, :],
                                             op0=ALU.mult, op1=ALU.add)
                dve.drain()
                dve.tensor_scalar(ang[:, 1, :], ang[:, 0, :], float(np.pi / 2), None, ALU.add)
                dve.drain()
                dve.tensor_scalar(ang[:, 2, :], ang[:, 1, :], float(np.pi), -TWO_PI, ALU.is_gt, ALU.mult)
                dve.drain()
                dve.tensor_tensor(ang[:, 1, :], ang[:, 1, :], ang[:, 2, :], ALU.add)
                dve.drain()
                dve.tensor_scalar(ang[:, 0:2, :], ang[:, 0:2, :], lim, -lim, ALU.min, ALU.max).then_inc(ang_ok, 1)

            def ffn(layer, after):
                c0, u0, n0 = C_FFN[layer], U_DOWN[layer], USE[(f"ffn{layer}", 0, 0)]

                def product(f):
                    for r in range(R):
                        b_ = (n0 + r) % 2
                        dve.wait_ge(silu_ok, 2 * FB * layer + 2 * f + r + 1)
                        dve.scalar_tensor_tensor(out=ffn_nat[:, 1, r, :], in0=acc[b_][:, 256:512], scalar=root_col(r),
                                                 in1=ffn_nat[:, 0, r, :], op0=ALU.mult, op1=ALU.mult).then_inc(acc_free[b_], 1)

                def turned(f):
                    dve.wait_ge(g_hi_ok, FB * layer + f + 1)
                    dve.tensor_tensor(ffl, bank[2][:, :].rearrange("p (k t) -> p k t", k=2), ffh,
                                      ALU.subtract).then_inc(g_lo_ok, 1)

                def block_(f, j, last=False):
                    turned(f - 1)
                    product(f)
                    if not last:
                        rest_main(c0 + f + 2, (c0 + j) % 2)
                    for s in range(2):
                        slot = (u0 + s) % 2
                        dve.wait_ge(s_hi_ok, u0 + 2 * f + s + 1)
                        dve.tensor_tensor(s_lo[:, slot, :], s_raw[:, slot, :], s_hi[:, slot, :],
                                          ALU.subtract).then_inc(s_lo_ok, 1)

                product(0)
                rest_main(c0 + 2, c0 % 2)
                if layer == 0:
                    angles()
                with dve.Fori(0, (FB - 1) // 2 - 1) as i:
                    block_(2 * i + 1, 1)
                    block_(2 * i + 2, 2)
                block_(FB - 2, 1)
                block_(FB - 1, 2, last=True)
                turned(FB - 1)
                for cc in range(2):
                    dve.wait_ge(s_used, u0 + 2 * FB - 2 + cc)
                    for r in range(R):
                        hs = h[:, r, cc * CH:(cc + 1) * CH]
                        ins = dve.tensor_tensor(hs, hs, bank[4 + 2 * r + cc][:, :], ALU.add)
                    ins.then_inc(h_ready if cc else h_half, 1)
                dve.drain()
                after()
                if layer == 1:
                    rest_main(c0 + FB + 1, (c0 + 2) % 2)

            def next_sides(layer):
                for s in range(2):
                    rest_side(U_DOWN[layer] + 2 * FB + s)

            def rotated(i, key, out):
                n = USE[key]
                dve.wait_ge(sw_ok, i + 1)
                dve.tensor_tensor(a_tmp[:, i % 2, :], acc[n % 2][:, 0:S], cosT, ALU.mult).then_inc(acc_free[n % 2], 1)
                dve.tensor_tensor(a_sw[:, i % 2, :], a_sw[:, i % 2, :], sinT, ALU.mult)
                dve.drain()
                dve.tensor_tensor(out, a_tmp[:, i % 2, :], a_sw[:, i % 2, :], ALU.add).then_inc(rot_ok, 1)
                after_key(key)

            def x1():
                rest_both("x1", lambda k: pcol("norm_mix1", k), C_AQ, C_AQ % 2, second=False)
                rstd("x1", [(R, D)])
                dve.drain().then_inc(rs_ok, 1)
                dve.wait_ge(tab_ok, 1)
                dve.wait_ge(rb_ps, 1)
                dve.scalar_tensor_tensor(out=sinT, in0=sinT, scalar=pcol("sign"), in1=bank[6][:, 0:S], op0=ALU.mult, op1=ALU.mult)
                dve.tensor_tensor(cosT, cosT, bank[6][:, 0:S], ALU.mult)
                dve.drain()
                for b in range(2):
                    rotated(b, ("ak", b), akT[:, b, :])
                rest_second(C_AQ, C_AQ % 2)
                for r in range(R):
                    n = USE[("av", r)]
                    dve.wait_ge(acc_free[n % 2], n // 2 + 1)
                    ins = dve.tensor_scalar(a_v[:, r, :], a_v[:, r, :], root_col(r), None, ALU.mult)
                ins.then_inc(av_ok, 1)

            ffn(0, x1)

            def rest_half(c, slot, g):
                dve.wait_ge(w_hi_ok, 2 * c + g + 1)
                dve.tensor_tensor(w_lo[:, slot, 4 * g:4 * g + 4, :], w_raw[:, g, :, :],
                                  w_hi[:, slot, 4 * g:4 * g + 4, :], ALU.subtract).then_inc(w_lo_ok, 1)

            for b in range(4):
                rotated(2 + b, ("aq", b), aqT[:, b, :])
                if b == 2:
                    rstd("meta", [(1, D)], rows=M)
                    dve.tensor_scalar(um[0:M, :], hm[0:M, :], stat[0:M, 24:25], None, ALU.mult).then_inc(um_ok, 1)
                if b in (1, 2):
                    rest_half(C_AKV + 2, C_AKV % 2, b - 1)

            def masked(n, tiles, sources, masks, scale=1.0, sink=None):
                s0 = 8 * (n % 4)
                dve.wait_ge(sc_ps, n + 1)
                if n >= 2:
                    dve.wait_ge(pt_ps, n - 1)
                for r in range(R):
                    dve.tensor_tensor_reduce(tiles(r), sources(r), masks(r), scale, float(np.finfo(np.float32).min), ALU.add, ALU.max,
                                             small[:, s0 + r:s0 + r + 1])
                dve.drain()
                mx, nm = small[:, s0:s0 + 2], small[:, s0 + 2:s0 + 4]
                if sink is None:
                    dve.tensor_scalar(nm, mx, -1.0, None, ALU.mult).then_inc(nm_ok, 1)
                else:
                    dve.tensor_scalar(nm, mx, sink, -1.0, ALU.max, ALU.mult).then_inc(nm_ok, 1)

            def attended(n, out, sink=False):
                s0 = 8 * (n % 4)
                dve.wait_ge(p_ok, n + 1)
                den = small[:, s0 + 4:s0 + 6]
                if sink:
                    dve.tensor_tensor(den, den, small[:, s0 + 6:s0 + 8], ALU.add)
                    dve.drain()
                dve.reciprocal(small[:, s0 + 6:s0 + 8], den)
                dve.wait_ge(o_ps, n + 1)
                dve.drain()
                dve.tensor_tensor(out, (bank[7] if n >= A2 else o_bank[n % 2])[:, 0:R * HD].rearrange("p (r e) -> p r e", r=R),
                                  small[:, s0 + 6:s0 + 8].rearrange("p (r e) -> p r e", e=1).to_broadcast([P, R, HD]),
                                  ALU.mult).then_inc(o_ok, 1)

            dve.wait_ge(c1_landed, 16)
            for n in range(-1, NH + 1):
                if n + 1 < NH:
                    m = n + 1
                    masked(m, lambda r: a_sm[:, m % 2, r, :], lambda r: sc_bank[m % 2][:, r * S:(r + 1) * S],
                           lambda r: a_mask[:, r, :], HD ** -0.5, pcol("sink", m))
                if n == 3:
                    dve.wait_ge(um_ps, 1)
                    g = pcol("pre_norm", 0, KT)
                    dve.tensor_tensor(m_tmp, bank[6][:, 0:KT * M].rearrange("p (k t) -> p k t", k=KT),
                                      g.rearrange("p (k t) -> p k t", t=1).to_broadcast([P, KT, M]), ALU.mult).then_inc(um_g, 1)
                    dve.tensor_tensor(gain_u, g, pcol("norm_final", 0, KT), ALU.mult)
                    dve.wait_ge(um_hi, 1)
                    dve.tensor_tensor(x_lo[:, :, 0:M], m_tmp, x_hi[:, :, 0:M], ALU.subtract).then_inc(um_lo, 1)
                if n in AOUT_SPLITS:
                    rest_half(C_AOUT, C_AOUT % 2, AOUT_SPLITS.index(n))
                if n >= 1:
                    attended(n - 1, a_o[:, :, (n - 1) * HD:n * HD], sink=True)
                if n in AQ_RIDERS:
                    j = AQ_RIDERS.index(n)
                    rotated(6 + j, ("aq", 4 + j), aqT[:, 4 + j, :])
            rest_both("a_out", None, C_AOUT + 1, (C_AOUT + 1) % 2)
            mixer_out("aout", C_AOUT, "f1", "norm_ffn1")
            def u_():
                rest_st("u", x_tile(x_hi), x_tile(x_lo), lambda k: gain_u[:, k:k + 1], ks=range(4))
                dve.wait_ge(rowg_landed[0], 16)
                for r in range(R):
                    dve.tensor_tensor(XN[:, r, :], h[:, r, :], row_g, ALU.mult).then_inc(hg_ok, 1)
                    rest_st("u", x_tile(x_hi), x_tile(x_lo), lambda k: gain_u[:, k:k + 1], ks=range(4 + 2 * r, 6 + 2 * r))
                rstd("fin", [(R, D)])
                dve.tensor_copy(scale_u, stat[:, 24:26])
                dve.tensor_tensor(half_u, stat[:, 24:26], stat[:, 24:26], ALU.mult)
                dve.drain().then_inc(rs_ok, 1)
                dve.wait_ge(ss_ok, RMS["u"] + 1)
                dve.tensor_tensor(stat[:, 0:R], stat[:, 0:R], half_u, ALU.mult)
                dve.drain()
                rstd("u", [(R, D)])
                dve.tensor_copy(stat[:, 0:R], scale_u)
                dve.drain()
                dve.tensor_tensor(scale_u, scale_u, stat[:, 24:26], ALU.mult)
                dve.drain()
                dve.tensor_scalar(half_u, scale_u, 0.5, None, ALU.mult).then_inc(ru_ok, 1)

            ffn(1, u_)
            for r in range(R):
                dve.tensor_scalar(h[:, r, :], XN[:, r, :], stat[:, r:r + 1], None, ALU.mult)
            dve.drain().then_inc(rs_ok, 1)
            next_sides(1)
            dve.memset(r_row[:, 0:M], 1.0)
            dve.wait_ge(ru_ps, 1)
            dve.tensor_copy(r_row[:, M:L], bank[6][:, 0:S])
            dve.drain()

            def keys_scaled(b):
                bk = acc_in(("fk", b))
                dve.tensor_tensor(fkT[:, b, :], bk[:, 0:L], r_row, ALU.mult).then_inc(acc_free[USE[("fk", b)] % 2], 1)
                if b >= FK_EARLY:
                    after_key(("fk", b))

            def queries_scaled(b):
                bk = acc_in(("fq", b))
                dve.scalar_tensor_tensor(out=fqT[:, b, :], in0=bk[:, 0:S], scalar=HD ** -0.5, in1=r_row[:, M:L],
                                         op0=ALU.mult, op1=ALU.mult).then_inc(acc_free[USE[("fq", b)] % 2], 1)
                after_key(("fq", b))

            for b in range(2):
                keys_scaled(b)
            rstd("cqkv", [(3, 256), (3, 128)])
            for i in range(3):
                dve.tensor_scalar(cqn[:, i, 0:256], cn[:, i, 0:256], root_col(i), None, ALU.mult)
                ins = dve.tensor_scalar(cqn[:, i, 256:384], cn[:, i, 256:384], root_col(3 + i), None, ALU.mult)
            ins.then_inc(xn_ready, 1)
            dve.wait_ge(f_ps, 1)
            fr = [f_row[0:NH, i, :] for i in range(4)]
            dve.tensor_scalar(fr[0], bank[4][0:NH, 0:L], par[0:NH, PC["fox_b"]:PC["fox_b"] + 1], None, ALU.add)
            dve.drain()
            dve.scalar_tensor_tensor(out=fr[1], in0=fr[0], scalar=-1.0, in1=fr[0], op0=ALU.mult, op1=ALU.max).then_inc(f1_ok, 1)
            dve.memset(fr[3], 1.0)
            dve.wait_ge(kpe_ps, 1)
            dve.wait_ge(c2_landed, 32)
            dve.tensor_tensor(kp[0:64, :], bank[5][0:64, 0:L], k_tab[0:64, :], ALU.mult).then_inc(kp_ok, 1)
            dve.wait_ge(f2_ok, 1)
            dve.drain()
            dve.scalar_tensor_tensor(out=fr[1], in0=fr[0], scalar=0.0, in1=fr[2], op0=ALU.min, op1=ALU.subtract)
            dve.drain()
            dve.tensor_tensor_scan(fr[2], fr[3], fr[1], 0.0, ALU.mult, ALU.add)
            dve.drain()
            dve.tensor_scalar(ncum, fr[2], -1.0, None, ALU.mult).then_inc(ncum_ok, 1)
            for b in range(2, FK_EARLY):
                keys_scaled(b)
            rest_st("cqkv", x_tile(cst_h, 0), x_tile(cst_l, 0), lambda k: pcol("q_norm", k), a=0)
            for p in range(8):
                if USE[("uk", p)] % 2 == 1:
                    b = acc_in(("uk", p))
                    dve.tensor_copy(kT[0:64, 2 * p, :], b[0:64, 0:L])
                    dve.tensor_copy(kT[0:64, 2 * p + 1, :], b[64:P, 0:L]).then_inc(acc_free[USE[("uk", p)] % 2], 1)
            rest_side(U_Q)
            rest_main(C_C0 + 2, C_C0 % 2)
            rest_side(U_Q + 1)

            def query(n):
                b = acc_in(("uq", n))
                if n >= 2:
                    dve.wait_ge(sc_ps, A2 + n - 1)
                dve.tensor_tensor(q_h[:, n % 2, :], b[:, 0:S], q_tab, ALU.mult).then_inc(acc_free[USE[("uq", n)] % 2], 1)

            def gate(key):
                if key[0] not in ("zm", "zf", "brm", "brf"):
                    return
                c, r = key[1], key[2]
                cols = slice(c * CH, (c + 1) * CH)
                if key in ZN:
                    i, z = ZN[key], acc[USE[key] % 2]
                    t = z_t[:, i % 2, :]
                    dve.wait_ge(th_ok, i + 1)
                    out = (o_mla if key[0] == "zm" else o_fox)[:, r, cols]
                    dve.scalar_tensor_tensor(out=t, in0=t, scalar=1.0, in1=z[:, :], op0=ALU.add,
                                             op1=ALU.mult).then_inc(acc_free[USE[key] % 2], 1)
                    dve.drain()
                    dve.scalar_tensor_tensor(out=out, in0=t, scalar=half_u[:, r:r + 1], in1=out, op0=ALU.mult,
                                             op1=ALU.mult).then_inc(z_ok, 1)
                    return
                b, y = acc_in(key), y_mix[:, r, cols]
                g = y if key[0] == "brm" else XN[:, r, cols]
                gate_key = ("ga" if key[0] == "brm" else "gb", c, r)
                dve.wait_ge(acc_free[USE[gate_key] % 2], USE[gate_key] // 2 + 1)
                ins = dve.scalar_tensor_tensor(out=g, in0=g, scalar=1.0, in1=b[:, :], op0=ALU.add, op1=ALU.mult)
                ins.then_inc(acc_free[USE[key] % 2], 1)
                if key[0] == "brm":
                    dve.drain().then_inc(z_ok, 1)
                else:
                    dve.drain()
                    dve.tensor_tensor(y, y, g, ALU.add).then_inc(z_ok, 1)

            def head_masked(n):
                s_ = sm[:, n % 2, :]
                b = sc_bank[n % 2]
                masked(A2 + n, lambda r: s_[:, 0:M + P] if r == 0 else s_[:, M + P:416],
                       lambda r: b[:, 0:M + P] if r == 0 else b[:, M + P:416],
                       lambda r: c_mask[:, P:L] if r == 0 else c_mask)

            def head_out(n):
                attended(A2 + n, (o_mla if n < NH else o_fox)[:, :, n % NH * HD:(n % NH + 1) * HD])

            for n in range(3):
                query(n)
            head_masked(0)
            for n in range(2 * NH):
                keys = RIDERS[n]
                if n + 1 < 2 * NH:
                    head_masked(n + 1)
                if n + 3 < NH:
                    query(n + 3)
                take = {"fk": keys_scaled, "fq": queries_scaled}
                if len(keys) == 2:
                    take[keys[0][0]](keys[0][1])
                if n:
                    head_out(n - 1)
                dve.wait_ge(pt_ps, A2 + n + 1)
                dve.tensor_copy(pt[:, 0:384], bank[5][:, 0:384]).then_inc(pt_ok, 1)
                if n in MLA_TURNS:
                    rest_st("o_mla", lambda k: y_hi[:, k, :], lambda k: y_lo[:, k, :], ks=MLA_TURNS[n])
                if len(keys) == 2:
                    take[keys[1][0]](keys[1][1])
                elif keys:
                    gate(keys[-1])
                    after_key(keys[-1])
                if n == 0:
                    rest_main(C_FK + 2, C_FK % 2)
                if n in (1, 5):
                    rest_side(U_Q + 2 + n // 4)
            head_out(2 * NH - 1)
            for i, key in enumerate(TAIL_KEYS):
                if i in TAIL_TURNS:
                    rest_st("o_fox", lambda k: y_hi[:, k, :], lambda k: y_lo[:, k, :], ks=TAIL_TURNS[i])
                if i == 4:
                    rest_st("o_fox", lambda k: y_hi[:, k, :], lambda k: y_lo[:, k, :], ks=(6, 7))
                if i == len(TAIL_KEYS) - 1:
                    rest_st("mixed", x_tile(x_hi), x_tile(x_lo), lambda k: 0.5, ks=(0, 1))
                gate(key)
                after_key(key)
            rest_both("mixed", lambda k: 0.5, C_OUT + 1, (C_OUT + 1) % 2, first=2)
            rstd("post", [(R, D)])
            dve.wait_ge(rowg_landed[1], 16)
            for r in range(R):
                dve.scalar_tensor_tensor(out=XN[:, r, :], in0=o_fox[:, r, :], scalar=root_col(r), in1=row_g,
                                         op0=ALU.mult, op1=ALU.mult)
                dve.drain()
                dve.tensor_tensor(XN[:, r, :], XN[:, r, :], h[:, r, :], ALU.add).then_inc(z_ok, 1)


def k_tiles(w):
    return w.reshape(-1, P, w.shape[1]).transpose(1, 0, 2)


def main_chunks(i):
    def cols(w, idx=None):
        w = w if idx is None else w[:, idx]
        n = w.shape[1]
        for a in range(0, n, CH):
            part = w[:, a:a + CH]
            if part.shape[1] < CH:
                part = np.concatenate([part, np.zeros((D, CH - part.shape[1]), part.dtype)], 1)
            yield part

    parts = [*cols(i["mlstm_w_in"][0][:, 0:3072]), *cols(i["mlstm_w_out"][0])]
    ff = 2816

    def ffn(j):
        w = i["ffn_w_in"][j]
        for f in range(FB):
            yield np.concatenate([w[:, f * 256:(f + 1) * 256], w[:, ff + f * 256:ff + (f + 1) * 256]], 1)

    parts += ffn(0)
    aw = i["attn_w_in"][0]
    parts += cols(aw[:, 1024:1536])
    parts += cols(aw, np.concatenate([np.arange(hd * HD, (hd + 1) * HD) for hd in HEADS]))
    parts += cols(i["attn_w_out"][0][np.concatenate([np.arange(hd * HD, (hd + 1) * HD) for hd in HEADS])])
    parts += ffn(1)
    w = i["w_in_2"][0]
    o = np.cumsum([0, 256, 128, 32, 1024, 1024, 1024, 1024, 16, 1024, 1024, 1024])
    seg = [w[:, o[j]:o[j + 1]] for j in range(11)]
    cq, ckv, kpe, zm, fq, fk, fv, fl, zf, ga, gb = seg
    swap = np.concatenate([np.arange(16, 32), np.arange(16)])
    parts += cols(np.concatenate([cq, ckv, kpe, kpe[:, swap], fl], 1))
    def turns(a, b):
        return a[:, :CH], b[:, :CH], a[:, CH:], b[:, CH:]

    for m in (fk, fq, fv, *turns(zm, ga), i["w_br_mla_2"][0], *turns(zf, gb), i["w_br_fox_2"][0], i["w_out_2"][0]):
        parts += cols(m)
    assert len(parts) == N_CHUNKS
    return np.stack([k_tiles(p).reshape(P, 2, 4 * CH).transpose(1, 0, 2) for p in parts])


HEADS = [8 * g + j + 4 * e for g in range(2) for j in range(4) for e in range(2)]


def side_units(i):
    g = i["mlstm_w_in"][0][:, 3072:]
    gates = np.zeros((D, P), g.dtype)
    for q in range(4):
        gates[:, 32 * q:32 * q + H0] = g[:, q * H0:(q + 1) * H0]
    units = [k_tiles(gates).reshape(P, D)]
    for j in range(2):
        units += list(i["ffn_w_out"][j].reshape(2 * FB, P, D))
    kv = i["w_ukv_2"][0].reshape(P, NH, 2, HD)
    units += [kv[:, :, 0].reshape(P, D), kv[:, :, 1].reshape(P, D)]
    q = i["w_uq_2"][0].reshape(256, NH, 96)
    pe = q[:, :, 64:]
    swap = np.concatenate([np.arange(16, 32), np.arange(16)])
    q = np.concatenate([q, pe[:, :, swap]], 2)
    for j in range(4):
        units.append(k_tiles(q[:, 4 * j:4 * j + 4].reshape(256, CH)).reshape(P, D))
    return np.stack(units)


def param_tile(i):
    t = np.zeros((P, N_PC), np.float32)

    def put(name, v):
        t[:v.shape[0], PC[name]:PC[name] + v.shape[1]] = v

    for j in range(2):
        put(f"norm_mix{j}", i["norm_mix_w"][j].reshape(KT, P).T)
        put(f"norm_ffn{j}", i["norm_ffn_w"][j].reshape(KT, P).T)
    put("mlstm_norm", i["mlstm_norm_w"][0].reshape(KT, P).T)
    put("norm_final", i["norm_final_w"].reshape(KT, P).T)
    put("pre_norm", i["pre_norm_g_2"][0].reshape(KT, P).T)
    put("q_norm", i["mla_q_norm_g_2"][0].reshape(2, P).T)
    put("kv_norm", i["mla_kv_norm_g_2"][0].reshape(1, P).T)
    put("b_gate", i["mlstm_b_gate"][0].reshape(4, H0).T)
    put("fox_b", i["fox_forget_b_2"][0].reshape(NH, 1))
    put("inv_freq", np.tile(np.float32(10000.0) ** (-np.arange(32, dtype=np.float32) / np.float32(32)), 4)[:, None])
    put("sign", np.where(np.arange(P) % 64 < 32, -1.0, 1.0)[:, None])
    put("sink", np.broadcast_to(i["attn_sink"][0][HEADS], (P, NH)))
    return t


def constants():
    a = np.arange(P)
    fwd = np.where(a[:, None] <= a[None, :], 0.0, NEG)
    sel = np.zeros((P, H0, P))
    for j in range(H0):
        sel[j, j] = 1.0
    l0 = np.concatenate([fwd, fwd.T, sel.reshape(P, -1)], 1)
    q = np.arange(S).reshape(R, P).T[:, :, None]
    l1 = np.where(np.abs(np.arange(S) - q) <= P, 0.0, NEG).reshape(P, -1)
    causal = np.where(np.arange(L)[None, :] - (M + P) <= a[:, None], 0.0, NEG)
    inv = np.float32(10000.0) ** (-np.arange(16, dtype=np.float32) / np.float32(16))
    ang = np.arange(L, dtype=np.float32)[None, :] * inv[:, None]
    cos, sin = np.cos(ang), np.sin(ang)
    k_tab = np.zeros((P, L))
    k_tab[0:64] = np.concatenate([cos, cos, -sin, sin])
    q_tab = np.concatenate([np.ones((64, L)), cos, cos, -sin, sin])[:, M:] * (1.0 / np.sqrt(96.0))
    k_sum = np.zeros((P, P))
    for j in range(64):
        k_sum[j, [64 + j % 32, 96 + j % 32]] = 1.0
    b2 = np.concatenate([causal, q_tab, k_tab, k_sum], 1)
    return [np.ascontiguousarray(t, np.float32) for t in (l0, l1, b2, np.eye(P))]


def kernel(**inputs):
    import concourse.bacc as bacc
    from concourse.bass_utils import run_bass_kernel_spmd

    i = {k: np.asarray(v) for k, v in inputs.items()}
    l0, l1, b2, eye = constants()
    rows = np.stack([np.broadcast_to(i["norm_final_w"], (P, D)), np.broadcast_to(i["post_norm_g_2"][0], (P, D))])
    arrays = {
        "w_main_dram": main_chunks(i), "w_side_dram": side_units(i), "params_dram": param_tile(i), "rows_dram": rows,
        "c_l0_dram": l0, "c_l1_dram": l1, "c_b2_dram": b2, "ident_dram": eye, "x_dram": i["x"][0],
        "meta_dram": i["meta_tokens_2"], "pos_dram": i["positions"].reshape(1, S),
    }
    arrays = {k: np.ascontiguousarray(v) for k, v in arrays.items()}
    nc = bacc.Bacc("TRN2", target_bir_lowering=False, num_devices=1)
    aps = [nc.dram_tensor(k, v.shape, mybir.dt.from_np(v.dtype), kind="ExternalInput").ap() for k, v in arrays.items()]
    out = nc.dram_tensor("out_dram", (S, D), F32, kind="ExternalOutput").ap()
    two_blocks(nc, *aps, out)
    r = run_bass_kernel_spmd(nc, [arrays], core_ids=[0])
    return r.results[0]["out_dram"].reshape(1, S, D)
```
